# Optimizing a Trainium2 kernel written in Bass

```python
import math
import jax, jax.numpy as jnp
from jax import lax
import numpy as np

D_MODEL = 1024
BATCH = 1
SEQ = 512
DEPTH = 1
DEC_BATCH = 8
DEC_SEQ = 4
PAST_LEN = 1024
PAGE_SIZE = 128

HEAD_DIM = 64
N_HEADS = (D_MODEL // 2) // HEAD_DIM
H_KV = 2
GROUP = N_HEADS // H_KV
CMP_BLOCK = 32
CMP_STRIDE = 16
CMP_HIDDEN = 2 * HEAD_DIM
SEL_BLOCK = 64
TOP_N = 16
WINDOW = 512
D_CONV = D_MODEL // 2
CONV_WIDTH = 3
D_FF = 128 * ((8 * D_MODEL // 3 + 127) // 128)
N_BUCKETS = 32
MAX_DISTANCE = 128
Q_BLOCK = 64
N_SUB = 3
EPS = 1e-6
NEG_INF = -1e9
FORCE_BONUS = 1e3
IN_SIZES = (N_HEADS * HEAD_DIM, 2 * H_KV * HEAD_DIM, 2 * H_KV * HEAD_DIM, 2 * H_KV * HEAD_DIM,
            3 * N_HEADS, D_CONV, D_CONV, D_CONV, 2 * D_MODEL)
IN_WIDTH = sum(IN_SIZES)

kernel_name = "nsa_shortconv_macaron_adaln_step"

def rms_norm(x, g):
    xf = x.astype(jnp.float32)
    y = xf * lax.rsqrt(jnp.mean(xf * xf, axis=-1, keepdims=True) + EPS)
    return (y * g.astype(jnp.float32)).astype(x.dtype)

def modulate(x, g, shift, scale):
    return rms_norm(x, g) * (1 + scale[:, None, :]) + shift[:, None, :]

def swiglu(u, w_gu, w_down):
    gate, val = jnp.split(u @ w_gu, 2, axis=-1)
    return (jax.nn.silu(gate) * val) @ w_down

def masked_softmax(s, mask):
    s = s.astype(jnp.float32)
    m = jnp.max(jnp.where(mask, s, NEG_INF), axis=-1, keepdims=True)
    e = jnp.exp(jnp.where(mask, s - m, NEG_INF))
    return e / jnp.maximum(jnp.sum(e, axis=-1, keepdims=True), 1e-30)

def rel_bucket(dist):
    n = jnp.maximum(dist, 0)
    max_exact = N_BUCKETS // 2
    nf = jnp.maximum(n, 1).astype(jnp.float32)
    large = max_exact + (jnp.log(nf / max_exact) / math.log(MAX_DISTANCE / max_exact)
                         * (N_BUCKETS - max_exact)).astype(jnp.int32)
    return jnp.where(n < max_exact, n, jnp.minimum(large, N_BUCKETS - 1))

def pos_bias(qpos, kpos, rel_bias):
    b = rel_bias[rel_bucket(qpos[:, None] - kpos[None, :])]
    b = b.reshape(b.shape[0], b.shape[1], H_KV, GROUP)
    return jnp.transpose(b, (2, 3, 0, 1)).astype(jnp.float32)

def compress_kv(rows, pe, w1, w2):
    B, L = rows.shape[:2]
    r = CMP_BLOCK // CMP_STRIDE
    n_ch = L // CMP_STRIDE
    n_c = (L - CMP_BLOCK) // CMP_STRIDE + 1
    ch = rows[:, :n_ch * CMP_STRIDE].reshape((B, n_ch, CMP_STRIDE) + rows.shape[2:])
    w1c = w1.reshape(2, r, CMP_STRIDE, HEAD_DIM, CMP_HIDDEN)
    pre = jnp.einsum('cld,clde->ce', pe, w1)[None, None, :, None, :]
    for m in range(r):
        pre = pre + jnp.einsum('bnlcgd,clde->bncge', ch[:, m:m + n_c], w1c[:, m])
    out = jnp.einsum('bncge,ced->bncgd', jax.nn.gelu(pre), w2)
    c_end = jnp.arange(n_c) * CMP_STRIDE + CMP_BLOCK - 1
    return out, c_end

def cmp_to_sel(p, n_sel):
    r_sel = SEL_BLOCK // CMP_STRIDE
    r_cmp = CMP_BLOCK // CMP_STRIDE
    left = r_cmp - 1
    right = r_sel * n_sel + r_cmp - 1 - left - p.shape[-1]
    pp = jnp.pad(p, [(0, 0)] * (p.ndim - 1) + [(left, right)])
    out = None
    for m in range(r_sel):
        for n in range(r_cmp):
            term = pp[..., m + n: m + n + r_sel * (n_sel - 1) + 1: r_sel]
            out = term if out is None else out + term
    return out

def sel_blocks(rows):
    B, L = rows.shape[:2]
    n_sel = -(-L // SEL_BLOCK)
    rows = jnp.pad(rows, ((0, 0), (0, n_sel * SEL_BLOCK - L), (0, 0), (0, 0), (0, 0)))
    return jnp.transpose(rows.reshape(B, n_sel, SEL_BLOCK, 2, H_KV, HEAD_DIM), (0, 4, 1, 2, 3, 5))

def nsa_attend(q, qpos, gates, kv_c, c_end, kv_s_blocks, kv_w, w_pos, rel_bias):
    B, Q = q.shape[:2]
    n_sel = kv_s_blocks.shape[2]
    qg = (q * HEAD_DIM ** -0.5).reshape(B, Q, H_KV, GROUP, HEAD_DIM)
    s_c = jnp.einsum('bqgrd,bngd->bgrqn', qg, kv_c[:, :, 0]) + pos_bias(qpos, c_end, rel_bias)
    p_c = masked_softmax(s_c, c_end[None, :] <= qpos[:, None])
    o_c = jnp.einsum('bgrqn,bngd->bqgrd', p_c, kv_c[:, :, 1])
    p_slc = cmp_to_sel(p_c.sum(axis=2), n_sel)
    blk = jnp.arange(n_sel)[None, :]
    cur = (qpos // SEL_BLOCK)[:, None]
    valid = blk * SEL_BLOCK <= qpos[:, None]
    forced = (blk == 0) | (blk == cur) | (blk == cur - 1)
    score = jnp.where(valid, p_slc + jnp.where(forced, FORCE_BONUS, 0.0), NEG_INF)
    _, idx = lax.top_k(score, min(TOP_N, n_sel))
    bi = jnp.arange(B)[:, None, None, None]
    gi = jnp.arange(H_KV)[None, :, None, None]
    n_keys = idx.shape[-1] * SEL_BLOCK
    sel = kv_s_blocks[bi, gi, idx].reshape(B, H_KV, Q, n_keys, 2, HEAD_DIM)
    k_pos = (idx[..., None] * SEL_BLOCK + jnp.arange(SEL_BLOCK)).reshape(B, H_KV, Q, n_keys)
    table = rel_bias.T.reshape(H_KV, GROUP, N_BUCKETS)
    b_s = jnp.moveaxis(table[gi, :, rel_bucket(qpos[None, None, :, None] - k_pos)], -1, 2)
    s_s = jnp.einsum('bqgrd,bgqkd->bgrqk', qg, sel[..., 0, :]) + b_s.astype(jnp.float32)
    p_s = masked_softmax(s_s, (k_pos <= qpos[None, None, :, None])[:, :, None])
    o_s = jnp.einsum('bgrqk,bgqkd->bqgrd', p_s, sel[..., 1, :])
    dist = qpos[:, None] - w_pos[None, :]
    s_w = jnp.einsum('bqgrd,bkgd->bgrqk', qg, kv_w[:, :, 0]) + pos_bias(qpos, w_pos, rel_bias)
    p_w = masked_softmax(s_w, (w_pos[None, :] >= 0) & (dist >= 0) & (dist < WINDOW))
    o_w = jnp.einsum('bgrqk,bkgd->bqgrd', p_w, kv_w[:, :, 1])
    g = gates.reshape(B, Q, 3, H_KV, GROUP)[..., None]
    o = g[:, :, 0] * o_c + g[:, :, 1] * o_s + g[:, :, 2] * o_w
    return o.reshape(B, Q, N_HEADS * HEAD_DIM).astype(q.dtype)

def nsa_prompt(q, kv_c_rows, kv_s_rows, kv_w_rows, gates, lw, rel_bias):
    B, T = q.shape[:2]
    kv_c, c_end = compress_kv(kv_c_rows, lw['pe_cmp'], lw['w_cmp1'], lw['w_cmp2'])
    kv_s_blocks = sel_blocks(kv_s_rows)
    n_q = T // Q_BLOCK
    band = WINDOW + Q_BLOCK
    w_idx = (jnp.arange(n_q) * Q_BLOCK)[:, None] + jnp.arange(band)[None, :]
    kv_w_pad = jnp.pad(kv_w_rows, ((0, 0), (WINDOW, 0), (0, 0), (0, 0), (0, 0)))
    kv_w_bands = jnp.moveaxis(kv_w_pad[:, w_idx], 1, 0)
    blocks = lambda t: jnp.moveaxis(t.reshape((B, n_q, Q_BLOCK) + t.shape[2:]), 1, 0)
    xs = (blocks(q), jnp.arange(T).reshape(n_q, Q_BLOCK), blocks(gates), kv_w_bands, w_idx - WINDOW)
    o = lax.map(lambda a: nsa_attend(a[0], a[1], a[2], kv_c, c_end, kv_s_blocks, a[3], a[4], rel_bias), xs)
    return jnp.moveaxis(o, 0, 1).reshape(B, T, N_HEADS * HEAD_DIM)

def nsa_sample(q, kv_c_new, kv_s_new, kv_w_new, gates, cache_c, cache_s, win_buf, page_table, lw, rel_bias):
    B, S = q.shape[:2]
    past = page_table.shape[1] * PAGE_SIZE
    gather = lambda pool: pool[page_table].reshape((B, past) + pool.shape[2:]).astype(kv_c_new.dtype)
    kv_c, c_end = compress_kv(jnp.concatenate([gather(cache_c), kv_c_new], axis=1),
                              lw['pe_cmp'], lw['w_cmp1'], lw['w_cmp2'])
    kv_s_blocks = sel_blocks(jnp.concatenate([gather(cache_s), kv_s_new], axis=1))
    kv_w = jnp.concatenate([win_buf.astype(kv_w_new.dtype), kv_w_new], axis=1)
    w_pos = past - win_buf.shape[1] + jnp.arange(kv_w.shape[1])
    qpos = past + jnp.arange(S)
    o = nsa_attend(q, qpos, gates, kv_c, c_end, kv_s_blocks, kv_w, w_pos, rel_bias)
    keep = min(WINDOW, kv_w.shape[1])
    return o, kv_w[:, kv_w.shape[1] - keep:]

def split_projection(u, w_in):
    B, T = u.shape[:2]
    p = u @ w_in
    parts = []
    off = 0
    for size in IN_SIZES:
        parts.append(p[..., off:off + size])
        off += size
    q, kc, ks, kw, gn, ch, cb, cc, mg = parts
    kv = lambda t: t.reshape(B, T, 2, H_KV, HEAD_DIM)
    return (q.reshape(B, T, N_HEADS, HEAD_DIM), kv(kc), kv(ks), kv(kw),
            jax.nn.sigmoid(gn).reshape(B, T, 3, N_HEADS), ch, cb, cc,
            jax.nn.sigmoid(mg).reshape(B, T, 2, D_MODEL))

def short_conv(h, gate_b, gate_c, w_conv, buf):
    T = h.shape[1]
    full = jnp.concatenate([buf.astype(h.dtype), gate_c * h], axis=1)
    out = w_conv[0] * full[:, 0:T]
    for k in range(1, CONV_WIDTH):
        out = out + w_conv[k] * full[:, k:k + T]
    return gate_b * out, full[:, T:]

def token_mixer(u, lw, rel_bias, past):
    B, T = u.shape[:2]
    q, kv_c, kv_s, kv_w, g_nsa, h_cv, b_cv, c_cv, g_merge = split_projection(u, lw['w_in'])
    if past is None:
        o_nsa = nsa_prompt(q, kv_c, kv_s, kv_w, g_nsa, lw, rel_bias)
        keep = min(WINDOW, T)
        win_new = kv_w[:, T - keep:]
        conv_buf = jnp.zeros((B, CONV_WIDTH - 1, D_CONV), u.dtype)
    else:
        cache_c, cache_s, win_buf, conv_buf, page_table = past
        o_nsa, win_new = nsa_sample(q, kv_c, kv_s, kv_w, g_nsa, cache_c, cache_s, win_buf, page_table, lw, rel_bias)
    y_cv, conv_new = short_conv(h_cv, b_cv, c_cv, lw['w_conv'], conv_buf)
    merged = g_merge[:, :, 0] * (o_nsa @ lw['w_nsa_out']) + g_merge[:, :, 1] * (y_cv @ lw['w_conv_out'])
    return merged @ lw['w_out'], (kv_c, kv_s, win_new, conv_new)

def decoder_layer(x, c, lw, rel_bias, past):
    B = x.shape[0]
    mod = (jax.nn.silu(c) @ lw['w_ada'] + lw['b_ada']).reshape(B, N_SUB, 3, D_MODEL)
    gn = lw['g_norm']
    h = x + 0.5 * mod[:, 0, 2][:, None] * swiglu(modulate(x, gn[0], mod[:, 0, 0], mod[:, 0, 1]),
                                                 lw['w_ffn1_gu'], lw['w_ffn1_down'])
    mix, state = token_mixer(modulate(h, gn[1], mod[:, 1, 0], mod[:, 1, 1]), lw, rel_bias, past)
    h = h + mod[:, 1, 2][:, None] * mix
    h = h + 0.5 * mod[:, 2, 2][:, None] * swiglu(modulate(h, gn[2], mod[:, 2, 0], mod[:, 2, 1]),
                                                 lw['w_ffn2_gu'], lw['w_ffn2_down'])
    return h, state

def setup_inputs(seed: int = 0) -> dict:
    key = jax.random.key(seed)
    ks = iter(jax.random.split(key, 32))
    nrm = lambda shape, scale: jax.random.normal(next(ks), shape, jnp.float32) * scale
    n_pages = PAST_LEN // PAGE_SIZE
    n_used = DEC_BATCH * n_pages
    n_phys = n_used + max(1, n_used // 4)
    win_buf = min(WINDOW, PAST_LEN)
    kv_row = (2, H_KV, HEAD_DIM)
    inputs = {
        "x_prompt": nrm((BATCH, SEQ, D_MODEL), 1.0),
        "x_sample": nrm((DEC_BATCH, DEC_SEQ, D_MODEL), 1.0),
        "cache_kv_cmp": nrm((DEPTH, n_phys, PAGE_SIZE) + kv_row, 1.0),
        "cache_kv_sel": nrm((DEPTH, n_phys, PAGE_SIZE) + kv_row, 1.0),
        "state_kv_win": nrm((DEPTH, DEC_BATCH, win_buf) + kv_row, 1.0),
        "state_conv": nrm((DEPTH, DEC_BATCH, CONV_WIDTH - 1, D_CONV), 1.0),
        "page_table": jax.random.permutation(next(ks), n_phys)[:n_used].reshape(DEC_BATCH, n_pages).astype(jnp.int32),
        "c_prompt": nrm((BATCH, D_MODEL), 1.0),
        "c_sample": nrm((DEC_BATCH, D_MODEL), 1.0),
        "w_ada": nrm((DEPTH, D_MODEL, N_SUB * 3 * D_MODEL), 0.5 * D_MODEL ** -0.5),
        "b_ada": nrm((DEPTH, N_SUB * 3 * D_MODEL), 0.02),
        "g_norm": 1.0 + nrm((DEPTH, N_SUB, D_MODEL), 0.05),
        "w_ffn1_gu": nrm((DEPTH, D_MODEL, 2 * D_FF), D_MODEL ** -0.5),
        "w_ffn1_down": nrm((DEPTH, D_FF, D_MODEL), D_FF ** -0.5),
        "w_ffn2_gu": nrm((DEPTH, D_MODEL, 2 * D_FF), D_MODEL ** -0.5),
        "w_ffn2_down": nrm((DEPTH, D_FF, D_MODEL), D_FF ** -0.5),
        "w_in": nrm((DEPTH, D_MODEL, IN_WIDTH), D_MODEL ** -0.5),
        "w_cmp1": nrm((DEPTH, 2, CMP_BLOCK, HEAD_DIM, CMP_HIDDEN), (CMP_BLOCK * HEAD_DIM) ** -0.5),
        "w_cmp2": nrm((DEPTH, 2, CMP_HIDDEN, HEAD_DIM), CMP_HIDDEN ** -0.5),
        "pe_cmp": nrm((DEPTH, 2, CMP_BLOCK, HEAD_DIM), 0.1),
        "w_conv": nrm((DEPTH, CONV_WIDTH, D_CONV), CONV_WIDTH ** -0.5),
        "w_nsa_out": nrm((DEPTH, N_HEADS * HEAD_DIM, D_MODEL), (N_HEADS * HEAD_DIM) ** -0.5),
        "w_conv_out": nrm((DEPTH, D_CONV, D_MODEL), D_CONV ** -0.5),
        "w_out": nrm((DEPTH, D_MODEL, D_MODEL), D_MODEL ** -0.5),
        "rel_bias": nrm((N_BUCKETS, N_HEADS), 0.5),
        "g_final": 1.0 + nrm((D_MODEL,), 0.05),
    }
    return inputs

def reference(x_prompt, x_sample, cache_kv_cmp, cache_kv_sel, state_kv_win, state_conv, page_table,
              c_prompt, c_sample, w_ada, b_ada, g_norm, w_ffn1_gu, w_ffn1_down, w_ffn2_gu, w_ffn2_down,
              w_in, w_cmp1, w_cmp2, pe_cmp, w_conv, w_nsa_out, w_conv_out, w_out, rel_bias, g_final):
    hp, hs = x_prompt, x_sample
    st_p, st_s = [], []
    for l in range(DEPTH):
        lw = dict(w_ada=w_ada[l], b_ada=b_ada[l], g_norm=g_norm[l], w_ffn1_gu=w_ffn1_gu[l],
                  w_ffn1_down=w_ffn1_down[l], w_ffn2_gu=w_ffn2_gu[l], w_ffn2_down=w_ffn2_down[l],
                  w_in=w_in[l], w_cmp1=w_cmp1[l], w_cmp2=w_cmp2[l], pe_cmp=pe_cmp[l], w_conv=w_conv[l],
                  w_nsa_out=w_nsa_out[l], w_conv_out=w_conv_out[l], w_out=w_out[l])
        hp, sp = decoder_layer(hp, c_prompt, lw, rel_bias, None)
        hs, ss = decoder_layer(hs, c_sample, lw, rel_bias,
                               (cache_kv_cmp[l], cache_kv_sel[l], state_kv_win[l], state_conv[l], page_table))
        st_p.append(sp)
        st_s.append(ss)
    y_prompt = rms_norm(hp, g_final)
    y_sample = rms_norm(hs, g_final)
    kv_cmp_p = jnp.stack([s[0] for s in st_p])
    kv_sel_p = jnp.stack([s[1] for s in st_p])
    kv_win_p = jnp.stack([s[2] for s in st_p])
    conv_p = jnp.stack([s[3] for s in st_p])
    kv_cmp_s = jnp.stack([s[0] for s in st_s])
    kv_sel_s = jnp.stack([s[1] for s in st_s])
    kv_win_s = jnp.stack([s[2] for s in st_s])
    conv_s = jnp.stack([s[3] for s in st_s])
    return (y_prompt, y_sample, kv_cmp_p, kv_sel_p, kv_win_p, conv_p, kv_cmp_s, kv_sel_s, kv_win_s, conv_s)


_drawn_inputs = setup_inputs


def setup_inputs(seed=0):
    import zlib

    import numpy as np

    out = dict(_drawn_inputs(seed))
    spreads = {}
    factors = {'cache_kv_cmp': 7.028, 'cache_kv_sel': 8.0, 'pe_cmp': 8.0, 'rel_bias': 5.191}
    for name, (base, spread) in spreads.items():
        noise = np.random.default_rng([zlib.crc32(name.encode()), seed]).standard_normal(out[name].shape)
        drawn = base * np.exp(spread * noise) if base else spread * noise
        out[name] = __import__('jax').numpy.asarray(drawn.astype(out[name].dtype))
    for name, factor in factors.items():
        out[name] = (out[name] * factor).astype(out[name].dtype)
    return out
```

```python
from contextlib import ExitStack

import numpy as np

import concourse.bass as bass
from concourse import mybir

F32 = mybir.dt.float32
F32R = mybir.dt.float32r
I32 = mybir.dt.int32
ALU = mybir.AluOpType
ACT = mybir.ActivationFunctionType
AX = mybir.AxisListType

P = 128
D = 1024
KD = D // P
TP, NB, SQ = 512, 8, 4
TS = NB * SQ
T = TP + TS
HT = T // 2
PA = TP - HT
DFF = 2816
KF = DFF // P
HD, NH, GQ = 64, 8, 4
PAST, PAGE = 1024, 128
NPG = PAST // PAGE
NPHYS = 80
WIN = 512
NC = 63
NCP = 31
NSEL = 14
DC = 512
KC = DC // P
NMOD = 9
EPS = 1e-6
NEG = -1e9
LA = 1155
LW = WIN + SQ - 1
SEL_W = PAST + TS
WIN_W = WIN + TS
RAWS, SPLITS = 4, 2
DOWN_K = [(0, 6), (6, 6), (12, 5), (17, 5)]
OFF_Q, OFF_KV, OFF_GN, OFF_H, OFF_B, OFF_C, OFF_MG = 0, 512, 1280, 1304, 1816, 2328, 2840

U_GU1 = 0
U_DN1 = U_GU1 + 2 * KF
U_WIN = U_DN1 + 4 * KD
U_MGB = U_WIN + 23
U_MGA = U_MGB + 2 * KD
U_NSA = U_MGA + KD
U_OUT = U_NSA + KD
U_GU2 = U_OUT + KD
U_DN2 = U_GU2 + 2 * KF
U_END = U_DN2 + 4 * KD
O_GU1 = 3
O_DN1 = O_GU1 + 2 * KF
O_WIN = O_DN1 + KD
O_MGB = O_WIN + 23
O_NSA = O_MGB + 2 * KD
O_OUT = O_NSA + KD
O_GU2 = O_OUT + KD
O_DN2 = O_GU2 + 2 * KF


def unit_k(u):
    for base in (U_DN1, U_DN2):
        if base <= u < base + 4 * KD:
            return DOWN_K[(u - base) % 4][1]
    if U_MGB <= u < U_MGA:
        return 8 if (u - U_MGB) % 2 == 0 else 4
    return 4 if U_NSA <= u < U_OUT else 8


C_ID, C_J, C_M, C_X, C_JI, C_VAL, C_END = 0, 128, 256, 384, 448, 462, 463
V_BADA, V_G, V_GF, V_WC, V_PE, V_END = 0, 72, 96, 104, 116, 148
S_SEL, S_WIN, S_CMP, S_END = 0, SEL_W, SEL_W + WIN_W, SEL_W + WIN_W + NC
S_PARTS = [(S_CMP, S_END), (S_WIN, S_CMP), (S_SEL, S_WIN)]


def build(nc, d):
    with ExitStack() as ctx:
        def sb(stack, name, shape, dt=F32):
            return stack.enter_context(nc.sbuf_tensor(name, shape, dt))

        def sem(name):
            return ctx.enter_context(nc.semaphore(name))

        h = sb(ctx, "h", [P, KD, T])
        mods = sb(ctx, "mods", [P, 72, NMOD])
        tmp = sb(ctx, "tmp", [P, 2, T])
        sg = sb(ctx, "sg", [P, 2, T])
        sq = sb(ctx, "sq", [P, T])
        ssq = sb(ctx, "ssq", [P, T])
        rinv = sb(ctx, "rinv", [P, T])
        smod = sb(ctx, "smod", [P, 2, TS])
        cst = sb(ctx, "cst", [P, C_END])
        ones = sb(ctx, "ones", [P, P])
        vec = sb(ctx, "vec", [P, V_END])
        kcT = sb(ctx, "kcT", [P, NB, NC])
        vc = sb(ctx, "vc", [NC, NB, P])
        peb = sb(ctx, "peb", [P, 2])
        sres = sb(ctx, "sres", [P, TS])
        ident = cst[:, C_ID:C_ID + P]

        s0 = ExitStack()
        w1 = sb(s0, "w1", [P, 2, 16, P])
        w2 = sb(s0, "w2", [P, 2, HD])
        ch = sb(s0, "ch", [P, 2, 2 * NPG, 8, 2, 2, 8])
        hid = sb(s0, "hid", [P, 2, 2, NB, 64])
        oneh = sb(s0, "oneh", [33, LA + LW])
        relx = sb(s0, "relx", [33, NH])
        Fsb = sb(s0, "Fsb", [NH, LA + LW])
        hank = sb(s0, "hank", [P, NH, 512])
        toep = sb(s0, "toep", [P, NH, 512])
        ada = sb(s0, "ada", [P, 2, KD, 512])
        cs = sb(s0, "cs", [P, KD, NMOD])
        csil = sb(s0, "csil", [P, KD, NMOD])
        ptab = sb(s0, "ptab", [1, NB * NPG], I32)
        s0.close()

        sr = ExitStack()
        raw = sb(sr, "raw", [P, RAWS, 8, P])
        wh = sb(sr, "wh", [P, SPLITS, 8, P], F32R)
        wl = sb(sr, "wl", [P, SPLITS, 8, P], F32R)
        uh = sb(sr, "uh", [P, KD, T], F32R)
        ul = sb(sr, "ul", [P, KD, T], F32R)
        hh = sb(sr, "hh", [P, KF, T], F32R)
        hl = sb(sr, "hl", [P, KF, T], F32R)
        sr.close()
        sa = ExitStack()
        toepg = sb(sa, "toepg", [P, GQ, 512])
        bsel = sb(sa, "bsel", [P, PAST])
        bwin = sb(sa, "bwin", [P, WIN])
        bnew0 = sb(sa, "bnew0", [P, SQ])
        bnew = sb(sa, "bnew", [P, 2, NB, SQ])
        ss = sb(sa, "ss", [P, S_END])
        pT = sb(sa, "pT", [P, 15, P])
        sx = sb(sa, "sx", [P, P])
        st = sb(sa, "st", [P, 20])
        sb(sa, "unused", [P, (RAWS + 2 * SPLITS) * D - GQ * 512 - PAST - WIN - SQ - 2 * TS - S_END - 15 * P - P - 20])

        sm = ExitStack()
        qT = sb(sm, "qT", [P, GQ, T])
        kT = sb(sm, "kT", [P, 3, T])
        vn = sb(sm, "vn", [P, 2, 5, P])
        mB = sb(sm, "mB", [P, KD, T])
        sgA = sb(sm, "sgA", [P, KD, T])
        gT = sb(sm, "gT", [24, T])
        grev = sb(sm, "grev", [24, NB, SQ])
        gq = sb(sm, "gq", [P, 4, 24])
        gs = sb(sm, "gs", [P, 2, 3])
        kcp = sb(sm, "kcp", [P, NCP])
        vcp = sb(sm, "vcp", [NCP, P])
        sm1 = ExitStack()
        vT = sb(sm1, "vT", [P, 3, T])
        uh2 = sb(sm1, "uh2", [P, KD, T], F32R)
        ul2 = sb(sm1, "ul2", [P, KD, T], F32R)
        fullp = sb(sm1, "fullp", [P, KC, 2 + TP])
        fulls = sb(sm1, "fulls", [P, KC, NB, 2 + SQ])
        yh = sb(sm1, "yh", [P, KC, T], F32R)
        yl = sb(sm1, "yl", [P, KC, T], F32R)
        sm1.close()
        sm2 = ExitStack()
        oh = sb(sm2, "oh", [P, GQ, T], F32R)
        ol = sb(sm2, "ol", [P, GQ, T], F32R)
        sm3 = ExitStack()
        kv = sb(sm3, "kv", [P, 4, NPG + 4, P])
        qb = sb(sm3, "qb", [P, 2, 4, NH, SQ])
        sp = sb(sm3, "sp", [P, 2, GQ, 512])
        pTp = sb(sm3, "pTp", [P, 2, GQ * P])
        stp = sb(sm3, "stp", [P, 2, 6, GQ])
        sm3.close()
        sm4 = ExitStack()
        w1p = sb(sm4, "w1p", [P, 2, 16, P])
        w2p = sb(sm4, "w2p", [P, 2, HD])
        chp = sb(sm4, "chp", [P, 8, 2, 2, 32])
        hidp = sb(sm4, "hidp", [P, 2, 2, 32])
        sm4.close()
        sm5 = ExitStack()
        mh = sb(sm5, "mh", [P, KD, T], F32R)
        ml = sb(sm5, "ml", [P, KD, T], F32R)
        sm5.close()
        sm2.close()
        sm.close()
        sa.close()

        PS = ctx.enter_context(nc.psum_tensor("PS", [P, 8, 512], F32))

        def out2(s):
            return PS[:, 2 * s:2 * s + 2, 0:HT]

        def halves(ap):
            return ap.rearrange("p (a t) -> p a t", a=2)

        def f(ap):
            return ap.bitcast(F32)

        consts_in = sem("consts_in")
        comp_in = sem("comp_in")
        ptab_in = sem("ptab_in")
        ch_in = [sem(f"ch_in{i}") for i in range(2)]
        bias_in = sem("bias_in")
        bias_out = sem("bias_out")
        hank_in = sem("hank_in")
        toep_out = sem("toep_out")
        x_in = sem("x_in")
        cond_in = sem("cond_in")
        ada_in = [sem(f"ada_in{i}") for i in range(2)]
        ada_used = sem("ada_used")
        ones_set = sem("ones_set")
        f_ready = sem("f_ready")
        f_copied = sem("f_copied")
        flip_ready = sem("flip_ready")
        flip_copied = sem("flip_copied")
        csil_ready = sem("csil_ready")
        ada_ready = sem("ada_ready")
        ada_copied = sem("ada_copied")
        mods_ready = sem("mods_ready")
        pe_ready = sem("pe_ready")
        pe_copied = sem("pe_copied")
        pre_ready = sem("pre_ready")
        hid_ready = sem("hid_ready")
        cmp_ready = sem("cmp_ready")
        cmp_copied = sem("cmp_copied")
        raw_in = [sem(f"raw_in{i}") for i in range(RAWS)]
        hi_ready = sem("hi_ready")
        lo_ready = sem("lo_ready")
        unit_used = sem("unit_used")
        psum_free = sem("psum_free")
        silu_ready = sem("silu_ready")
        hid_hi = sem("hid_hi")
        hid_lo = sem("hid_lo")
        h_ready = sem("h_ready")
        sq_ready = sem("sq_ready")
        ssq_ready = sem("ssq_ready")
        ssum_ready = sem("ssum_ready")
        ms_ready = sem("ms_ready")
        root_ready = sem("root_ready")
        rinv_ready = sem("rinv_ready")
        nt_ready = sem("nt_ready")
        nt_mod = sem("nt_mod")
        ns_part = sem("ns_part")
        ns_mod = sem("ns_mod")
        u_hi = sem("u_hi")
        u_lo = sem("u_lo")
        kv_ready = sem("kv_ready")
        out_done = sem("out_done")
        gn_ready = sem("gn_ready")
        sig_ready = sem("sig_ready")
        grev_ready = sem("grev_ready")
        conv_in = sem("conv_in")
        conv_set = sem("conv_set")
        y_ready = sem("y_ready")
        y_hi = sem("y_hi")
        y_lo = sem("y_lo")
        sgb_ready = sem("sgb_ready")
        sga_ready = sem("sga_ready")
        dchain = sem("dchain")
        achain = sem("achain")
        pchain = sem("pchain")
        gate_out = sem("gate_out")
        gate_in = sem("gate_in")
        compp_in = sem("compp_in")
        gv_ready = sem("gv_ready")
        gv_copied = sem("gv_copied")
        chp_ready = sem("chp_ready")
        pep_ready = sem("pep_ready")
        prep_ready = sem("prep_ready")
        hidp_ready = sem("hidp_ready")
        cmpp_ready = sem("cmpp_ready")
        cmpp_copied = sem("cmpp_copied")
        att_bias_in = sem("att_bias_in")
        toepg_in = sem("toepg_in")
        kv_in = [sem(f"kv_in{i}") for i in range(4)]
        kv_used = sem("kv_used")
        qb_ready = sem("qb_ready")
        s_scores = sem("s_scores")
        s_evac = sem("s_evac")
        s_exp = sem("s_exp")
        s_prob = sem("s_prob")
        s_gsum = sem("s_gsum")
        s_max = sem("s_max")
        s_tr = sem("s_tr")
        s_trc = sem("s_trc")
        so_hi = sem("so_hi")
        so_lo = sem("so_lo")
        p_scores = sem("p_scores")
        p_evac = sem("p_evac")
        p_max = sem("p_max")
        p_exp = sem("p_exp")
        p_prob = sem("p_prob")
        p_tr = sem("p_tr")
        p_trc = sem("p_trc")
        p_pv = sem("p_pv")
        po_hi = sem("po_hi")
        po_lo = sem("po_lo")
        m_ready = sem("m_ready")
        m_hi = sem("m_hi")
        m_lo = sem("m_lo")
        y_out_ready = sem("y_out_ready")
        y_out_sent = [sem(f"y_out_sent{i}") for i in range(2)]
        win_sent = sem("win_sent")

        class Chain:

            def __init__(self, eng, s):
                self.eng, self.s, self.n = eng, s, 0

            def __call__(self, ins):
                self.n += 1
                ins.then_inc(self.s, 1)
                self.eng.wait_ge(self.s, self.n)

        block = ctx.enter_context(nc.Block())

        def sample_o(o, g, hb, q):
            t0 = TP + 16 * hb
            return o[64 * g:64 * g + 64, :, t0:t0 + 16].rearrange("p r (b q) -> p q r b", q=SQ)[:, q]

        def sample_psum(g, hb, q):
            src = PS[64 * g:64 * g + 64, 6 + hb, 0:P].rearrange("p (b h q) -> p q h b", b=4, h=NH)
            return src[:, SQ - 1 - q, 4 * g:4 * g + 4]

        def prompt_psum(g, u):
            return PS[64 * g:64 * g + 64, 6 + u % 2, :].rearrange("p (r q) -> p r q", r=GQ)

        JOBS = [(g, i, br) for g in range(2) for i in range(4) for br in range(3)]

        TR0 = [0]
        for _, i_, br_ in JOBS:
            TR0.append(TR0[-1] + (1 if br_ == 0 else i_ + 1))

        def nkeys(i, br):
            return 8 * i + 7 if br == 0 else P * (i + 1)

        def toep_cols(i, br):
            c = 384 - P * i
            return slice(c + 31, c + 32 + 16 * (8 * i + 6), 16) if br == 0 else slice(c, 512)

        @block.sync
        def _(sp_):
            e = sp_
            e.dma_start(ptab[:, :], d["ptab"]).then_inc(ptab_in, 16)
            e.dma_start(w1[:, :, :, :], d["w1"]).then_inc(comp_in, 16)
            e.dma_start(w2[:, :, :], d["w2"]).then_inc(comp_in, 16)
            e.dma_start(vec[:, :], d["vec"]).then_inc(consts_in, 16)
            e.wait_ge(ptab_in, 16)

            def pages(t):
                for j in range(2 * NPG):
                    r = e.value_load(ptab[0:1, 16 * t + j:16 * t + j + 1], min_val=0, max_val=NPHYS - 1)
                    e.dma_start(ch[:, t % 2, j].rearrange("p a b c n -> p (a b c n)"),
                                d["cmp_pages"][bass.ds(r, 1)].rearrange("o p n -> (o p) n")
                                ).then_inc(ch_in[t % 2], 16)

            pages(0)
            e.dma_start(cst[:, :], d["cst"]).then_inc(consts_in, 16)
            e.dma_start(oneh[:, :], d["oneh"]).then_inc(bias_in, 16)
            e.dma_start(relx[:, :], d["relx"]).then_inc(bias_in, 16)
            e.dma_start(cs[:, :, :], d["cT"]).then_inc(cond_in, 16)
            pages(1)

            for j in range(2):
                e.dma_start(ada[:, j], d["w_ada"][j]).then_inc(ada_in[j], 16)
            e.dma_start(h[:, :, :], d["xT"]).then_inc(x_in, 16)
            e.wait_ge(f_copied, 4)
            e.dma_start(d["F"], Fsb[:, :]).then_inc(bias_out, 16)
            e.wait_ge(bias_out, 16)
            for hd in range(NH):
                e.dma_start(hank[:, hd, :], bass.AP(tensor=d["F"].tensor, offset=hd * (LA + LW) + 516,
                                                    ap=[[1, P], [1, 512]])).then_inc(hank_in, 16)
            for t in range(2, 4):
                e.wait_ge(pre_ready, 2 * (t - 1))
                pages(t)
            e.wait_ge(flip_copied, NH)
            e.dma_start(d["toep"], toep[:, :, :]).then_inc(toep_out, 16)
            with e.Fori(1, 9) as i:
                for j in range(2):
                    e.wait_ge(ada_used, 2 * i + j - 1)
                    e.dma_start(ada[:, j], d["w_ada"][bass.ds(2 * i + j, 1)].rearrange("o p k n -> (o p) k n")
                                ).then_inc(ada_in[j], 16)
            e.dma_start(d["win_old"], d["win_src"]).then_inc(win_sent, 16)
            e.wait_ge(ada_used, 18)
            e.wait_ge(cmp_ready, 1)
            e.wait_ge(toep_out, 16)

            def load(u, src, more=0):
                s = u % RAWS
                n = src.shape[-1] // P
                if u >= RAWS:
                    e.wait_ge(lo_ready, u - RAWS + 1 + more)
                e.dma_start(raw[:, s, 0:n, :].rearrange("p k m -> p (k m)"), src).then_inc(raw_in[s], 16)

            def row(ap, i):
                return ap[bass.ds(i, 1)].rearrange("o p n -> (o p) n")

            def ffn_loads(w_gu, w_dn, ug, ud):
                for u in range(4):
                    load(ug + u, w_gu[u])
                with e.Fori(0, KF // 2 - 1) as i:
                    for j in range(4):
                        load(ug + 4 + j, row(w_gu, 4 * i + 4 + j), 4 * i)
                with e.Fori(0, KD) as m:
                    for j, (k0, n) in enumerate(DOWN_K):
                        load(ud + j, row(w_dn, m)[:, k0 * P:(k0 + n) * P], 4 * m)

            ffn_loads(d["w_gu1"], d["w_dn1"], U_GU1, U_DN1)
            for u in range(23):
                load(U_WIN + u, d["w_in"][u])
                if u == 4:
                    e.wait_ge(unit_used, U_WIN)
                    for ct in range(KC):
                        e.dma_start(fulls[:, ct, :, 0:2], d["convT"][:, ct]).then_inc(conv_in, 16)
            for m in range(KD):
                load(U_MGB + 2 * m, d["w_in"][23 + m])
                load(U_MGB + 2 * m + 1, d["w_co"][m])
            for m in range(KD):
                load(U_MGA + m, d["w_in"][31 + m])
            e.wait_ge(psum_free, O_WIN + 10)
            for j in range(3):
                e.dma_start(d["kvT"][2 * j], kT[:, j, :]).then_inc(out_done, 16)
                e.dma_start(d["kvT"][2 * j + 1], vT[:, j, :]).then_inc(out_done, 16)
            e.wait_ge(psum_free, O_MGB)
            e.dma_start(d["conv_p"], fullp[:, :, TP:TP + 2]).then_inc(out_done, 16)
            e.dma_start(d["conv_s"], fulls[:, :, :, 2:2 + SQ]).then_inc(out_done, 16)
            e.wait_ge(grev_ready, 1)
            e.dma_start(d["gscr"], grev[:, :, :].rearrange("p b q -> p (b q)")).then_inc(gate_out, 16)
            e.wait_ge(gate_out, 16)
            for hb in range(2):
                for b in range(4):
                    for br in range(3):
                        e.dma_start(gs[32 * b:32 * b + 32, hb, br:br + 1],
                                    bass.AP(tensor=d["gscr"].tensor, offset=br * NH * TS + SQ * (4 * hb + b),
                                            ap=[[TS, NH], [1, SQ], [1, 1]])).then_inc(gate_in, 16)
            e.wait_ge(sga_ready, KD)
            e.wait_ge(out_done, 8 * 16)
            e.dma_start(w1p[:, :, :, :], d["w1"]).then_inc(compp_in, 16)
            e.dma_start(w2p[:, :, :], d["w2"]).then_inc(compp_in, 16)
            for b in range(4):
                r0 = 32 * b
                fd = d["F"].tensor
                L = LA + LW
                e.dma_start(bsel[r0:r0 + 32, :], bass.AP(tensor=fd, offset=0, ap=[[L, NH], [1, SQ], [1, PAST]])
                            ).then_inc(att_bias_in, 16)
                e.dma_start(bwin[r0:r0 + 32, :], bass.AP(tensor=fd, offset=LA, ap=[[L, NH], [1, SQ], [1, WIN]])
                            ).then_inc(att_bias_in, 16)
                e.dma_start(bnew0[r0:r0 + 32, :], bass.AP(tensor=fd, offset=PAST, ap=[[L, NH], [1, SQ], [1, SQ]])
                            ).then_inc(att_bias_in, 16)
            e.dma_start(toepg[:, :, :], d["toep"][:, 0:GQ, :]).then_inc(toepg_in, 16)
            e.wait_ge(cmpp_copied, 2)
            for hb in range(2):
                for v in range(2):
                    for b in range(4):
                        n = 8 * hb + 4 * v + b
                        if n >= 4:
                            e.wait_ge(kv_used, n - 3)
                        for j in range(NPG):
                            bj = (4 * hb + b) * NPG + j
                            r = e.value_load(d["ptab"][0:1, bj:bj + 1], min_val=0, max_val=NPHYS - 1)
                            e.dma_start(kv[:, b, j, :], d["sel_pages"][v][bass.ds(r, 1)].rearrange("o p n -> (o p) n")
                                        ).then_inc(kv_in[b], 16)
                        e.dma_start(kv[:, b, NPG:NPG + 4, :], d["win_tiles"][v, 4 * hb + b]).then_inc(kv_in[b], 16)
            e.wait_ge(p_evac, GQ * len(JOBS) // 2)
            e.dma_start(toepg[:, :, :], d["toep"][:, GQ:NH, :]).then_inc(toepg_in, 16)
            e.wait_ge(p_evac, GQ * len(JOBS))
            e.wait_ge(so_hi, 2)
            for m in range(KD):
                load(U_NSA + m, d["w_no"][m])
            for m in range(KD):
                load(U_OUT + m, d["w_out"][m])
            ffn_loads(d["w_gu2"], d["w_dn2"], U_GU2, U_DN2)
            for k in range(KD):
                e.wait_ge(y_out_ready, k + 1)
                e.dma_start(d["yT"][k], tmp[:, k % 2, :]).then_inc(y_out_sent[k % 2], 16)
            for s in y_out_sent:
                e.wait_ge(s, 16 * KD // 2)
            e.wait_ge(win_sent, 16)
            e.wait_ge(gate_in, 24 * 16)
            e.wait_ge(toep_out, 16)

        @block.gpsimd
        def _(e):
            e.memset(ones[:, :], 1.0).then_inc(ones_set, 1)

            def sum_squares(n):
                e.memset(ssq[:, :], 0.0).then_inc(ssq_ready, 1)
                if n == 0:
                    e.wait_ge(x_in, 16)
                with e.Fori(0, KD) as k:
                    if n:
                        e.wait_ge(h_ready, 8 * (n - 1) + 1 + k)
                    e.wait_ge(ssq_ready, 9 * n + 1 + k)
                    e.tensor_tensor(sq[:, :], h[:, bass.ds(k, 1), :].rearrange("p o t -> p (o t)"),
                                    h[:, bass.ds(k, 1), :].rearrange("p o t -> p (o t)"), ALU.mult).then_inc(sq_ready, 1)
                    e.wait_ge(sq_ready, 8 * n + 1 + k)
                    e.tensor_tensor(ssq[:, :], ssq[:, :], sq[:, :], ALU.add).then_inc(ssq_ready, 1)

            def modulate_samples(n):
                for k in range(KD):
                    c = 8 * n + k
                    t3 = tmp[:, k % 2, TP:T].rearrange("p (b q) -> p b q", b=NB)
                    s3 = smod[:, k % 2, :].rearrange("p (b q) -> p b q", b=NB)
                    gain = mods[:, 24 * n + 8 + k, 1:NMOD].unsqueeze(2).broadcast_to([P, NB, SQ])
                    shift = mods[:, 24 * n + k, 1:NMOD].unsqueeze(2).broadcast_to([P, NB, SQ])
                    e.wait_ge(nt_ready, c + 1)
                    e.tensor_tensor(s3, t3, gain, ALU.mult).then_inc(ns_part, 1)
                    e.wait_ge(ns_part, c + 1)
                    e.tensor_tensor(t3, s3, shift, ALU.add).then_inc(ns_mod, 1)

            for n in range(4):
                if n > 0:
                    e.wait_ge(ssum_ready, n)
                sum_squares(n)
                if n == 0:
                    e.wait_ge(mods_ready, 1)
                if n < 3:
                    modulate_samples(n)

        @block.scalar
        def _(e):
            e.wait_ge(cond_in, 16)
            e.activation(csil[:, :, :], cs[:, :, :], ACT.Silu).then_inc(csil_ready, 1)
            e.wait_ge(pe_copied, 1)
            for t in range(4):
                for c in range(2):
                    e.wait_ge(pre_ready, 2 * t + c + 1)
                    pre = PS[:, 2 * (t % 2) + c, 1:257].rearrange("p (g b n) -> p g b n", g=2, b=2)
                    for g in range(2):
                        ins = e.activation(hid[:, c, g, 2 * t:2 * t + 2, 0:NC], pre[:, g, :, 0:NC],
                                           ACT.Gelu_apprx_tanh, bias=peb[:, c:c + 1])
                    ins.then_inc(hid_ready, 1)

            def split(u, more=0, nk=None):
                n = nk or unit_k(u)
                e.wait_ge(raw_in[u % RAWS], 16 * (u // RAWS + 1) + 4 * more)
                if u >= SPLITS:
                    e.wait_ge(unit_used, u - SPLITS + 1 + more)
                e.activation(wh[:, u % SPLITS, 0:n, :], raw[:, u % RAWS, 0:n, :], ACT.Copy).then_inc(hi_ready, 1)

            def root(n):
                e.wait_ge(ms_ready, n + 1)
                e.activation(rinv[:, :], rinv[:, :], ACT.Sqrt).then_inc(root_ready, 1)

            def norm(n, hi):
                root(n)

                def rounded(k):
                    e.wait_ge(nt_mod, 8 * n + k + 1)
                    e.wait_ge(ns_mod, 8 * n + k + 1)
                    e.activation(hi[:, k, :], tmp[:, k % 2, :], ACT.Copy).then_inc(u_hi, 1)

                for k in range(KD):
                    e.wait_ge(nt_ready, 8 * n + k + 1)
                    e.activation(tmp[:, k % 2, 0:TP], tmp[:, k % 2, 0:TP], ACT.Identity,
                                 scale=mods[:, 24 * n + 8 + k, 0:1], bias=mods[:, 24 * n + k, 0:1]).then_inc(nt_mod, 1)
                    if k:
                        rounded(k - 1)
                rounded(KD - 1)

            def ffn(ug, ud, og):
                def tile(fi, i=0, nk=None):
                    split(ug + 2 * fi + 2, 4 * i, nk)
                    e.wait_ge(unit_used, ug + 2 * fi + 1 + 4 * i)
                    e.activation(halves(sg[:, fi % 2, :]), out2(2 * (fi % 2)), ACT.Silu).then_inc(silu_ready, 1)
                    split(ug + 2 * fi + 3, 4 * i, nk)
                    e.wait_ge(psum_free, og + 2 * fi + 2 + 4 * i)
                    dst = hh[:, fi, :] if isinstance(i, int) else \
                        hh[:, bass.ds(2 * i + fi, 1), :].rearrange("p o t -> p (o t)")
                    e.activation(dst, tmp[:, fi % 2, :], ACT.Copy).then_inc(hid_hi, 1)

                with e.Fori(0, KF // 2 - 1) as i:
                    tile(0, i)
                    tile(1, i)
                tile(KF - 2)
                tile(KF - 1)

            def down(ud):
                with e.Fori(0, KD - 1) as m:
                    for j in range(4):
                        split(ud + j + 2, 4 * m)
                for u in range(ud + 4 * KD - 2, ud + 4 * KD + 2):
                    if u < U_END:
                        split(u)

            e.wait_ge(mods_ready, 1)
            e.wait_ge(toep_out, 16)
            split(0)
            split(1)
            norm(0, uh)
            ffn(U_GU1, U_DN1, O_GU1)
            down(U_DN1)
            norm(1, uh2)
            for n in range(23):
                split(U_WIN + n + 2)
                if n == 11:
                    e.wait_ge(psum_free, O_WIN + 11)
                    e.activation(gT[:, :], gT[:, :], ACT.Sigmoid).then_inc(sig_ready, 1)
                    e.wait_ge(sig_ready, 1)
                    for q in range(SQ):
                        ins = e.activation(grev[:, :, SQ - 1 - q],
                                           gT[:, TP:T].rearrange("p (b q) -> p b q", b=NB)[:, :, q], ACT.Copy)
                    ins.then_inc(grev_ready, 1)
                if n >= 13 and (n - 13) % 3 == 0:
                    e.wait_ge(psum_free, O_WIN + n + 1)
                    e.activation(yh[:, (n - 13) // 3, :], tmp[:, 1, :], ACT.Copy).then_inc(y_hi, 1)
            for m in range(KD):
                split(U_MGB + 2 * m + 2)
                e.wait_ge(unit_used, U_MGB + 2 * m + 1)
                if m == 0:
                    e.wait_ge(psum_free, O_MGB)
                e.activation(halves(sg[:, m % 2, :]), out2(2 * (m % 2)), ACT.Sigmoid).then_inc(sgb_ready, 1)
                split(U_MGB + 2 * m + 3)
            for m in range(KD):
                if m + 2 < KD:
                    split(U_MGA + m + 2)
                e.wait_ge(unit_used, U_MGA + m + 1)
                e.activation(halves(sgA[:, m, :]), out2(m % 4), ACT.Sigmoid).then_inc(sga_ready, 1)

            for c in range(2):
                e.wait_ge(prep_ready, c + 1)
                e.activation(hidp[:, c, :, 0:NCP],
                             PS[:, c, 1:65].rearrange("p (g n) -> p g n", g=2)[:, :, 0:NCP],
                             ACT.Gelu_apprx_tanh, bias=peb[:, c:c + 1]).then_inc(hidp_ready, 1)

            for hb in range(2):
                for j, (a, b) in enumerate(S_PARTS):
                    e.wait_ge(s_max, 3 * hb + j + 1)
                    e.activation(ss[:, a:b], ss[:, a:b], ACT.Exp, bias=st[:, 3 + j:4 + j],
                                 accum_out=st[:, 6 + j:7 + j]).then_inc(s_exp, 1)
                for q in range(4):
                    e.wait_ge(s_tr, 4 * hb + q + 1)
                    if hb:
                        e.wait_ge(kv_used, 8)
                    bank = PS[:, 4 + q % 2, :].rearrange("p (a r) -> p a r", a=4)
                    if q < 3:
                        e.activation(pT[:, 4 * q:4 * q + 4, :], bank, ACT.Copy).then_inc(s_trc, 1)
                    else:
                        e.activation(pT[0:TS, 12:14, :], bank[0:TS, 0:2, :], ACT.Copy)
                        e.activation(pT[0:NC, 14, :], bank[0:NC, 2, :], ACT.Copy).then_inc(s_trc, 1)
                e.wait_ge(kv_used, 8 * hb + 8)
                e.wait_ge(out_done, 8 * 16)
                for g in range(2):
                    for q in range(SQ):
                        ins = e.activation(sample_o(oh, g, hb, q), sample_psum(g, hb, q), ACT.Copy)
                ins.then_inc(so_hi, 1)

            def p_exps(j):
                g, i, br = JOBS[j]
                n = nkeys(i, br)
                e.wait_ge(p_max, j + 1)
                for r in range(GQ):
                    e.activation(sp[:, j % 2, r, 0:n], sp[:, j % 2, r, 0:n], ACT.Exp,
                                 bias=stp[:, j % 2, 0, r:r + 1],
                                 accum_out=stp[:, j % 2, 1, r:r + 1]).then_inc(p_exp, 1)

            p_exps(0)
            for j, (g, i, br) in enumerate(JOBS):
                for tr in range(TR0[j], TR0[j + 1]):
                    n = nkeys(i, br) if br == 0 else P
                    e.wait_ge(p_tr, tr + 1)
                    if tr >= 2:
                        e.wait_ge(p_pv, tr - 1)
                    e.activation(pTp[0:n, tr % 2, :], PS[0:n, 4 + tr % 2, :], ACT.Copy).then_inc(p_trc, 1)
                if j + 1 < len(JOBS):
                    p_exps(j + 1)
                if br == 2:
                    e.wait_ge(p_pv, TR0[j + 1])
                    e.activation(oh[64 * g:64 * g + 64, :, P * i:P * i + P], prompt_psum(g, j // 3),
                                 ACT.Copy).then_inc(po_hi, 1)

            split(U_NSA)
            split(U_NSA + 1)
            for m in range(KD):
                split(U_NSA + m + 2)
                e.wait_ge(m_ready, m + 1)
                e.activation(mh[:, m, :], tmp[:, m % 2, :], ACT.Copy).then_inc(m_hi, 1)
            for u in range(U_OUT + 2, U_OUT + KD + 2):
                split(u)
            norm(2, uh)
            ffn(U_GU2, U_DN2, O_GU2)
            down(U_DN2)
            root(3)

        @block.vector
        def _(e):
            chained = [0]

            def chain(ins):
                chained[0] += 1
                ins.then_inc(dchain, 1)
                e.wait_ge(dchain, chained[0])

            e.wait_ge(pe_ready, 1)
            e.tensor_copy(peb[:, :], PS[:, 7, 0:2]).then_inc(pe_copied, 1)
            for c in range(4):
                a, b = 512 * c, min(512 * c + 512, LA + LW)
                e.wait_ge(f_ready, c + 1)
                e.tensor_copy(Fsb[:, a:b], PS[0:NH, 4 + c % 2, 0:b - a]).then_inc(f_copied, 1)
            e.wait_ge(consts_in, 32)
            for hd in range(NH):
                e.wait_ge(flip_ready, hd + 1)
                e.tensor_copy(toep[:, hd, :], PS[:, 4 + hd % 2, :]).then_inc(flip_copied, 1)
            with e.Fori(0, 9) as i:
                for j in range(2):
                    e.wait_ge(ada_used, 2 * i + j + 1)
                    e.tensor_tensor(mods[:, bass.ds(8 * i + 4 * j, 4), :],
                                    PS[:, 6 + j, 0:4 * NMOD].rearrange("p (m c) -> p m c", m=4),
                                    vec[:, bass.ds(V_BADA + 8 * i + 4 * j, 4)].unsqueeze(2).broadcast_to([P, 4, NMOD]),
                                    ALU.add).then_inc(ada_copied, 1)
            e.wait_ge(ada_copied, 18)
            for n in range(3):
                gain = mods[:, 24 * n + 8:24 * n + 16, :]
                ins = e.scalar_tensor_tensor(
                    out=gain, in0=gain, scalar=1.0,
                    in1=vec[:, V_G + 8 * n:V_G + 8 * n + 8].unsqueeze(2).broadcast_to([P, KD, NMOD]),
                    op0=ALU.add, op1=ALU.mult)
                if n != 1:
                    gate = mods[:, 24 * n + 16:24 * n + 24, :]
                    ins = e.tensor_scalar(gate, gate, 0.5, None, ALU.mult)
            ins.then_inc(mods_ready, 1)
            e.wait_ge(cmp_ready, 1)
            e.tensor_copy(kcT[:, :, :], PS[:, 0, 0:NB * NC].rearrange("p (b n) -> p b n", b=NB))
            e.tensor_copy(vc[:, :, :], PS[0:NC, 1:3, :].rearrange("p a (b f) -> p (a b) f", b=4)
                          ).then_inc(psum_free, O_GU1)
            e.wait_ge(mods_ready, 1)
            e.wait_ge(toep_out, 16)

            def lo(u, more=0, nk=None):
                n = nk or unit_k(u)
                e.wait_ge(hi_ready, u + 1 + more)
                e.tensor_tensor(wl[:, u % SPLITS, 0:n, :], raw[:, u % RAWS, 0:n, :], f(wh[:, u % SPLITS, 0:n, :]),
                                ALU.subtract).then_inc(lo_ready, 1)

            def inv_root(n):
                e.wait_ge(ssum_ready, n + 1)
                e.tensor_scalar(halves(rinv[:, :]), out2(2), 1.0 / D, EPS, ALU.mult, ALU.add).then_inc(ms_ready, 1)
                e.wait_ge(root_ready, n + 1)
                e.reciprocal(rinv[:, :], rinv[:, :]).then_inc(rinv_ready, 1)
                e.wait_ge(rinv_ready, n + 1)

            def norm(n, hi, low):
                inv_root(n)

                def scaled(k):
                    e.tensor_tensor(tmp[:, k % 2, :], h[:, k, :], rinv[:, :], ALU.mult).then_inc(nt_ready, 1)

                scaled(0)
                for k in range(KD):
                    if k + 1 < KD:
                        if k:
                            e.wait_ge(u_lo, 8 * n + k)
                        scaled(k + 1)
                    e.wait_ge(u_hi, 8 * n + k + 1)
                    e.tensor_tensor(low[:, k, :], tmp[:, k % 2, :], f(hi[:, k, :]), ALU.subtract).then_inc(u_lo, 1)
                e.wait_ge(u_lo, 8 * n + KD)

            def residual(m, more, gate, slot, of, n):
                at = slice(m, m + 1) if isinstance(more, int) else bass.ds(more + m, 1)
                gat = slice(gate + m, gate + m + 1) if isinstance(more, int) else bass.ds(more + m + gate, 1)
                ht = h[:, at, :].rearrange("p o t -> p (o t)")
                gm = mods[:, gat, :].rearrange("p o c -> p (o c)")
                o = out2(slot)
                e.scalar_tensor_tensor(out=ht[:, 0:HT], in0=o[:, 0, :], scalar=gm[:, 0:1], in1=ht[:, 0:HT],
                                       op0=ALU.mult, op1=ALU.add)
                e.scalar_tensor_tensor(out=ht[:, HT:TP], in0=o[:, 1, 0:PA], scalar=gm[:, 0:1], in1=ht[:, HT:TP],
                                       op0=ALU.mult, op1=ALU.add)
                e.tensor_tensor(sres[:, :].rearrange("p (b q) -> p b q", b=NB),
                                o[:, 1, PA:HT].rearrange("p (b q) -> p b q", b=NB),
                                gm[:, 1:NMOD].unsqueeze(2).broadcast_to([P, NB, SQ]), ALU.mult).then_inc(psum_free, 1)
                e.wait_ge(psum_free, of + m + 1 + more)
                e.tensor_tensor(ht[:, TP:T], ht[:, TP:T], sres[:, :], ALU.add).then_inc(h_ready, 1)
                e.wait_ge(h_ready, n + m + 1 + more)

            def ffn(ug, og, n):
                def tile(fi, i=0):
                    lo(ug + 2 * fi + 2, 4 * i)
                    e.wait_ge(silu_ready, KF * n + fi + 1 + 2 * i)
                    e.wait_ge(unit_used, ug + 2 * fi + 2 + 4 * i)
                    e.tensor_tensor(halves(tmp[:, fi % 2, :]), halves(sg[:, fi % 2, :]), out2(2 * (fi % 2) + 1),
                                    ALU.mult).then_inc(psum_free, 2)
                    lo(ug + 2 * fi + 3, 4 * i)
                    e.wait_ge(hid_hi, KF * n + fi + 1 + 2 * i)
                    at = slice(fi, fi + 1) if isinstance(i, int) else bass.ds(2 * i + fi, 1)
                    e.tensor_tensor(hl[:, at, :].rearrange("p o t -> p (o t)"), tmp[:, fi % 2, :],
                                    f(hh[:, at, :].rearrange("p o t -> p (o t)")), ALU.subtract).then_inc(hid_lo, 1)
                    e.wait_ge(hid_lo, KF * n + fi + 1 + 2 * i)

                with e.Fori(0, KF // 2 - 1) as i:
                    tile(0, i)
                    tile(1, i)
                tile(KF - 2)
                tile(KF - 1)

            def down(ud, od, gate, n):
                with e.Fori(0, KD // 2 - 1) as i:
                    for m in range(2):
                        for j in range(4):
                            lo(ud + 4 * m + j + 2, 8 * i)
                        e.wait_ge(unit_used, ud + 4 * m + 4 + 8 * i)
                        residual(m, 2 * i, gate, m, od, n)
                for m in range(KD - 2, KD):
                    for j in range(4):
                        if ud + 4 * m + j + 2 < U_END:
                            lo(ud + 4 * m + j + 2)
                    e.wait_ge(unit_used, ud + 4 * m + 4)
                    residual(m, 0, gate, m % 2, od, n)

            lo(0)
            lo(1)
            norm(0, uh, ul)
            ffn(U_GU1, O_GU1, 0)
            down(U_DN1, O_DN1, 16, 0)
            norm(1, uh2, ul2)
            e.memset(fullp[:, :, 0:2], 0.0).then_inc(conv_set, 1)
            for n in range(23):
                lo(U_WIN + n + 2)
                e.wait_ge(unit_used, U_WIN + n + 1)
                o = out2(n % 4)
                if n < 4:
                    e.tensor_scalar(halves(qT[:, n, :]), o, HD ** -0.5, None, ALU.mult).then_inc(psum_free, 1)
                elif n < 10:
                    dst = (kT if n % 2 == 0 else vT)[:, (n - 4) // 2, :]
                    e.tensor_copy(halves(dst), o).then_inc(psum_free, 1)
                elif n == 10:
                    e.tensor_copy(halves(gT[:, :]), o[0:24]).then_inc(psum_free, 1)
                else:
                    ct, what = divmod(n - 11, 3)
                    if what == 0:
                        e.tensor_copy(halves(tmp[:, 0, :]), o).then_inc(psum_free, 1)
                    elif what == 1:
                        e.wait_ge(psum_free, O_WIN + n)
                        e.tensor_tensor(fullp[:, ct, 2:2 + HT], o[:, 0, :], tmp[:, 0, 0:HT], ALU.mult)
                        e.tensor_tensor(fullp[:, ct, 2 + HT:2 + TP], o[:, 1, 0:PA], tmp[:, 0, HT:TP], ALU.mult)
                        e.tensor_tensor(fulls[:, ct, :, 2:2 + SQ],
                                        o[:, 1, PA:HT].rearrange("p (b q) -> p b q", b=NB),
                                        tmp[:, 0, TP:T].rearrange("p (b q) -> p b q", b=NB), ALU.mult
                                        ).then_inc(psum_free, 1)
                    else:
                        e.wait_ge(psum_free, O_WIN + n)
                        if ct == 0:
                            e.wait_ge(conv_set, 1)
                            e.wait_ge(conv_in, 16 * KC)
                        for tap in range(3):
                            w = vec[:, V_WC + 4 * tap + ct:V_WC + 4 * tap + ct + 1]
                            src, dst = sg[:, (tap + 1) % 2, :], sg[:, tap % 2, :]
                            p_in, s_in = fullp[:, ct, tap:tap + TP], fulls[:, ct, :, tap:tap + SQ]
                            s3 = dst[:, TP:T].rearrange("p (b q) -> p b q", b=NB)
                            if tap == 0:
                                e.tensor_scalar(dst[:, 0:TP], p_in, w, None, ALU.mult)
                                chain(e.tensor_scalar(s3, s_in, w, None, ALU.mult))
                            else:
                                e.scalar_tensor_tensor(out=dst[:, 0:TP], in0=p_in, scalar=w, in1=src[:, 0:TP],
                                                       op0=ALU.mult, op1=ALU.add)
                                chain(e.scalar_tensor_tensor(
                                    out=s3, in0=s_in, scalar=w,
                                    in1=src[:, TP:T].rearrange("p (b q) -> p b q", b=NB),
                                    op0=ALU.mult, op1=ALU.add))
                        e.tensor_tensor(halves(tmp[:, 1, :]), halves(sg[:, 0, :]), o, ALU.mult).then_inc(psum_free, 1)
                        e.wait_ge(y_hi, ct + 1)
                        e.tensor_tensor(yl[:, ct, :], tmp[:, 1, :], f(yh[:, ct, :]), ALU.subtract).then_inc(y_lo, 1)
            for m in range(KD):
                lo(U_MGB + 2 * m + 2)
                e.wait_ge(sgb_ready, m + 1)
                e.wait_ge(unit_used, U_MGB + 2 * m + 2)
                e.tensor_tensor(halves(mB[:, m, :]), halves(sg[:, m % 2, :]), out2(2 * (m % 2) + 1),
                                ALU.mult).then_inc(psum_free, 2)
                lo(U_MGB + 2 * m + 3)
            for m in range(2, KD):
                lo(U_MGA + m)

            e.wait_ge(sga_ready, KD)
            for c, src in enumerate((kT, vT)):
                for g in range(2):
                    for l2 in range(2):
                        e.tensor_copy(chp[64 * l2:64 * l2 + 64, :, c, g, :],
                                      src[64 * g:64 * g + 64, 0, 0:TP].rearrange("p (n lp l) -> p l lp n", lp=8, l=2)[:, l2]
                                      ).then_inc(chp_ready, 1)
            e.wait_ge(gv_ready, 1)
            for br in range(2):
                e.tensor_copy(vn[:, br, 0:4, :], PS[:, 2 * br, :].rearrange("p (t c) -> p t c", t=4))
                e.tensor_copy(vn[0:TS, br, 4, :], PS[0:TS, 2 * br + 1, 0:P])
            e.tensor_copy(gq[:, :, :], PS[:, 4, 0:96].rearrange("p (t c) -> p t c", t=4)).then_inc(gv_copied, 1)
            e.wait_ge(cmpp_ready, 1)
            e.tensor_copy(kcp[:, :], PS[:, 2, 0:NCP]).then_inc(cmpp_copied, 1)
            e.tensor_copy(vcp[:, :], PS[0:NCP, 3, 0:P]).then_inc(cmpp_copied, 1)
            e.wait_ge(out_done, 8 * 16)
            e.wait_ge(cmpp_copied, 2)
            chain(e.memset(qb[:, :, :, :, :], 0.0))
            for g in range(2):
                for q in range(SQ):
                    ins = e.tensor_copy(
                        qb[64 * g:64 * g + 64, :, :, 4 * g:4 * g + 4, SQ - 1 - q].rearrange("p a b r -> p (a b) r"),
                        qT[64 * g:64 * g + 64, :, TP:T].rearrange("p r (b q) -> p q b r", q=SQ)[:, q])
            ins.then_inc(qb_ready, 1)

            e.wait_ge(att_bias_in, 12 * 16)
            for hb in range(2):
                ins = e.tensor_tensor(bnew[:, hb, :, :], cst[:, C_X + TS * hb:C_X + TS * hb + TS].rearrange(
                    "p (b q) -> p b q", b=NB), bnew0[:, :].unsqueeze(1).broadcast_to([P, NB, SQ]), ALU.add)
            chain(ins)
            e.wait_ge(gate_in, 24 * 16)
            for hb in range(2):
                e.wait_ge(s_scores, hb + 1)
                if hb:
                    e.wait_ge(s_tr, 4)
                bn = bnew[:, hb, :, :].rearrange("p b q -> p (b q)")
                chain(e.tensor_tensor(ss[:, S_CMP:S_END], PS[:, 3, 2 * TS:2 * TS + NC], bsel[:, 31:PAST:16], ALU.add))
                e.tensor_reduce(st[:, 3:4], ss[:, S_CMP:S_END], AX.X, ALU.max, negate=True).then_inc(s_max, 1)
                e.tensor_tensor(ss[:, S_WIN:S_WIN + WIN], PS[:, 2, :], bwin[:, :], ALU.add)
                chain(e.tensor_tensor(ss[:, S_WIN + WIN:S_WIN + WIN_W], PS[:, 3, TS:2 * TS], bn, ALU.add))
                e.tensor_reduce(st[:, 4:5], ss[:, S_WIN:S_WIN + WIN_W], AX.X, ALU.max, negate=True).then_inc(s_max, 1)
                e.tensor_tensor(ss[:, 0:512], PS[:, 0, :], bsel[:, 0:512], ALU.add)
                e.tensor_tensor(ss[:, 512:1024], PS[:, 1, :], bsel[:, 512:1024], ALU.add)
                e.tensor_tensor(ss[:, PAST:SEL_W], PS[:, 3, 0:TS], bn, ALU.add).then_inc(s_evac, 1)
                e.wait_ge(s_exp, 3 * hb + 1)
                chain(e.tensor_scalar(st[:, 9:10], st[:, 6:7], 1e-30, None, ALU.max))
                chain(e.reciprocal(st[:, 10:11], st[:, 9:10]))
                e.tensor_scalar(ss[:, S_CMP:S_END], ss[:, S_CMP:S_END], st[:, 10:11], None, ALU.mult).then_inc(s_prob, 1)
                e.wait_ge(s_gsum, hb + 1)
                chain(e.tensor_copy(sx[:, 0:NC], PS[:, 4, 0:NC]))
                e.tensor_tensor(sx[:, 64:78], sx[:, 3:56:4], sx[:, 7:60:4], ALU.add)
                chain(e.tensor_tensor(sx[:, 80:94], sx[:, 4:57:4], sx[:, 5:58:4], ALU.add))
                chain(e.tensor_tensor(sx[:, 96:110], sx[:, 80:94], sx[:, 6:59:4], ALU.add))
                chain(e.scalar_tensor_tensor(out=sx[:, 112:126], in0=sx[:, 96:110], scalar=2.0, in1=sx[:, 64:78],
                                             op0=ALU.mult, op1=ALU.add))
                chain(e.tensor_reduce(st[:, 11:12], sx[:, 112:126], AX.X, ALU.min))
                chain(e.scalar_tensor_tensor(out=sx[:, 80:94], in0=sx[:, 112:126], scalar=st[:, 11:12],
                                             in1=cst[:, C_JI:C_JI + NSEL], op0=ALU.is_le, op1=ALU.mult))
                chain(e.tensor_reduce(st[:, 12:13], sx[:, 80:94], AX.X, ALU.max))
                chain(e.tensor_scalar(sx[:, 96:110], cst[:, C_JI:C_JI + NSEL], st[:, 12:13], NEG, ALU.is_equal, ALU.mult))
                e.wait_ge(s_evac, hb + 1)
                sel = ss[:, 64:960].rearrange("p (j k) -> p j k", k=64)
                chain(e.tensor_tensor(sel, sel, sx[:, 96:110].unsqueeze(2).broadcast_to([P, NSEL, 64]), ALU.add))
                e.tensor_reduce(st[:, 5:6], ss[:, 0:SEL_W], AX.X, ALU.max, negate=True).then_inc(s_max, 1)
                e.wait_ge(s_exp, 3 * hb + 3)
                chain(e.tensor_scalar(st[:, 13:15], st[:, 7:9], 1e-30, None, ALU.max))
                chain(e.reciprocal(st[:, 15:17], st[:, 13:15]))
                e.tensor_tensor(st[:, 17:18], st[:, 15:16], gs[:, hb, 2:3], ALU.mult)
                chain(e.tensor_tensor(st[:, 18:19], st[:, 16:17], gs[:, hb, 1:2], ALU.mult))
                e.tensor_scalar(ss[:, S_WIN:S_WIN + WIN_W], ss[:, S_WIN:S_WIN + WIN_W], st[:, 17:18], None, ALU.mult)
                e.tensor_scalar(ss[:, 0:SEL_W], ss[:, 0:SEL_W], st[:, 18:19], None, ALU.mult)
                e.wait_ge(s_prob, 2 * hb + 1)
                e.tensor_scalar(ss[:, S_CMP:S_END], ss[:, S_CMP:S_END], gs[:, hb, 0:1], None, ALU.mult).then_inc(s_prob, 1)
                e.wait_ge(so_hi, hb + 1)
                for g in range(2):
                    for q in range(SQ):
                        ins = e.tensor_tensor(sample_o(ol, g, hb, q), sample_psum(g, hb, q),
                                              f(sample_o(oh, g, hb, q)), ALU.subtract)
                ins.then_inc(so_lo, 1)

            def p_add(j):
                g, i, br = JOBS[j]
                n = nkeys(i, br)
                if j >= 2:
                    e.wait_ge(p_tr, TR0[j - 1])
                if j in (0, len(JOBS) // 2):
                    e.wait_ge(toepg_in, 16 * (g + 1))
                for r in range(GQ):
                    e.wait_ge(p_scores, GQ * j + r + 1)
                    e.tensor_tensor_reduce(sp[:, j % 2, r, 0:n], PS[:, r, 0:n], toepg[:, r, toep_cols(i, br)],
                                           1.0, -3e38, ALU.add, ALU.max, stp[:, j % 2, 2, r:r + 1]).then_inc(p_evac, 1)
                e.wait_ge(p_evac, GQ * (j + 1))
                e.tensor_scalar(stp[:, j % 2, 0, :], stp[:, j % 2, 2, :], -1.0, None, ALU.mult).then_inc(p_max, 1)

            def p_scale(j):
                g, i, br = JOBS[j]
                n = nkeys(i, br)
                s = stp[:, j % 2]
                e.wait_ge(p_exp, GQ * (j + 1))
                chain(e.tensor_scalar(s[:, 3, :], s[:, 1, :], 1e-30, None, ALU.max))
                chain(e.reciprocal(s[:, 4, :], s[:, 3, :]))
                chain(e.tensor_tensor(s[:, 5, :], s[:, 4, :], gq[:, i, 8 * br + 4 * g:8 * br + 4 * g + 4], ALU.mult))
                if br == 0 and i == 0:
                    chain(e.tensor_scalar(s[:, 5, :], s[:, 5, :], cst[:, C_VAL:C_VAL + 1], None, ALU.mult))
                for r in range(GQ):
                    e.tensor_scalar(sp[:, j % 2, r, 0:n], sp[:, j % 2, r, 0:n], s[:, 5, r:r + 1], None,
                                    ALU.mult).then_inc(p_prob, 1)

            p_add(0)
            for j, (g, i, br) in enumerate(JOBS):
                p_scale(j)
                if j + 1 < len(JOBS):
                    p_add(j + 1)
                if br == 2:
                    u = j // 3
                    e.wait_ge(po_hi, u + 1)
                    e.tensor_tensor(ol[64 * g:64 * g + 64, :, P * i:P * i + P], prompt_psum(g, u),
                                    f(oh[64 * g:64 * g + 64, :, P * i:P * i + P]), ALU.subtract).then_inc(po_lo, 1)

            lo(U_NSA)
            lo(U_NSA + 1)
            for m in range(KD):
                lo(U_NSA + m + 2)
                e.wait_ge(unit_used, U_NSA + m + 1)
                e.tensor_tensor(halves(tmp[:, m % 2, :]), halves(sgA[:, m, :]), out2(m % 4), ALU.mult
                                ).then_inc(psum_free, 1)
                e.wait_ge(psum_free, O_NSA + m + 1)
                e.tensor_tensor(tmp[:, m % 2, :], tmp[:, m % 2, :], mB[:, m, :], ALU.add).then_inc(m_ready, 1)
                e.wait_ge(m_hi, m + 1)
                e.tensor_tensor(ml[:, m, :], tmp[:, m % 2, :], f(mh[:, m, :]), ALU.subtract).then_inc(m_lo, 1)
            for m in range(KD):
                lo(U_OUT + m + 2)
                e.wait_ge(unit_used, U_OUT + m + 1)
                residual(m, 0, 24 + 16, m % 4, O_OUT, KD)
            norm(2, uh, ul)
            ffn(U_GU2, O_GU2, 1)
            down(U_DN2, O_DN2, 48 + 16, 2 * KD)
            inv_root(3)
            for k in range(KD):
                if k >= 2:
                    e.wait_ge(y_out_sent[k % 2], 16 * (k // 2))
                e.scalar_tensor_tensor(out=tmp[:, k % 2, :], in0=h[:, k, :], scalar=vec[:, V_GF + k:V_GF + k + 1],
                                       in1=rinv[:, :], op0=ALU.mult, op1=ALU.mult).then_inc(y_out_ready, 1)

        @block.tensor
        def _(e):
            mm = e.matmul

            e.wait_ge(comp_in, 32)
            e.wait_ge(consts_in, 32)
            for c in range(2):
                for kt in range(16):
                    ins = mm(PS[:, 7, c:c + 1], w1[:, c, kt, :], vec[:, V_PE + 16 * c + kt:V_PE + 16 * c + kt + 1],
                             start=kt == 0, stop=kt == 15)
            ins.then_inc(pe_ready, 1)
            e.wait_ge(bias_in, 32)
            for c in range(4):
                a, b = 512 * c, min(512 * c + 512, LA + LW)
                if c >= 2:
                    e.wait_ge(f_copied, c - 1)
                mm(PS[0:NH, 4 + c % 2, 0:b - a], relx[:, :], oneh[:, a:b], start=True, stop=True).then_inc(f_ready, 1)

            def compress(t):
                e.wait_ge(ch_in[t % 2], 16 * 2 * NPG * (t // 2 + 1))
                for c in range(2):
                    if t >= 2:
                        e.wait_ge(hid_ready, 2 * (t - 2) + c + 1)
                    for m in range(2):
                        for lp in range(8):
                            ins = mm(PS[:, 2 * (t % 2) + c, 1 - m:257 - m].rearrange("p (g j n) -> p g j n", g=2, n=8),
                                     w1[:, c, 8 * m + lp, :],
                                     ch[:, t % 2, :, lp, c, :, :].rearrange("p j g n -> p g j n"),
                                     start=(m + lp == 0), stop=(m == 1 and lp == 7), skip_group_check=True)
                    ins.then_inc(pre_ready, 1)

            compress(0)
            compress(1)
            e.wait_ge(hank_in, 16 * NH)
            e.wait_ge(f_copied, 4)
            for hd in range(NH):
                if hd >= 2:
                    e.wait_ge(flip_copied, hd - 1)
                mm(PS[:, 4 + hd % 2, :], cst[:, C_J:C_J + P], hank[:, hd, :], start=True, stop=True).then_inc(flip_ready, 1)
            compress(2)
            compress(3)
            e.wait_ge(hid_ready, 8)
            for g in range(2):
                mm(PS[64 * g:64 * g + 64, 0, 0:NB * NC].rearrange("p (b n) -> p b n", b=NB), w2[:, 0, :],
                   hid[:, 0, g, :, 0:NC], start=True, stop=True)
            for b in range(NB):
                for g in range(2):
                    c0 = (b % 4) * P + 64 * g
                    ins = mm(PS[0:NC, 1 + b // 4, c0:c0 + HD], hid[:, 1, g, b, 0:NC], w2[:, 1, :], start=True, stop=True)
            ins.then_inc(cmp_ready, 1)
            e.wait_ge(csil_ready, 1)
            e.wait_ge(pe_copied, 1)

            def ada_products(i, j, first):
                e.wait_ge(ada_in[j], 16 + 16 * i)
                if not first:
                    e.wait_ge(ada_copied, 2 * i + j - 1)
                for mt in range(4):
                    for k in range(KD):
                        ins = mm(PS[:, 6 + j, NMOD * mt:NMOD * mt + NMOD], ada[:, j, k, P * mt:P * mt + P],
                                 csil[:, k, :], start=(k == 0), stop=(k == KD - 1))
                ins.then_inc(ada_used, 1)

            ada_products(0, 0, True)
            ada_products(0, 1, True)
            with e.Fori(1, 9) as i:
                ada_products(i, 0, False)
                ada_products(i, 1, False)

            def unit(u, slot, xh, xl, k0, first, last, more=0, ready=None):
                n = unit_k(u)
                o = out2(slot)
                e.wait_ge(lo_ready, u + 1 + more)
                for k in range(n):
                    if ready is not None:
                        e.wait_ge(ready[0], ready[1] + k0 + k + 1)
                    for w, x in ((wh, xh), (wh, xl), (wl, xh)):
                        for a in range(2):
                            ins = mm(o[:, a, :], w[:, u % SPLITS, k, :], x[:, k0 + k, HT * a:HT * a + HT],
                                     start=(first and k == 0 and w is wh and x is xh),
                                     stop=(last and k == n - 1 and w is wl))
                ins.then_inc(unit_used, 1)

            def norm_sum(n):
                e.wait_ge(ssq_ready, 9 * n + 9)
                for a in range(2):
                    ins = mm(out2(2)[:, a, :], ones[:, :], ssq[:, HT * a:HT * a + HT], start=True, stop=True)
                ins.then_inc(ssum_ready, 1)

            def ffn(ug, og, n, nn):
                def tile(fi, i=0, ready=None):
                    e.wait_ge(psum_free, og + 2 * fi - 2 + 4 * i)
                    unit(ug + 2 * fi, 2 * (fi % 2), uh, ul, 0, True, True, 4 * i, ready)
                    unit(ug + 2 * fi + 1, 2 * (fi % 2) + 1, uh, ul, 0, True, True, 4 * i)

                tile(0, 0, (u_lo, 8 * nn))
                tile(1)
                with e.Fori(0, KF // 2 - 1) as i:
                    tile(2, i)
                    tile(3, i)

            def down(ud, od, n):
                def tile(m, i=0, ready=None):
                    e.wait_ge(psum_free, od + m - 1 + 2 * i)
                    for j, (k0, nk) in enumerate(DOWN_K):
                        unit(ud + 4 * m + j, m % 2, hh, hl, k0, j == 0, j == 3, 8 * i, ready)

                tile(0, 0, (hid_lo, KF * n))
                tile(1)
                with e.Fori(0, KD // 2 - 1) as i:
                    tile(2, i)
                    tile(3, i)

            e.wait_ge(psum_free, O_GU1)
            e.wait_ge(flip_copied, NH)
            norm_sum(0)
            ffn(U_GU1, O_GU1, 0, 0)
            down(U_DN1, O_DN1, 0)
            norm_sum(1)
            for n in range(23):
                if n >= 4:
                    e.wait_ge(psum_free, O_WIN + n - 3)
                unit(U_WIN + n, n % 4, uh2, ul2, 0, True, True, 0, (u_lo, 8) if n == 0 else None)
            for m in range(KD):
                e.wait_ge(psum_free, O_MGB - 1 + m if m < 2 else O_MGB + 2 * m - 2)
                unit(U_MGB + 2 * m, 2 * (m % 2), uh2, ul2, 0, True, True)
                unit(U_MGB + 2 * m + 1, 2 * (m % 2) + 1, yh, yl, 0, True, True, 0, (y_lo, 0) if m == 0 else None)
            for m in range(KD):
                if m < 4:
                    e.wait_ge(psum_free, O_MGB + (14 if m < 2 else 16))
                else:
                    e.wait_ge(sga_ready, m - 3)
                unit(U_MGA + m, m % 4, uh2, ul2, 0, True, True)

            e.wait_ge(sga_ready, KD)
            e.wait_ge(sig_ready, 1)
            for br in range(2):
                for t in range(5):
                    n = P if t < 4 else TS
                    dst = PS[:, 2 * br, P * t:P * t + P] if t < 4 else PS[0:TS, 2 * br + 1, 0:P]
                    e.transpose(dst, vT[:, 1 + br, P * t:P * t + n], ident)
            for t in range(4):
                ins = e.transpose(PS[:, 4, 24 * t:24 * t + 24], gT[:, P * t:P * t + P], ident[0:24, 0:24])
            ins.then_inc(gv_ready, 1)
            e.wait_ge(compp_in, 32)
            e.wait_ge(chp_ready, 8)
            e.wait_ge(gv_copied, 1)
            for c in range(2):
                for m in range(2):
                    for lp in range(8):
                        ins = mm(PS[:, c, 1 - m:65 - m].rearrange("p (g n) -> p g n", g=2), w1p[:, c, 8 * m + lp, :],
                                 chp[:, lp, c, :, :], start=(m + lp == 0), stop=(m == 1 and lp == 7),
                                 skip_group_check=True)
                ins.then_inc(prep_ready, 1)
            e.wait_ge(hidp_ready, 2)
            for g in range(2):
                mm(PS[64 * g:64 * g + 64, 2, 0:NCP], w2p[:, 0, :], hidp[:, 0, g, 0:NCP], start=True, stop=True)
                ins = mm(PS[0:NCP, 3, 64 * g:64 * g + 64], hidp[:, 1, g, 0:NCP], w2p[:, 1, :], start=True, stop=True)
            ins.then_inc(cmpp_ready, 1)

            e.wait_ge(qb_ready, 1)
            for hb in range(2):
                if hb:
                    e.wait_ge(s_evac, 1)
                q_all = qb[:, hb].rearrange("p b h q -> p (b h q)")
                for b in range(4):
                    q_b = q_all[:, 32 * b:32 * b + 32]
                    rows = slice(32 * b, 32 * b + 32)
                    e.wait_ge(kv_in[b], 144 * (2 * hb + 1))
                    for c in range(3):
                        mm(PS[rows, c, :], q_b, kv[:, b, 4 * c:4 * c + 4, :].rearrange("p t k -> p (t k)"),
                           start=True, stop=True)
                    mm(PS[rows, 3, 2 * TS:2 * TS + NC], q_b, kcT[:, 4 * hb + b, :],
                       start=True, stop=True).then_inc(kv_used, 1)
                mm(PS[:, 3, 0:TS], q_all, kT[:, 1, TP:T], start=True, stop=True)
                mm(PS[:, 3, TS:2 * TS], q_all, kT[:, 2, TP:T], start=True, stop=True).then_inc(s_scores, 1)
                e.wait_ge(s_prob, 2 * hb + 1)
                if hb:
                    e.wait_ge(s_trc, 4)
                mm(PS[:, 4, 0:NC], cst[:, C_M:C_M + P], ss[:, S_CMP:S_END], start=True, stop=True).then_inc(s_gsum, 1)
                e.wait_ge(s_prob, 2 * hb + 2)
                for x in range(15):
                    if x % 4 == 0 and 4 * hb + x // 4 - 1 > 0:
                        e.wait_ge(s_trc, 4 * hb + x // 4 - 1)
                    a, n = (P * x, P) if x < 8 else (S_WIN + P * (x - 8), P) if x < 12 else \
                        (PAST, TS) if x == 12 else (S_WIN + WIN, TS) if x == 13 else (S_CMP, NC)
                    ins = e.transpose(PS[0:n, 4 + (x // 4) % 2, P * (x % 4):P * (x % 4) + P], ss[:, a:a + n], ident)
                    if x % 4 == 3 or x == 14:
                        ins.then_inc(s_tr, 1)
                e.wait_ge(s_trc, 4 * hb + 4)
                out = PS[:, 6 + hb, 0:P]
                for br in range(2):
                    mm(out, vn[0:TS, br, 4, :], pT[0:TS, 12 + br, :], start=(br == 0), stop=False, skip_group_check=True)
                for b in range(4):
                    rows = slice(32 * b, 32 * b + 32)
                    e.wait_ge(kv_in[b], 144 * (2 * hb + 2))
                    mm(out[:, rows], vc[:, 4 * hb + b, :], pT[0:NC, 14, rows], start=False, stop=False,
                       skip_group_check=True)
                    for x in range(12):
                        ins = mm(out[:, rows], kv[:, b, x, :], pT[:, x, rows], start=False,
                                 stop=(b == 3 and x == 11), skip_group_check=True)
                    ins.then_inc(kv_used, 1)

            e.wait_ge(so_lo, 2)

            def p_score(j):
                g, i, br = JOBS[j]
                n = nkeys(i, br)
                half = slice(64 * g, 64 * g + 64)
                keys = kcp[half, 0:n] if br == 0 else kT[half, br, 0:n]
                for r in range(GQ):
                    if j:
                        e.wait_ge(p_evac, GQ * (j - 1) + r + 1)
                    mm(PS[:, r, 0:n], qT[half, r, P * i:P * i + P], keys, start=True, stop=True).then_inc(p_scores, 1)

            def p_values(j):
                g, i, br = JOBS[j]
                n = nkeys(i, br) if br == 0 else P
                u = j // 3
                out = prompt_psum(g, u)

                def turn(tr):
                    kt = tr - TR0[j]
                    if tr >= 2:
                        e.wait_ge(p_trc, tr - 1)
                    for r in range(GQ):
                        if kt == 0:
                            e.wait_ge(p_prob, GQ * j + r + 1)
                        ins = e.transpose(PS[0:n, 4 + tr % 2, P * r:P * r + P], sp[:, j % 2, r, P * kt:P * kt + n], ident)
                    ins.then_inc(p_tr, 1)

                turn(TR0[j])
                for tr in range(TR0[j], TR0[j + 1]):
                    if tr + 1 < TR0[j + 1]:
                        turn(tr + 1)
                    kt = tr - TR0[j]
                    v = vcp[0:n, 64 * g:64 * g + 64] if br == 0 else vn[:, br - 1, kt, 64 * g:64 * g + 64]
                    e.wait_ge(p_trc, tr + 1)
                    if br == 0 and u >= 2:
                        e.wait_ge(po_lo, u - 1)
                    mm(out, v, pTp[0:n, tr % 2, :].rearrange("p (r q) -> p r q", r=GQ), start=(br == 0),
                       stop=(br == 2 and tr + 1 == TR0[j + 1])).then_inc(p_pv, 1)

            p_score(0)
            for j in range(len(JOBS)):
                if j + 1 < len(JOBS):
                    p_score(j + 1)
                p_values(j)

            e.wait_ge(po_lo, 8)
            for m in range(KD):
                if m >= 4:
                    e.wait_ge(psum_free, O_NSA + m - 3)
                unit(U_NSA + m, m % 4, oh, ol, 0, True, True)
            for m in range(KD):
                e.wait_ge(psum_free, O_OUT + m - 3)
                unit(U_OUT + m, m % 4, mh, ml, 0, True, True, 0, (m_lo, 0) if m == 0 else None)
            norm_sum(2)
            ffn(U_GU2, O_GU2, 1, 2)
            down(U_DN2, O_DN2, 1)
            norm_sum(3)


def _bucket(n):
    n = np.maximum(n, 0)
    nf = np.maximum(n, 1).astype(np.float32)
    large = 16 + (np.log(nf / np.float32(16)) / np.float32(np.log(8.0)) * np.float32(16)).astype(np.int32)
    return np.where(n < 16, n, np.minimum(large, 31))


def _constants():
    cst = np.zeros((P, C_END), np.float32)
    cst[:, C_ID:C_ID + P] = np.eye(P)
    cst[:, C_J:C_J + P] = np.eye(P)[::-1]
    row = np.arange(P)
    key = (row // 32) * 100 + (row % 32 // 16) * 10 + row % 4
    cst[:, C_M:C_M + P] = key[:, None] == key[None, :]
    for hb in range(2):
        b = np.arange(TS) // SQ
        cst[:, C_X + TS * hb:C_X + TS * hb + TS] = np.where(b[None, :] == 4 * hb + row[:, None] // 32, 0.0, NEG)
    cst[:, C_JI:C_JI + NSEL] = np.arange(1, NSEL + 1)
    cst[:, C_VAL] = row >= 31
    oneh = np.zeros((33, LA + LW), np.float32)
    dist = np.concatenate([1027 - np.arange(LA), 515 - np.arange(LW)])
    seen = (dist >= 0) & ((np.arange(LA + LW) < LA) | (dist < WIN))
    oneh[np.where(seen, _bucket(dist), 32), np.arange(LA + LW)] = 1.0
    return cst, oneh


_OUTS = {
    "yT": (KD, P, T), "kvT": (6, P, T), "conv_p": (P, KC, 2), "conv_s": (P, KC, NB, SQ),
    "win_old": (NB, WIN - SQ, 256),
}
_SCRATCH = {"F": (NH, LA + LW), "toep": (P, NH, 512), "gscr": (24, TS)}


def _tiles(w, cols=P):
    k, n = w.shape
    return np.ascontiguousarray(w.reshape(k // P, P, n // cols, cols).transpose(2, 1, 0, 3)).reshape(n // cols, P, -1)


def _layout(x_prompt, x_sample, cache_kv_cmp, cache_kv_sel, state_kv_win, state_conv, page_table, c_prompt, c_sample,
            w_ada, b_ada, g_norm, w_ffn1_gu, w_ffn1_down, w_ffn2_gu, w_ffn2_down, w_in, w_cmp1, w_cmp2, pe_cmp,
            w_conv, w_nsa_out, w_conv_out, w_out, rel_bias, g_final):
    def fm(x):
        return np.ascontiguousarray(x.reshape(x.shape[0], -1, P).transpose(2, 1, 0))

    def gate_value(w):
        t = _tiles(w)
        return np.ascontiguousarray(t.reshape(2, KF, P, -1).transpose(1, 0, 2, 3)).reshape(2 * KF, P, -1)

    cst, oneh = _constants()
    w = w_in[0]
    blocks = [np.concatenate([w[:, 64 * r:64 * r + 64], w[:, 256 + 64 * r:320 + 64 * r]], 1) for r in range(4)]
    blocks += [w[:, OFF_KV + P * j:OFF_KV + P * j + P] for j in range(6)]
    blocks += [w[:, OFF_GN:OFF_GN + P]]
    for ct in range(KC):
        blocks += [w[:, o + P * ct:o + P * ct + P] for o in (OFF_C, OFF_H, OFF_B)]
    blocks += [w[:, OFF_MG + D + P * m:OFF_MG + D + P * m + P] for m in range(KD)]
    blocks += [w[:, OFF_MG + P * m:OFF_MG + P * m + P] for m in range(KD)]
    no = w_nsa_out[0].reshape(2, 4, HD, D).transpose(1, 0, 2, 3).reshape(DC, D)
    cmp_pages = cache_kv_cmp[0].reshape(NPHYS, 8, 8, 2, 2, 2, HD)
    cmp_pages = cmp_pages.transpose(0, 3, 6, 2, 4, 5, 1).reshape(NPHYS, P, 256)
    sel = cache_kv_sel[0].reshape(NPHYS, PAGE, 2, P)
    win = state_kv_win[0].reshape(NB, 4, P, 2, P)
    w1 = w_cmp1[0].reshape(2, 16, P, P).transpose(2, 0, 1, 3)
    vec = np.concatenate([b_ada[0].reshape(72, P), g_norm[0].reshape(24, P), g_final.reshape(8, P),
                          w_conv[0].reshape(12, P), pe_cmp[0].reshape(32, P)]).T
    a = {
        "ptab": page_table.reshape(1, -1),
        "w1": w1, "w2": w_cmp2[0].transpose(1, 0, 2), "vec": vec, "cst": cst, "oneh": oneh,
        "relx": np.concatenate([rel_bias, np.full((1, NH), NEG, np.float32)]),
        "cmp_pages": cmp_pages,
        "sel_pages": np.stack([sel[:, :, 0].transpose(0, 2, 1), sel[:, :, 1]]),
        "win_tiles": np.stack([win[:, :, :, 0].transpose(0, 3, 1, 2), win[:, :, :, 1].transpose(0, 2, 1, 3)]),
        "win_src": state_kv_win[0].reshape(NB, WIN, 256)[:, SQ:],
        "cT": fm(np.concatenate([c_prompt, c_sample])),
        "xT": fm(np.concatenate([x_prompt[0], x_sample.reshape(TS, D)])),
        "convT": state_conv[0].reshape(NB, 2, KC, P).transpose(3, 2, 0, 1),
        "w_ada": _tiles(w_ada[0], 512).reshape(18, P, KD, 512),
        "w_gu1": gate_value(w_ffn1_gu[0]), "w_dn1": _tiles(w_ffn1_down[0]),
        "w_gu2": gate_value(w_ffn2_gu[0]), "w_dn2": _tiles(w_ffn2_down[0]),
        "w_in": np.stack([_tiles(b)[0] for b in blocks]),
        "w_no": _tiles(no), "w_co": _tiles(w_conv_out[0]), "w_out": _tiles(w_out[0]),
    }
    return {k: np.ascontiguousarray(v) for k, v in a.items()}


def _results(r):
    y = r["yT"].transpose(2, 0, 1).reshape(T, D)
    kv = r["kvT"].reshape(3, 2, 2, HD, T).transpose(0, 4, 1, 2, 3)
    kvp = [kv[j, :TP][None, None] for j in range(3)]
    kvs = [kv[j, TP:].reshape(1, NB, SQ, 2, 2, HD) for j in range(3)]
    old = r["win_old"].reshape(1, NB, WIN - SQ, 2, 2, HD)
    win_s = np.concatenate([old, kvs[2]], axis=2)
    conv_p = r["conv_p"].transpose(2, 1, 0).reshape(1, 1, 2, DC)
    conv_s = r["conv_s"].transpose(2, 3, 1, 0).reshape(NB, SQ, DC)[None, :, SQ - 2:]
    out = (y[:TP][None], y[TP:].reshape(NB, SQ, D), kvp[0], kvp[1], kvp[2], conv_p, kvs[0], kvs[1], win_s, conv_s)
    return tuple(np.ascontiguousarray(x) for x in out)


def _program(nc, arrays):
    d = {}
    for name, a in arrays.items():
        d[name] = nc.dram_tensor("in_" + name, a.shape, mybir.dt.from_np(a.dtype), kind="ExternalInput").ap()
    for name, shape in _OUTS.items():
        d[name] = nc.dram_tensor("out_" + name, shape, F32, kind="ExternalOutput").ap()
    for name, shape in _SCRATCH.items():
        d[name] = nc.dram_tensor("scr_" + name, shape, F32, kind="Internal").ap()
    build(nc, d)


def kernel(**inputs):
    import concourse.bacc as _bacc
    from concourse.bass_utils import run_bass_kernel_spmd as _run

    nc = _bacc.Bacc("TRN2", target_bir_lowering=False, num_devices=1)
    arrays = _layout(**{k: np.asarray(v) for k, v in inputs.items()})
    _program(nc, arrays)
    r = _run(nc, [{"in_" + k: v for k, v in arrays.items()}], core_ids=[0])
    return _results({k: r.results[0]["out_" + k] for k in _OUTS})
```

```python
from contextlib import ExitStack

import numpy as np

import concourse.bass as bass
from concourse import mybir

F32 = mybir.dt.float32
F32R = mybir.dt.float32r
I32 = mybir.dt.int32
ALU = mybir.AluOpType
ACT = mybir.ActivationFunctionType
AX = mybir.AxisListType

P = 128
D = 1024
KD = D // P
TP, NB, SQ = 512, 8, 4
TS = NB * SQ
T = TP + TS
HT = T // 2
PA = TP - HT
DFF = 2816
KF = DFF // P
HD, NH, GQ = 64, 8, 4
PAST, PAGE = 1024, 128
NPG = PAST // PAGE
NPHYS = 80
WIN = 512
NC = 63
NCP = 31
NSEL = 14
DC = 512
KC = DC // P
NMOD = 9
EPS = 1e-6
NEG = -1e9
LA = 1155
LW = WIN + SQ - 1
SEL_W = PAST + TS
WIN_W = WIN + TS
RAWS, SPLITS = 4, 2
ADAS = 3
NADA = 18
DOWN_K = [(0, 6), (6, 6), (12, 5), (17, 5)]
OFF_Q, OFF_KV, OFF_GN, OFF_H, OFF_B, OFF_C, OFF_MG = 0, 512, 1280, 1304, 1816, 2328, 2840

U_GU1 = 0
U_DN1 = U_GU1 + 2 * KF
U_WIN = U_DN1 + 4 * KD
U_MGB = U_WIN + 23
U_MGA = U_MGB + 2 * KD
U_NSA = U_MGA + KD
U_OUT = U_NSA + KD
U_GU2 = U_OUT + KD
U_DN2 = U_GU2 + 2 * KF
U_END = U_DN2 + 4 * KD
O_GU1 = 3
O_DN1 = O_GU1 + 2 * KF
O_WIN = O_DN1 + KD
O_MGB = O_WIN + 23
O_NSA = O_MGB + 2 * KD
O_OUT = O_NSA + KD
O_GU2 = O_OUT + KD
O_DN2 = O_GU2 + 2 * KF


def unit_k(u):
    for base in (U_DN1, U_DN2):
        if base <= u < base + 4 * KD:
            return DOWN_K[(u - base) % 4][1]
    if U_MGB <= u < U_MGA:
        return 8 if (u - U_MGB) % 2 == 0 else 4
    return 4 if U_NSA <= u < U_OUT else 8


C_ID, C_J, C_M, C_X, C_JI, C_VAL, C_SUM, C_END = 0, 128, 256, 384, 448, 462, 463, 472
V_BADA, V_G, V_GF, V_WC, V_PE, V_END = 0, 72, 96, 104, 116, 148
S_SEL, S_WIN, S_CMP, S_END = 0, SEL_W, SEL_W + WIN_W, SEL_W + WIN_W + NC
S_PARTS = [(S_CMP, S_END), (S_WIN, S_CMP), (S_SEL, S_WIN)]


def build(nc, d):
    with ExitStack() as ctx:
        def sb(stack, name, shape, dt=F32):
            return stack.enter_context(nc.sbuf_tensor(name, shape, dt))

        def sem(name):
            return ctx.enter_context(nc.semaphore(name))

        h = sb(ctx, "h", [P, KD, T])
        mods = sb(ctx, "mods", [P, 72, NMOD])
        tmp = sb(ctx, "tmp", [P, 2, T])
        sg = sb(ctx, "sg", [P, 2, T])
        sq = sb(ctx, "sq", [P, T])
        ssq = sb(ctx, "ssq", [P, T])
        rinv = sb(ctx, "rinv", [P, T])
        smod = sb(ctx, "smod", [P, 2, TS])
        cst = sb(ctx, "cst", [P, C_END])
        ones = sb(ctx, "ones", [P, P])
        vec = sb(ctx, "vec", [P, V_END])
        kcT = sb(ctx, "kcT", [P, NB, NC])
        vc = sb(ctx, "vc", [NC, NB, P])
        peb = sb(ctx, "peb", [P, 2])
        sres = sb(ctx, "sres", [P, TS])
        ptab = sb(ctx, "ptab", [1, NB * NPG], I32)
        ident = cst[:, C_ID:C_ID + P]

        sr0 = ExitStack()
        raw = sb(sr0, "raw", [P, RAWS, 8, P])

        s0 = ExitStack()
        w1 = sb(s0, "w1", [P, 2, 16, P])
        w2 = sb(s0, "w2", [P, 2, HD])
        ch = sb(s0, "ch", [P, 2, 2 * NPG, 8, 2, 2, 8])
        hid = sb(s0, "hid", [P, 2, 2, NB, 64])
        oneh = sb(s0, "oneh", [33, LA + LW])
        relx = sb(s0, "relx", [33, NH])
        Fsb = sb(s0, "Fsb", [NH, LA + LW])
        hank = sb(s0, "hank", [P, NH, 512])
        toep = sb(s0, "toep", [P, NH, 512])
        ada = sb(s0, "ada", [P, ADAS, KD, 512])
        part = sb(s0, "part", [P, 2, 512])
        cs = sb(s0, "cs", [P, KD, NMOD])
        csil = sb(s0, "csil", [P, KD, 32])
        s0.close()

        sr = ExitStack()
        wh = sb(sr, "wh", [P, SPLITS, 8, P], F32R)
        wl = sb(sr, "wl", [P, SPLITS, 8, P], F32R)
        uh = sb(sr, "uh", [P, KD, T], F32R)
        ul = sb(sr, "ul", [P, KD, T], F32R)
        hh = sb(sr, "hh", [P, KF, T], F32R)
        hl = sb(sr, "hl", [P, KF, T], F32R)
        sr.close()
        sr0.close()
        sa = ExitStack()
        toep_g = [sb(sa, f"toep_g{g}", [P, GQ, 512]) for g in range(2)]
        bsel = sb(sa, "bsel", [P, PAST])
        bwin = sb(sa, "bwin", [P, WIN])
        bnew0 = sb(sa, "bnew0", [P, SQ])
        bnew = sb(sa, "bnew", [P, 2, NB, SQ])
        ss = sb(sa, "ss", [P, S_END])
        sx = sb(sa, "sx", [P, P])
        st = sb(sa, "st", [P, 20])
        sb(sa, "unused", [P, (RAWS + 2 * SPLITS) * D - 2 * GQ * 512 - PAST - WIN - SQ - 2 * TS - S_END - P - 20])

        sm = ExitStack()
        qT = sb(sm, "qT", [P, GQ, T])
        kT = sb(sm, "kT", [P, 3, T])
        vn = sb(sm, "vn", [P, 2, 5, P])
        mB = sb(sm, "mB", [P, KD, T])
        sgA = sb(sm, "sgA", [P, KD, T])
        gT = sb(sm, "gT", [24, T])
        grev = sb(sm, "grev", [24, NB, SQ])
        gq = sb(sm, "gq", [P, 4, 24])
        gs = sb(sm, "gs", [P, 2, 3])
        kz = sb(sm, "kz", [P, 2, 2, TP])
        kcz = sb(sm, "kcz", [P, 2, NCP])
        vcp = sb(sm, "vcp", [NCP, P])
        sm1 = ExitStack()
        vT = sb(sm1, "vT", [P, 3, T])
        uh2 = sb(sm1, "uh2", [P, KD, T], F32R)
        ul2 = sb(sm1, "ul2", [P, KD, T], F32R)
        fullp = sb(sm1, "fullp", [P, KC, 2 + TP])
        fulls = sb(sm1, "fulls", [P, KC, NB, 2 + SQ])
        yh = sb(sm1, "yh", [P, KC, T], F32R)
        yl = sb(sm1, "yl", [P, KC, T], F32R)
        sm1.close()
        sm4 = ExitStack()
        sb(sm4, "in_use", [P, 3 * T + 2 * KD * T])
        w2p = sb(sm4, "w2p", [P, 2, HD])
        chp = sb(sm4, "chp", [P, 8, 2, 2, 32])
        hidp = sb(sm4, "hidp", [P, 2, 2, 32])
        sb(sm4, "unused_conv", [P, KC * (2 + TP) + KC * NB * (2 + SQ) - 2 * HD - 8 * 128 - 128])
        w1p = sb(sm4, "w1p", [P, 2, 16, P])
        sm4.close()
        sm2 = ExitStack()
        oh = sb(sm2, "oh", [P, GQ, T], F32R)
        ol = sb(sm2, "ol", [P, GQ, T], F32R)
        sm3 = ExitStack()
        kv = sb(sm3, "kv", [P, 4, NPG + 4, P])
        qb = sb(sm3, "qb", [P, 2, 4, NH, SQ])
        pT = sb(sm3, "pT", [P, 15, P])
        sp = sb(sm3, "sp", [P, 2, GQ, 512])
        pTp = sb(sm3, "pTp", [P, 2, GQ * P])
        stp = sb(sm3, "stp", [P, 2, 6, GQ])
        sm3.close()
        sm5 = ExitStack()
        mh = sb(sm5, "mh", [P, KD, T], F32R)
        ml = sb(sm5, "ml", [P, KD, T], F32R)
        sm5.close()
        sm2.close()
        sm.close()
        sa.close()

        PS = ctx.enter_context(nc.psum_tensor("PS", [P, 8, 512], F32))

        def out2(s):
            return PS[:, 2 * s:2 * s + 2, 0:HT]

        def halves(ap):
            return ap.rearrange("p (a t) -> p a t", a=2)

        def f(ap):
            return ap.bitcast(F32)

        consts_in = sem("consts_in")
        comp_in = sem("comp_in")
        ptab_in = sem("ptab_in")
        ch_in = [sem(f"ch_in{i}") for i in range(2)]
        bias_in = sem("bias_in")
        bias_out = sem("bias_out")
        hank_in = sem("hank_in")
        toep_out = sem("toep_out")
        x_in = sem("x_in")
        cond_in = sem("cond_in")
        ada_in = [sem(f"ada_in{i}") for i in range(ADAS)]
        ada_used = sem("ada_used")
        ones_set = sem("ones_set")
        f_ready = sem("f_ready")
        f_copied = sem("f_copied")
        flip_ready = sem("flip_ready")
        flip_copied = sem("flip_copied")
        csil_zero = sem("csil_zero")
        csil_ready = sem("csil_ready")
        part_ready = sem("part_ready")
        part_copied = sem("part_copied")
        ada_copied = sem("ada_copied")
        mods_ready = sem("mods_ready")
        pe_ready = sem("pe_ready")
        pe_copied = sem("pe_copied")
        pre_ready = sem("pre_ready")
        hid_ready = sem("hid_ready")
        cmp_ready = sem("cmp_ready")
        cmp_copied = sem("cmp_copied")
        raw_in = [sem(f"raw_in{i}") for i in range(RAWS)]
        hi_ready = sem("hi_ready")
        lo_ready = sem("lo_ready")
        unit_used = sem("unit_used")
        psum_free = sem("psum_free")
        silu_ready = sem("silu_ready")
        hid_hi = sem("hid_hi")
        hid_lo = sem("hid_lo")
        h_ready = sem("h_ready")
        sq_ready = sem("sq_ready")
        ssq_ready = sem("ssq_ready")
        ssum_ready = sem("ssum_ready")
        ms_ready = sem("ms_ready")
        root_ready = sem("root_ready")
        rinv_ready = sem("rinv_ready")
        nt_ready = sem("nt_ready")
        nt_mod = sem("nt_mod")
        ns_part = sem("ns_part")
        ns_mod = sem("ns_mod")
        u_hi = sem("u_hi")
        u_lo = sem("u_lo")
        kv_ready = sem("kv_ready")
        out_done = sem("out_done")
        gn_ready = sem("gn_ready")
        sig_ready = sem("sig_ready")
        grev_ready = sem("grev_ready")
        conv_in = sem("conv_in")
        conv_set = sem("conv_set")
        y_ready = sem("y_ready")
        y_hi = sem("y_hi")
        y_lo = sem("y_lo")
        sgb_ready = sem("sgb_ready")
        sga_ready = sem("sga_ready")
        dchain = sem("dchain")
        achain = sem("achain")
        pchain = sem("pchain")
        gate_out = sem("gate_out")
        gate_in = sem("gate_in")
        compp_in = sem("compp_in")
        gv_ready = sem("gv_ready")
        gv_copied = sem("gv_copied")
        chp_ready = sem("chp_ready")
        pep_ready = sem("pep_ready")
        prep_ready = sem("prep_ready")
        hidp_ready = sem("hidp_ready")
        cmpp_ready = sem("cmpp_ready")
        cmpp_copied = sem("cmpp_copied")
        att_bias_in = sem("att_bias_in")
        toepg_in = sem("toepg_in")
        kz_zero = sem("kz_zero")
        kz_ready = sem("kz_ready")
        kv_in = [sem(f"kv_in{i}") for i in range(4)]
        v_used = sem("v_used")
        qb_ready = sem("qb_ready")
        s_work = sem("s_work")
        s_free = sem("s_free")
        s_exp = sem("s_exp")
        s_prob = sem("s_prob")
        s_max = sem("s_max")
        so_hi = sem("so_hi")
        so_lo = sem("so_lo")
        p_scores = sem("p_scores")
        p_evac = sem("p_evac")
        p_max = sem("p_max")
        p_exp = sem("p_exp")
        p_prob = sem("p_prob")
        p_tr = sem("p_tr")
        p_trc = sem("p_trc")
        p_pv = sem("p_pv")
        po_hi = sem("po_hi")
        po_lo = sem("po_lo")
        m_ready = sem("m_ready")
        m_hi = sem("m_hi")
        m_lo = sem("m_lo")
        y_out_ready = sem("y_out_ready")
        y_out_sent = [sem(f"y_out_sent{i}") for i in range(2)]
        win_sent = sem("win_sent")

        class Chain:

            def __init__(self, eng, s):
                self.eng, self.s, self.n = eng, s, 0

            def __call__(self, ins):
                self.n += 1
                ins.then_inc(self.s, 1)
                self.eng.wait_ge(self.s, self.n)

        block = ctx.enter_context(nc.Block())

        def sample_o(o, g, hb, q):
            t0 = TP + 16 * hb
            return o[64 * g:64 * g + 64, :, t0:t0 + 16].rearrange("p r (b q) -> p q r b", q=SQ)[:, q]

        def sample_psum(g, hb, q):
            src = PS[64 * g:64 * g + 64, S_BANK, 0:P].rearrange("p (b h q) -> p q h b", b=4, h=NH)
            return src[:, SQ - 1 - q, 4 * g:4 * g + 4]

        def prompt_psum(g, u):
            return PS[64 * g:64 * g + 64, 5 + u % 2, :].rearrange("p (r q) -> p r q", r=GQ)

        S_BANK, S_ITEMS, S_STEPS, S_FIRST = 7, 9, 10, 2

        def sample_step(j):
            n = j - S_FIRST
            return divmod(n, S_STEPS) if 0 <= n < 2 * S_STEPS else None

        def score_bank(j, r):
            return (GQ * j + r) % 3

        JOBS = [(g, i, br) for g in range(2) for i in range(4) for br in range(3)]

        TR0 = [0]
        for _, i_, br_ in JOBS:
            TR0.append(TR0[-1] + (1 if br_ == 0 else i_ + 1))

        def nkeys(i, br):
            return 8 * i + 7 if br == 0 else P * (i + 1)

        def toep_cols(i, br):
            c = 384 - P * i
            return slice(c + 31, c + 32 + 16 * (8 * i + 6), 16) if br == 0 else slice(c, 512)

        @block.sync
        def _(sp_):
            e = sp_
            page_regs = [e.alloc_register(f"page{j}") for j in range(NPG)]
            e.dma_start(ptab[:, :], d["ptab"]).then_inc(ptab_in, 16)
            e.dma_start(w1[:, :, :, :], d["w1"]).then_inc(comp_in, 16)
            e.dma_start(w2[:, :, :], d["w2"]).then_inc(comp_in, 16)
            e.dma_start(vec[:, :], d["vec"]).then_inc(consts_in, 16)
            e.wait_ge(ptab_in, 16)

            def pages(t):
                if t >= 2:
                    e.wait_ge(pre_ready, 2 * (t - 1))
                for j0 in range(0, 2 * NPG, NPG):
                    e.load(page_regs, ptab[0:1, 16 * t + j0:16 * t + j0 + NPG])
                    for j in range(NPG):
                        r = e.snap(page_regs[j], min_val=0, max_val=NPHYS - 1)
                        e.dma_start(ch[:, t % 2, j0 + j].rearrange("p a b c n -> p (a b c n)"),
                                    d["cmp_pages"][bass.ds(r, 1)].rearrange("o p n -> (o p) n")
                                    ).then_inc(ch_in[t % 2], 16)

            def ada_load(l):
                if l >= ADAS:
                    e.wait_ge(part_ready, l - ADAS + 1)
                e.dma_start(ada[:, l % ADAS], d["w_ada"][l]).then_inc(ada_in[l % ADAS], 16)

            pages(0)
            e.dma_start(cs[:, :, :], d["cT"]).then_inc(cond_in, 16)
            e.dma_start(cst[:, :], d["cst"]).then_inc(consts_in, 16)
            e.dma_start(oneh[:, :], d["oneh"]).then_inc(bias_in, 16)
            e.dma_start(relx[:, :], d["relx"]).then_inc(bias_in, 16)
            ada_load(0)
            pages(1)
            ada_load(1)
            ada_load(2)
            e.wait_ge(f_copied, 4)
            e.dma_start(d["F"], Fsb[:, :]).then_inc(bias_out, 16)
            e.wait_ge(bias_out, 16)
            for hd in range(NH):
                e.dma_start(hank[:, hd, :], bass.AP(tensor=d["F"].tensor, offset=hd * (LA + LW) + 516,
                                                    ap=[[1, P], [1, 512]])).then_inc(hank_in, 16)
            e.dma_start(h[:, :, :], d["xT"]).then_inc(x_in, 16)
            for g in range(1, 4):
                if g < 3:
                    pages(g + 1)
                for l in range(ADAS * g, ADAS * g + ADAS):
                    ada_load(l)
            e.wait_ge(flip_copied, NH)
            e.dma_start(d["toep"], toep[:, :, :]).then_inc(toep_out, 16)
            for u in range(RAWS):
                e.dma_start(raw[:, u, :, :].rearrange("p k m -> p (k m)"), d["w_gu1"][u]).then_inc(raw_in[u], 16)
            for l in range(4 * ADAS, NADA):
                ada_load(l)
            e.dma_start(d["win_old"], d["win_src"]).then_inc(win_sent, 16)

            def load(u, src, more=0):
                s = u % RAWS
                n = src.shape[-1] // P
                if u >= RAWS:
                    e.wait_ge(lo_ready, u - RAWS + 1 + more)
                e.dma_start(raw[:, s, 0:n, :].rearrange("p k m -> p (k m)"), src).then_inc(raw_in[s], 16)

            def row(ap, i):
                return ap[bass.ds(i, 1)].rearrange("o p n -> (o p) n")

            def ffn_loads(w_gu, w_dn, ug, ud):
                if ug:
                    for u in range(4):
                        load(ug + u, w_gu[u])
                with e.Fori(0, KF // 2 - 1) as i:
                    for j in range(4):
                        load(ug + 4 + j, row(w_gu, 4 * i + 4 + j), 4 * i)
                with e.Fori(0, KD) as m:
                    for j, (k0, n) in enumerate(DOWN_K):
                        load(ud + j, row(w_dn, m)[:, k0 * P:(k0 + n) * P], 4 * m)

            ffn_loads(d["w_gu1"], d["w_dn1"], U_GU1, U_DN1)
            for u in range(23):
                load(U_WIN + u, d["w_in"][u])
                if u == 4:
                    e.wait_ge(unit_used, U_WIN)
                    for ct in range(KC):
                        e.dma_start(fulls[:, ct, :, 0:2], d["convT"][:, ct]).then_inc(conv_in, 16)
            for m in range(KD):
                load(U_MGB + 2 * m, d["w_in"][23 + m])
                load(U_MGB + 2 * m + 1, d["w_co"][m])
            e.wait_ge(psum_free, O_WIN + 10)
            for j in range(3):
                e.dma_start(d["kvT"][2 * j], kT[:, j, :]).then_inc(out_done, 16)
                e.dma_start(d["kvT"][2 * j + 1], vT[:, j, :]).then_inc(out_done, 16)
            e.wait_ge(psum_free, O_MGB)
            e.dma_start(d["conv_p"], fullp[:, :, TP:TP + 2]).then_inc(out_done, 16)
            e.dma_start(d["conv_s"], fulls[:, :, :, 2:2 + SQ]).then_inc(out_done, 16)
            for m in range(KD):
                load(U_MGA + m, d["w_in"][31 + m])
                if m == 5:
                    e.wait_ge(unit_used, U_MGA)
                    e.dma_start(w1p[:, :, :, :], d["w1"]).then_inc(compp_in, 16)
                    e.wait_ge(out_done, 8 * 16)
                    e.dma_start(w2p[:, :, :], d["w2"]).then_inc(compp_in, 16)
            e.wait_ge(lo_ready, U_MGA + KD)
            for g in range(2):
                e.dma_start(toep_g[g][:, :, :], d["toep"][:, GQ * g:GQ * g + GQ, :]).then_inc(toepg_in, 16)
            e.wait_ge(grev_ready, 1)
            e.dma_start(d["gscr"], grev[:, :, :].rearrange("p b q -> p (b q)")).then_inc(gate_out, 16)
            e.wait_ge(unit_used, U_MGA + KD)
            for b in range(4):
                r0 = 32 * b
                fd = d["F"].tensor
                L = LA + LW
                e.dma_start(bsel[r0:r0 + 32, :], bass.AP(tensor=fd, offset=0, ap=[[L, NH], [1, SQ], [1, PAST]])
                            ).then_inc(att_bias_in, 16)
                e.dma_start(bwin[r0:r0 + 32, :], bass.AP(tensor=fd, offset=LA, ap=[[L, NH], [1, SQ], [1, WIN]])
                            ).then_inc(att_bias_in, 16)
                e.dma_start(bnew0[r0:r0 + 32, :], bass.AP(tensor=fd, offset=PAST, ap=[[L, NH], [1, SQ], [1, SQ]])
                            ).then_inc(att_bias_in, 16)

            def cached(hb, v):
                for b in range(4):
                    bj = (4 * hb + b) * NPG
                    e.load(page_regs, ptab[0:1, bj:bj + NPG])
                    for j in range(NPG):
                        r = e.snap(page_regs[j], min_val=0, max_val=NPHYS - 1)
                        e.dma_start(kv[:, b, j, :], d["sel_pages"][v][bass.ds(r, 1)].rearrange("o p n -> (o p) n")
                                    ).then_inc(kv_in[b], 16)
                    e.dma_start(kv[:, b, NPG:NPG + 4, :], d["win_tiles"][v, 4 * hb + b]).then_inc(kv_in[b], 16)

            e.wait_ge(cmpp_copied, 2)
            cached(0, 0)
            e.wait_ge(gate_out, 16)
            for hb in range(2):
                for b in range(4):
                    for br in range(3):
                        e.dma_start(gs[32 * b:32 * b + 32, hb, br:br + 1],
                                    bass.AP(tensor=d["gscr"].tensor, offset=br * NH * TS + SQ * (4 * hb + b),
                                            ap=[[TS, NH], [1, SQ], [1, 1]])).then_inc(gate_in, 16)
            e.wait_ge(s_work, 4)
            cached(0, 1)
            e.wait_ge(v_used, 1)
            cached(1, 0)
            e.wait_ge(s_work, S_ITEMS + 4)
            cached(1, 1)
            e.wait_ge(p_evac, GQ * len(JOBS))
            e.wait_ge(so_hi, 2)
            for m in range(KD):
                load(U_NSA + m, d["w_no"][m])
            for m in range(KD):
                load(U_OUT + m, d["w_out"][m])
            ffn_loads(d["w_gu2"], d["w_dn2"], U_GU2, U_DN2)
            for k in range(KD):
                e.wait_ge(y_out_ready, k + 1)
                e.dma_start(d["yT"][k], tmp[:, k % 2, :]).then_inc(y_out_sent[k % 2], 16)
            for s in y_out_sent:
                e.wait_ge(s, 16 * KD // 2)
            e.wait_ge(win_sent, 16)
            e.wait_ge(gate_in, 24 * 16)
            e.wait_ge(toep_out, 16)

        @block.gpsimd
        def _(e):
            e.memset(csil[:, :, :], 0.0).then_inc(csil_zero, 1)
            e.memset(ones[:, :], 1.0).then_inc(ones_set, 1)

            def sum_squares(n):
                e.memset(ssq[:, :], 0.0).then_inc(ssq_ready, 1)
                if n == 0:
                    e.wait_ge(x_in, 16)
                with e.Fori(0, KD) as k:
                    if n:
                        e.wait_ge(h_ready, 8 * (n - 1) + 1 + k)
                    e.wait_ge(ssq_ready, 9 * n + 1 + k)
                    e.tensor_tensor(sq[:, :], h[:, bass.ds(k, 1), :].rearrange("p o t -> p (o t)"),
                                    h[:, bass.ds(k, 1), :].rearrange("p o t -> p (o t)"), ALU.mult).then_inc(sq_ready, 1)
                    e.wait_ge(sq_ready, 8 * n + 1 + k)
                    e.tensor_tensor(ssq[:, :], ssq[:, :], sq[:, :], ALU.add).then_inc(ssq_ready, 1)

            def modulate_samples(n):
                for k in range(KD):
                    c = 8 * n + k
                    t3 = tmp[:, k % 2, TP:T].rearrange("p (b q) -> p b q", b=NB)
                    s3 = smod[:, k % 2, :].rearrange("p (b q) -> p b q", b=NB)
                    gain = mods[:, 24 * n + 8 + k, 1:NMOD].unsqueeze(2).broadcast_to([P, NB, SQ])
                    shift = mods[:, 24 * n + k, 1:NMOD].unsqueeze(2).broadcast_to([P, NB, SQ])
                    e.wait_ge(nt_ready, c + 1)
                    e.tensor_tensor(s3, t3, gain, ALU.mult).then_inc(ns_part, 1)
                    e.wait_ge(ns_part, c + 1)
                    e.tensor_tensor(t3, s3, shift, ALU.add).then_inc(ns_mod, 1)

            for n in range(4):
                if n > 0:
                    e.wait_ge(ssum_ready, n)
                sum_squares(n)
                if n == 0:
                    e.wait_ge(mods_ready, 1)
                if n < 3:
                    modulate_samples(n)
                if n == 1:
                    e.memset(kcz[:, :, :], 0.0).then_inc(kz_zero, 1)
                    e.memset(kz[:, :, :, :], 0.0).then_inc(kz_zero, 1)
                    e.wait_ge(kz_zero, 2)
                    for br in range(2):
                        e.wait_ge(psum_free, O_WIN + 7 + 2 * br)
                        for g in range(2):
                            e.tensor_copy(kz[64 * g:64 * g + 64, g, br, :], kT[64 * g:64 * g + 64, 1 + br, 0:TP]
                                          ).then_inc(kz_ready, 1)
                            e.wait_ge(kz_ready, 2 * br + g + 1)

        @block.scalar
        def _(e):
            e.wait_ge(cond_in, 16)
            e.wait_ge(csil_zero, 1)
            e.activation(csil[:, :, 0:NMOD], cs[:, :, :], ACT.Silu).then_inc(csil_ready, 1)

            def copy_part(l, more=0):
                e.wait_ge(part_ready, l + 1 + more)
                if l >= 2:
                    e.wait_ge(ada_used, l - 1 + more)
                e.activation(part[:, l % 2, :], PS[:, 6 + l % 2, :], ACT.Copy).then_inc(part_copied, 1)

            e.wait_ge(pe_copied, 1)
            for t in range(4):
                for c in range(2):
                    e.wait_ge(pre_ready, 2 * t + c + 1)
                    pre = PS[:, 2 * (t % 2) + c, 1:257].rearrange("p (g b n) -> p g b n", g=2, b=2)
                    for g in range(2):
                        ins = e.activation(hid[:, c, g, 2 * t:2 * t + 2, 0:NC], pre[:, g, :, 0:NC],
                                           ACT.Gelu_apprx_tanh, bias=peb[:, c:c + 1])
                    ins.then_inc(hid_ready, 1)
                for l in range(ADAS * t, ADAS * t + ADAS):
                    copy_part(l)
            for l in range(4 * ADAS, NADA):
                copy_part(l)

            def split(u, more=0, nk=None):
                n = nk or unit_k(u)
                e.wait_ge(raw_in[u % RAWS], 16 * (u // RAWS + 1) + 4 * more)
                if u >= SPLITS:
                    e.wait_ge(unit_used, u - SPLITS + 1 + more)
                e.activation(wh[:, u % SPLITS, 0:n, :], raw[:, u % RAWS, 0:n, :], ACT.Copy).then_inc(hi_ready, 1)

            def root(n):
                e.wait_ge(ms_ready, n + 1)
                e.activation(rinv[:, :], rinv[:, :], ACT.Sqrt).then_inc(root_ready, 1)

            def norm(n, hi):
                root(n)

                def rounded(k):
                    e.wait_ge(nt_mod, 8 * n + k + 1)
                    e.wait_ge(ns_mod, 8 * n + k + 1)
                    e.activation(hi[:, k, :], tmp[:, k % 2, :], ACT.Copy).then_inc(u_hi, 1)

                for k in range(KD):
                    e.wait_ge(nt_ready, 8 * n + k + 1)
                    e.activation(tmp[:, k % 2, 0:TP], tmp[:, k % 2, 0:TP], ACT.Identity,
                                 scale=mods[:, 24 * n + 8 + k, 0:1], bias=mods[:, 24 * n + k, 0:1]).then_inc(nt_mod, 1)
                    if k:
                        rounded(k - 1)
                rounded(KD - 1)

            def ffn(ug, ud, og):
                def tile(fi, i=0, nk=None):
                    split(ug + 2 * fi + 2, 4 * i, nk)
                    e.wait_ge(unit_used, ug + 2 * fi + 1 + 4 * i)
                    e.activation(halves(sg[:, fi % 2, :]), out2(2 * (fi % 2)), ACT.Silu).then_inc(silu_ready, 1)
                    split(ug + 2 * fi + 3, 4 * i, nk)
                    e.wait_ge(psum_free, og + 2 * fi + 2 + 4 * i)
                    dst = hh[:, fi, :] if isinstance(i, int) else \
                        hh[:, bass.ds(2 * i + fi, 1), :].rearrange("p o t -> p (o t)")
                    e.activation(dst, tmp[:, fi % 2, :], ACT.Copy).then_inc(hid_hi, 1)

                with e.Fori(0, KF // 2 - 1) as i:
                    tile(0, i)
                    tile(1, i)
                tile(KF - 2)
                tile(KF - 1)

            def down(ud):
                with e.Fori(0, KD - 1) as m:
                    for j in range(4):
                        split(ud + j + 2, 4 * m)
                for u in range(ud + 4 * KD - 2, ud + 4 * KD + 2):
                    if u < U_END:
                        split(u)

            e.wait_ge(mods_ready, 1)
            e.wait_ge(toep_out, 16)
            split(0)
            split(1)
            norm(0, uh)
            ffn(U_GU1, U_DN1, O_GU1)
            down(U_DN1)
            norm(1, uh2)
            for n in range(23):
                split(U_WIN + n + 2)
                if n == 11:
                    e.wait_ge(psum_free, O_WIN + 11)
                    e.activation(gT[:, :], gT[:, :], ACT.Sigmoid).then_inc(sig_ready, 1)
                    e.wait_ge(sig_ready, 1)
                    for q in range(SQ):
                        ins = e.activation(grev[:, :, SQ - 1 - q],
                                           gT[:, TP:T].rearrange("p (b q) -> p b q", b=NB)[:, :, q], ACT.Copy)
                    ins.then_inc(grev_ready, 1)
                if n >= 13 and (n - 13) % 3 == 0:
                    e.wait_ge(psum_free, O_WIN + n + 1)
                    e.activation(yh[:, (n - 13) // 3, :], tmp[:, 1, :], ACT.Copy).then_inc(y_hi, 1)
            for m in range(KD):
                split(U_MGB + 2 * m + 2)
                e.wait_ge(unit_used, U_MGB + 2 * m + 1)
                if m == 0:
                    e.wait_ge(psum_free, O_MGB)
                e.activation(halves(sg[:, m % 2, :]), out2(2 * (m % 2)), ACT.Sigmoid).then_inc(sgb_ready, 1)
                split(U_MGB + 2 * m + 3)
            for m in range(KD):
                if m + 2 < KD:
                    split(U_MGA + m + 2)
                e.wait_ge(unit_used, U_MGA + m + 1)
                e.activation(halves(sgA[:, m, :]), out2(m % 2), ACT.Sigmoid).then_inc(sga_ready, 1)

            for c in range(2):
                e.wait_ge(prep_ready, c + 1)
                e.activation(hidp[:, c, :, 0:NCP],
                             PS[:, 4 + c, 1:65].rearrange("p (g n) -> p g n", g=2)[:, :, 0:NCP],
                             ACT.Gelu_apprx_tanh, bias=peb[:, c:c + 1]).then_inc(hidp_ready, 1)

            def s_turned(hb, k):
                if (k, hb) == (6, 1):
                    e.wait_ge(v_used, 1)
                for q in (2 * (k - 6), 2 * (k - 6) + 1):
                    e.wait_ge(s_work, S_ITEMS * hb + 5 + q + 1)
                    bank = PS[:, S_BANK, :].rearrange("p (a r) -> p a r", a=4)
                    if q < 3:
                        e.activation(pT[:, 4 * q:4 * q + 4, :], bank, ACT.Copy).then_inc(s_free, 1)
                    else:
                        e.activation(pT[0:TS, 12:14, :], bank[0:TS, 0:2, :], ACT.Copy)
                        e.activation(pT[0:NC, 14, :], bank[0:NC, 2, :], ACT.Copy).then_inc(s_free, 1)

            def s_exps(hb, j):
                a, b = S_PARTS[j]
                e.wait_ge(s_max, 3 * hb + j + 1)
                e.activation(ss[:, a:b], ss[:, a:b], ACT.Exp, bias=st[:, 3 + j:4 + j],
                             accum_out=st[:, 6 + j:7 + j]).then_inc(s_exp, 1)

            def s_output(hb):
                e.wait_ge(v_used, hb + 1)
                for g in range(2):
                    for q in range(SQ):
                        ins = e.activation(sample_o(oh, g, hb, q), sample_psum(g, hb, q), ACT.Copy)
                ins.then_inc(so_hi, 1)

            def p_exps(j):
                g, i, br = JOBS[j]
                n = nkeys(i, br)
                e.wait_ge(p_max, j + 1)
                for r in range(GQ):
                    e.activation(sp[:, j % 2, r, 0:n], sp[:, j % 2, r, 0:n], ACT.Exp,
                                 bias=stp[:, j % 2, 0, r:r + 1],
                                 accum_out=stp[:, j % 2, 1, r:r + 1]).then_inc(p_exp, 1)

            e.wait_ge(out_done, 8 * 16)
            p_exps(0)
            for j, (g, i, br) in enumerate(JOBS):
                hb, k = sample_step(j) or (0, -1)
                if k in (6, 7):
                    s_turned(hb, k)
                for tr in range(TR0[j], TR0[j + 1]):
                    n = nkeys(i, br) if br == 0 else P
                    e.wait_ge(p_tr, tr + 1)
                    if tr >= 2:
                        e.wait_ge(p_pv, tr - 1)
                    e.activation(pTp[0:n, tr % 2, :], PS[0:n, 3 + tr % 2, :], ACT.Copy).then_inc(p_trc, 1)
                if j + 1 < len(JOBS):
                    p_exps(j + 1)
                if br == 2:
                    e.wait_ge(p_pv, TR0[j + 1])
                    e.activation(oh[64 * g:64 * g + 64, :, P * i:P * i + P], prompt_psum(g, j // 3),
                                 ACT.Copy).then_inc(po_hi, 1)
                if k in (0, 1, 4):
                    s_exps(hb, {0: 0, 1: 1, 4: 2}[k])
                if k == 9:
                    s_output(hb)

            split(U_NSA)
            split(U_NSA + 1)
            for m in range(KD):
                split(U_NSA + m + 2)
                e.wait_ge(m_ready, m + 1)
                e.activation(mh[:, m, :], tmp[:, m % 2, :], ACT.Copy).then_inc(m_hi, 1)
            for u in range(U_OUT + 2, U_OUT + KD + 2):
                split(u)
            norm(2, uh)
            ffn(U_GU2, U_DN2, O_GU2)
            down(U_DN2)
            root(3)

        @block.vector
        def _(e):
            chained = [0]

            def chain(ins):
                chained[0] += 1
                ins.then_inc(dchain, 1)
                e.wait_ge(dchain, chained[0])

            e.wait_ge(pe_ready, 1)
            e.tensor_copy(peb[:, :], PS[:, 7, 0:2]).then_inc(pe_copied, 1)
            for c in range(4):
                a, b = 512 * c, min(512 * c + 512, LA + LW)
                e.wait_ge(f_ready, c + 1)
                e.tensor_copy(Fsb[:, a:b], PS[0:NH, 4 + c % 2, 0:b - a]).then_inc(f_copied, 1)

            def add_bias(l):
                e.wait_ge(ada_used, l + 1)
                e.tensor_tensor(mods[:, 4 * l:4 * l + 4, :],
                                PS[:, 5, 0:4 * NMOD].rearrange("p (m c) -> p m c", m=4),
                                vec[:, V_BADA + 4 * l:V_BADA + 4 * l + 4].unsqueeze(2).broadcast_to([P, 4, NMOD]),
                                ALU.add).then_inc(ada_copied, 1)

            e.wait_ge(consts_in, 32)
            for l in range(NADA):
                if l == 2 * ADAS - 1:
                    for hd in range(NH):
                        e.wait_ge(flip_ready, hd + 1)
                        e.tensor_copy(toep[:, hd, :], PS[:, 4, :]).then_inc(flip_copied, 1)
                add_bias(l)
            e.wait_ge(ada_copied, NADA)
            for n in range(3):
                gain = mods[:, 24 * n + 8:24 * n + 16, :]
                ins = e.scalar_tensor_tensor(
                    out=gain, in0=gain, scalar=1.0,
                    in1=vec[:, V_G + 8 * n:V_G + 8 * n + 8].unsqueeze(2).broadcast_to([P, KD, NMOD]),
                    op0=ALU.add, op1=ALU.mult)
                if n != 1:
                    gate = mods[:, 24 * n + 16:24 * n + 24, :]
                    ins = e.tensor_scalar(gate, gate, 0.5, None, ALU.mult)
            ins.then_inc(mods_ready, 1)
            e.wait_ge(cmp_ready, 1)
            e.tensor_copy(kcT[:, :, :], PS[:, 0, 0:NB * NC].rearrange("p (b n) -> p b n", b=NB))
            e.tensor_copy(vc[:, :, :], PS[0:NC, 1:3, :].rearrange("p a (b f) -> p (a b) f", b=4)
                          ).then_inc(psum_free, O_GU1)
            e.wait_ge(mods_ready, 1)
            e.wait_ge(toep_out, 16)

            def lo(u, more=0, nk=None):
                n = nk or unit_k(u)
                e.wait_ge(hi_ready, u + 1 + more)
                e.tensor_tensor(wl[:, u % SPLITS, 0:n, :], raw[:, u % RAWS, 0:n, :], f(wh[:, u % SPLITS, 0:n, :]),
                                ALU.subtract).then_inc(lo_ready, 1)

            def inv_root(n):
                e.wait_ge(ssum_ready, n + 1)
                e.tensor_scalar(halves(rinv[:, :]), out2(2), 1.0 / D, EPS, ALU.mult, ALU.add).then_inc(ms_ready, 1)
                e.wait_ge(root_ready, n + 1)
                e.reciprocal(rinv[:, :], rinv[:, :]).then_inc(rinv_ready, 1)
                e.wait_ge(rinv_ready, n + 1)

            def norm(n, hi, low):
                inv_root(n)

                def scaled(k):
                    e.tensor_tensor(tmp[:, k % 2, :], h[:, k, :], rinv[:, :], ALU.mult).then_inc(nt_ready, 1)

                scaled(0)
                for k in range(KD):
                    if k + 1 < KD:
                        if k:
                            e.wait_ge(u_lo, 8 * n + k)
                        scaled(k + 1)
                    e.wait_ge(u_hi, 8 * n + k + 1)
                    e.tensor_tensor(low[:, k, :], tmp[:, k % 2, :], f(hi[:, k, :]), ALU.subtract).then_inc(u_lo, 1)
                e.wait_ge(u_lo, 8 * n + KD)

            def residual(m, more, gate, slot, of, n):
                at = slice(m, m + 1) if isinstance(more, int) else bass.ds(more + m, 1)
                gat = slice(gate + m, gate + m + 1) if isinstance(more, int) else bass.ds(more + m + gate, 1)
                ht = h[:, at, :].rearrange("p o t -> p (o t)")
                gm = mods[:, gat, :].rearrange("p o c -> p (o c)")
                o = out2(slot)
                e.scalar_tensor_tensor(out=ht[:, 0:HT], in0=o[:, 0, :], scalar=gm[:, 0:1], in1=ht[:, 0:HT],
                                       op0=ALU.mult, op1=ALU.add)
                e.scalar_tensor_tensor(out=ht[:, HT:TP], in0=o[:, 1, 0:PA], scalar=gm[:, 0:1], in1=ht[:, HT:TP],
                                       op0=ALU.mult, op1=ALU.add)
                e.tensor_tensor(sres[:, :].rearrange("p (b q) -> p b q", b=NB),
                                o[:, 1, PA:HT].rearrange("p (b q) -> p b q", b=NB),
                                gm[:, 1:NMOD].unsqueeze(2).broadcast_to([P, NB, SQ]), ALU.mult).then_inc(psum_free, 1)
                e.wait_ge(psum_free, of + m + 1 + more)
                e.tensor_tensor(ht[:, TP:T], ht[:, TP:T], sres[:, :], ALU.add).then_inc(h_ready, 1)
                e.wait_ge(h_ready, n + m + 1 + more)

            def ffn(ug, og, n):
                def tile(fi, i=0):
                    lo(ug + 2 * fi + 2, 4 * i)
                    e.wait_ge(silu_ready, KF * n + fi + 1 + 2 * i)
                    e.wait_ge(unit_used, ug + 2 * fi + 2 + 4 * i)
                    e.tensor_tensor(halves(tmp[:, fi % 2, :]), halves(sg[:, fi % 2, :]), out2(2 * (fi % 2) + 1),
                                    ALU.mult).then_inc(psum_free, 2)
                    lo(ug + 2 * fi + 3, 4 * i)
                    e.wait_ge(hid_hi, KF * n + fi + 1 + 2 * i)
                    at = slice(fi, fi + 1) if isinstance(i, int) else bass.ds(2 * i + fi, 1)
                    e.tensor_tensor(hl[:, at, :].rearrange("p o t -> p (o t)"), tmp[:, fi % 2, :],
                                    f(hh[:, at, :].rearrange("p o t -> p (o t)")), ALU.subtract).then_inc(hid_lo, 1)
                    e.wait_ge(hid_lo, KF * n + fi + 1 + 2 * i)

                with e.Fori(0, KF // 2 - 1) as i:
                    tile(0, i)
                    tile(1, i)
                tile(KF - 2)
                tile(KF - 1)

            def down(ud, od, gate, n):
                with e.Fori(0, KD // 2 - 1) as i:
                    for m in range(2):
                        for j in range(4):
                            lo(ud + 4 * m + j + 2, 8 * i)
                        e.wait_ge(unit_used, ud + 4 * m + 4 + 8 * i)
                        residual(m, 2 * i, gate, m, od, n)
                for m in range(KD - 2, KD):
                    for j in range(4):
                        if ud + 4 * m + j + 2 < U_END:
                            lo(ud + 4 * m + j + 2)
                    e.wait_ge(unit_used, ud + 4 * m + 4)
                    residual(m, 0, gate, m % 2, od, n)

            lo(0)
            lo(1)
            norm(0, uh, ul)
            ffn(U_GU1, O_GU1, 0)
            down(U_DN1, O_DN1, 16, 0)
            norm(1, uh2, ul2)
            e.memset(fullp[:, :, 0:2], 0.0).then_inc(conv_set, 1)
            for n in range(23):
                lo(U_WIN + n + 2)
                e.wait_ge(unit_used, U_WIN + n + 1)
                o = out2(n % 4)
                if n < 4:
                    e.tensor_scalar(halves(qT[:, n, :]), o, HD ** -0.5, None, ALU.mult).then_inc(psum_free, 1)
                elif n < 10:
                    dst = (kT if n % 2 == 0 else vT)[:, (n - 4) // 2, :]
                    e.tensor_copy(halves(dst), o).then_inc(psum_free, 1)
                elif n == 10:
                    e.tensor_copy(halves(gT[:, :]), o[0:24]).then_inc(psum_free, 1)
                else:
                    ct, what = divmod(n - 11, 3)
                    if what == 0:
                        e.tensor_copy(halves(tmp[:, 0, :]), o).then_inc(psum_free, 1)
                    elif what == 1:
                        e.wait_ge(psum_free, O_WIN + n)
                        e.tensor_tensor(fullp[:, ct, 2:2 + HT], o[:, 0, :], tmp[:, 0, 0:HT], ALU.mult)
                        e.tensor_tensor(fullp[:, ct, 2 + HT:2 + TP], o[:, 1, 0:PA], tmp[:, 0, HT:TP], ALU.mult)
                        e.tensor_tensor(fulls[:, ct, :, 2:2 + SQ],
                                        o[:, 1, PA:HT].rearrange("p (b q) -> p b q", b=NB),
                                        tmp[:, 0, TP:T].rearrange("p (b q) -> p b q", b=NB), ALU.mult
                                        ).then_inc(psum_free, 1)
                    else:
                        e.wait_ge(psum_free, O_WIN + n)
                        if ct == 0:
                            e.wait_ge(conv_set, 1)
                            e.wait_ge(conv_in, 16 * KC)
                        for tap in range(3):
                            w = vec[:, V_WC + 4 * tap + ct:V_WC + 4 * tap + ct + 1]
                            src, dst = sg[:, (tap + 1) % 2, :], sg[:, tap % 2, :]
                            p_in, s_in = fullp[:, ct, tap:tap + TP], fulls[:, ct, :, tap:tap + SQ]
                            s3 = dst[:, TP:T].rearrange("p (b q) -> p b q", b=NB)
                            if tap == 0:
                                e.tensor_scalar(dst[:, 0:TP], p_in, w, None, ALU.mult)
                                chain(e.tensor_scalar(s3, s_in, w, None, ALU.mult))
                            else:
                                e.scalar_tensor_tensor(out=dst[:, 0:TP], in0=p_in, scalar=w, in1=src[:, 0:TP],
                                                       op0=ALU.mult, op1=ALU.add)
                                chain(e.scalar_tensor_tensor(
                                    out=s3, in0=s_in, scalar=w,
                                    in1=src[:, TP:T].rearrange("p (b q) -> p b q", b=NB),
                                    op0=ALU.mult, op1=ALU.add))
                        e.tensor_tensor(halves(tmp[:, 1, :]), halves(sg[:, 0, :]), o, ALU.mult).then_inc(psum_free, 1)
                        e.wait_ge(y_hi, ct + 1)
                        e.tensor_tensor(yl[:, ct, :], tmp[:, 1, :], f(yh[:, ct, :]), ALU.subtract).then_inc(y_lo, 1)
            for m in range(KD):
                lo(U_MGB + 2 * m + 2)
                e.wait_ge(sgb_ready, m + 1)
                e.wait_ge(unit_used, U_MGB + 2 * m + 2)
                e.tensor_tensor(halves(mB[:, m, :]), halves(sg[:, m % 2, :]), out2(2 * (m % 2) + 1),
                                ALU.mult).then_inc(psum_free, 2)
                lo(U_MGB + 2 * m + 3)
            for m in range(2, KD):
                lo(U_MGA + m)
                if m == 3:
                    e.wait_ge(out_done, 8 * 16)
                    for c, src in enumerate((kT, vT)):
                        for g in range(2):
                            for l2 in range(2):
                                e.tensor_copy(
                                    chp[64 * l2:64 * l2 + 64, :, c, g, :],
                                    src[64 * g:64 * g + 64, 0, 0:TP].rearrange("p (n lp l) -> p l lp n", lp=8, l=2)[:, l2]
                                    ).then_inc(chp_ready, 1)
                if m == 5:
                    e.wait_ge(gv_ready, 1)
                    for br in range(2):
                        e.tensor_copy(vn[:, br, 0:4, :], PS[:, 4 + br, :].rearrange("p (t c) -> p t c", t=4))
                    e.tensor_copy(vn[0:TS, :, 4, :], PS[0:TS, 6, 0:2 * P].rearrange("p (b c) -> p b c", b=2))
                    e.tensor_copy(gq[:, :, :], PS[:, 7, 0:96].rearrange("p (t c) -> p t c", t=4)).then_inc(gv_copied, 1)
            e.wait_ge(cmpp_ready, 1)
            e.wait_ge(kz_zero, 2)
            for g in range(2):
                rows = slice(64 * g, 64 * g + 64)
                ins = e.tensor_copy(kcz[rows, g, :], PS[rows, 6, 0:NCP])
            ins.then_inc(cmpp_copied, 1)
            e.tensor_copy(vcp[:, :], PS[0:NCP, 7, 0:P]).then_inc(cmpp_copied, 1)

            def sample_queries():
                chain(e.memset(qb[:, :, :, :, :], 0.0))
                for g in range(2):
                    for q in range(SQ):
                        ins = e.tensor_copy(
                            qb[64 * g:64 * g + 64, :, :, 4 * g:4 * g + 4, SQ - 1 - q].rearrange("p a b r -> p (a b) r"),
                            qT[64 * g:64 * g + 64, :, TP:T].rearrange("p r (b q) -> p q b r", q=SQ)[:, q])
                ins.then_inc(qb_ready, 1)

            def s_item(hb, w):
                e.wait_ge(s_work, S_ITEMS * hb + w + 1)

            def s_read(hb, w, ins):
                ins.then_inc(s_free, 1)
                e.wait_ge(s_free, S_ITEMS * hb + w + 1)

            def s_step(hb, k):
                bank = PS[:, S_BANK, :]
                if k == 0:
                    if hb == 0:
                        e.wait_ge(att_bias_in, 12 * 16)
                        for half in range(2):
                            ins = e.tensor_tensor(
                                bnew[:, half, :, :], cst[:, C_X + TS * half:C_X + TS * half + TS].rearrange(
                                    "p (b q) -> p b q", b=NB), bnew0[:, :].unsqueeze(1).broadcast_to([P, NB, SQ]), ALU.add)
                        chain(ins)
                    bn = bnew[:, hb, :, :].rearrange("p b q -> p (b q)")
                    s_item(hb, 0)
                    e.tensor_tensor(ss[:, PAST:SEL_W], bank[:, 0:TS], bn, ALU.add)
                    e.tensor_tensor(ss[:, S_WIN + WIN:S_WIN + WIN_W], bank[:, TS:2 * TS], bn, ALU.add)
                    s_read(hb, 0, e.tensor_tensor(ss[:, S_CMP:S_END], bank[:, 2 * TS:2 * TS + NC],
                                                  bsel[:, 31:PAST:16], ALU.add))
                    e.tensor_reduce(st[:, 3:4], ss[:, S_CMP:S_END], AX.X, ALU.max, negate=True).then_inc(s_max, 1)
                elif k == 1:
                    s_item(hb, 1)
                    s_read(hb, 1, e.tensor_tensor(ss[:, S_WIN:S_WIN + WIN], bank, bwin[:, :], ALU.add))
                    e.tensor_reduce(st[:, 4:5], ss[:, S_WIN:S_WIN + WIN_W], AX.X, ALU.max, negate=True
                                    ).then_inc(s_max, 1)
                    e.wait_ge(s_exp, 3 * hb + 1)
                    chain(e.tensor_scalar(st[:, 9:10], st[:, 6:7], 1e-30, None, ALU.max))
                    chain(e.reciprocal(st[:, 10:11], st[:, 9:10]))
                    e.tensor_scalar(ss[:, S_CMP:S_END], ss[:, S_CMP:S_END], st[:, 10:11], None, ALU.mult
                                    ).then_inc(s_prob, 1)
                elif k in (2, 3):
                    c0 = 512 * (k - 2)
                    s_item(hb, k)
                    s_read(hb, k, e.tensor_tensor(ss[:, c0:c0 + 512], bank, bsel[:, c0:c0 + 512], ALU.add))
                elif k == 4:
                    s_item(hb, 4)
                    s_read(hb, 4, e.tensor_copy(sx[:, 0:NC], bank[:, 0:NC]))
                    e.tensor_tensor(sx[:, 64:78], sx[:, 3:56:4], sx[:, 7:60:4], ALU.add)
                    chain(e.tensor_tensor(sx[:, 80:94], sx[:, 4:57:4], sx[:, 5:58:4], ALU.add))
                    chain(e.tensor_tensor(sx[:, 96:110], sx[:, 80:94], sx[:, 6:59:4], ALU.add))
                    chain(e.scalar_tensor_tensor(out=sx[:, 112:126], in0=sx[:, 96:110], scalar=2.0, in1=sx[:, 64:78],
                                                 op0=ALU.mult, op1=ALU.add))
                    chain(e.tensor_reduce(st[:, 11:12], sx[:, 112:126], AX.X, ALU.min))
                    chain(e.scalar_tensor_tensor(out=sx[:, 80:94], in0=sx[:, 112:126], scalar=st[:, 11:12],
                                                 in1=cst[:, C_JI:C_JI + NSEL], op0=ALU.is_le, op1=ALU.mult))
                    chain(e.tensor_reduce(st[:, 12:13], sx[:, 80:94], AX.X, ALU.max))
                    chain(e.tensor_scalar(sx[:, 96:110], cst[:, C_JI:C_JI + NSEL], st[:, 12:13], NEG,
                                          ALU.is_equal, ALU.mult))
                    sel = ss[:, 64:960].rearrange("p (j k) -> p j k", k=64)
                    chain(e.tensor_tensor(sel, sel, sx[:, 96:110].unsqueeze(2).broadcast_to([P, NSEL, 64]), ALU.add))
                    e.tensor_reduce(st[:, 5:6], ss[:, 0:SEL_W], AX.X, ALU.max, negate=True).then_inc(s_max, 1)
                elif k == 5:
                    if hb == 0:
                        e.wait_ge(gate_in, 24 * 16)
                    e.wait_ge(s_prob, 2 * hb + 1)
                    e.tensor_scalar(ss[:, S_CMP:S_END], ss[:, S_CMP:S_END], gs[:, hb, 0:1], None, ALU.mult)
                    e.wait_ge(s_exp, 3 * hb + 3)
                    chain(e.tensor_scalar(st[:, 13:15], st[:, 7:9], 1e-30, None, ALU.max))
                    chain(e.reciprocal(st[:, 15:17], st[:, 13:15]))
                    e.tensor_tensor(st[:, 17:18], st[:, 15:16], gs[:, hb, 2:3], ALU.mult)
                    chain(e.tensor_tensor(st[:, 18:19], st[:, 16:17], gs[:, hb, 1:2], ALU.mult))
                    e.tensor_scalar(ss[:, S_WIN:S_WIN + WIN_W], ss[:, S_WIN:S_WIN + WIN_W], st[:, 17:18], None, ALU.mult)
                    e.tensor_scalar(ss[:, 0:SEL_W], ss[:, 0:SEL_W], st[:, 18:19], None, ALU.mult).then_inc(s_prob, 1)
                elif k == 9:
                    e.wait_ge(so_hi, hb + 1)
                    for g in range(2):
                        for q in range(SQ):
                            ins = e.tensor_tensor(sample_o(ol, g, hb, q), sample_psum(g, hb, q),
                                                  f(sample_o(oh, g, hb, q)), ALU.subtract)
                    ins.then_inc(so_lo, 1)

            def p_add(j):
                g, i, br = JOBS[j]
                n = nkeys(i, br)
                if j >= 2:
                    e.wait_ge(p_tr, TR0[j - 1])
                if j == 0:
                    e.wait_ge(toepg_in, 32)
                for r in range(GQ):
                    e.wait_ge(p_scores, GQ * j + r + 1)
                    e.tensor_tensor_reduce(sp[:, j % 2, r, 0:n], PS[:, score_bank(j, r), 0:n],
                                           toep_g[g][:, r, toep_cols(i, br)],
                                           1.0, -3e38, ALU.add, ALU.max, stp[:, j % 2, 2, r:r + 1]).then_inc(p_evac, 1)
                e.wait_ge(p_evac, GQ * (j + 1))
                e.tensor_scalar(stp[:, j % 2, 0, :], stp[:, j % 2, 2, :], -1.0, None, ALU.mult).then_inc(p_max, 1)

            def p_scale(j):
                g, i, br = JOBS[j]
                n = nkeys(i, br)
                s = stp[:, j % 2]
                e.wait_ge(p_exp, GQ * (j + 1))
                chain(e.tensor_scalar(s[:, 3, :], s[:, 1, :], 1e-30, None, ALU.max))
                chain(e.reciprocal(s[:, 4, :], s[:, 3, :]))
                chain(e.tensor_tensor(s[:, 5, :], s[:, 4, :], gq[:, i, 8 * br + 4 * g:8 * br + 4 * g + 4], ALU.mult))
                if br == 0 and i == 0:
                    chain(e.tensor_scalar(s[:, 5, :], s[:, 5, :], cst[:, C_VAL:C_VAL + 1], None, ALU.mult))
                for r in range(GQ):
                    e.tensor_scalar(sp[:, j % 2, r, 0:n], sp[:, j % 2, r, 0:n], s[:, 5, r:r + 1], None,
                                    ALU.mult).then_inc(p_prob, 1)

            p_add(0)
            sample_queries()
            for j, (g, i, br) in enumerate(JOBS):
                p_scale(j)
                if j + 1 < len(JOBS):
                    p_add(j + 1)
                if sample_step(j):
                    s_step(*sample_step(j))
                if br == 2:
                    u = j // 3
                    e.wait_ge(po_hi, u + 1)
                    e.tensor_tensor(ol[64 * g:64 * g + 64, :, P * i:P * i + P], prompt_psum(g, u),
                                    f(oh[64 * g:64 * g + 64, :, P * i:P * i + P]), ALU.subtract).then_inc(po_lo, 1)

            lo(U_NSA)
            lo(U_NSA + 1)
            for m in range(KD):
                lo(U_NSA + m + 2)
                e.wait_ge(unit_used, U_NSA + m + 1)
                e.tensor_tensor(halves(tmp[:, m % 2, :]), halves(sgA[:, m, :]), out2(m % 4), ALU.mult
                                ).then_inc(psum_free, 1)
                e.wait_ge(psum_free, O_NSA + m + 1)
                e.tensor_tensor(tmp[:, m % 2, :], tmp[:, m % 2, :], mB[:, m, :], ALU.add).then_inc(m_ready, 1)
                e.wait_ge(m_hi, m + 1)
                e.tensor_tensor(ml[:, m, :], tmp[:, m % 2, :], f(mh[:, m, :]), ALU.subtract).then_inc(m_lo, 1)
            for m in range(KD):
                lo(U_OUT + m + 2)
                e.wait_ge(unit_used, U_OUT + m + 1)
                residual(m, 0, 24 + 16, m % 4, O_OUT, KD)
            norm(2, uh, ul)
            ffn(U_GU2, O_GU2, 1)
            down(U_DN2, O_DN2, 48 + 16, 2 * KD)
            inv_root(3)
            for k in range(KD):
                if k >= 2:
                    e.wait_ge(y_out_sent[k % 2], 16 * (k // 2))
                e.scalar_tensor_tensor(out=tmp[:, k % 2, :], in0=h[:, k, :], scalar=vec[:, V_GF + k:V_GF + k + 1],
                                       in1=rinv[:, :], op0=ALU.mult, op1=ALU.mult).then_inc(y_out_ready, 1)

        @block.tensor
        def _(e):
            mm = e.matmul

            e.wait_ge(comp_in, 32)
            e.wait_ge(consts_in, 32)
            for c in range(2):
                for kt in range(16):
                    ins = mm(PS[:, 7, c:c + 1], w1[:, c, kt, :], vec[:, V_PE + 16 * c + kt:V_PE + 16 * c + kt + 1],
                             start=kt == 0, stop=kt == 15)
            ins.then_inc(pe_ready, 1)
            e.wait_ge(bias_in, 32)
            for c in range(4):
                a, b = 512 * c, min(512 * c + 512, LA + LW)
                if c >= 2:
                    e.wait_ge(f_copied, c - 1)
                mm(PS[0:NH, 4 + c % 2, 0:b - a], relx[:, :], oneh[:, a:b], start=True, stop=True).then_inc(f_ready, 1)

            def compress(t):
                e.wait_ge(ch_in[t % 2], 16 * 2 * NPG * (t // 2 + 1))
                for c in range(2):
                    if t >= 2:
                        e.wait_ge(hid_ready, 2 * (t - 2) + c + 1)
                    for m in range(2):
                        for lp in range(8):
                            ins = mm(PS[:, 2 * (t % 2) + c, 1 - m:257 - m].rearrange("p (g j n) -> p g j n", g=2, n=8),
                                     w1[:, c, 8 * m + lp, :],
                                     ch[:, t % 2, :, lp, c, :, :].rearrange("p j g n -> p g j n"),
                                     start=(m + lp == 0), stop=(m == 1 and lp == 7), skip_group_check=True)
                    ins.then_inc(pre_ready, 1)

            def partial(l):
                e.wait_ge(ada_in[l % ADAS], 16 * (l // ADAS + 1))
                if l >= 2:
                    e.wait_ge(part_copied, l - 1)
                for k in range(KD):
                    q = k % 4
                    ins = mm(PS[32 * q:32 * q + 32, 6 + l % 2, :], csil[:, k, :], ada[:, l % ADAS, k, :],
                             start=(k < 4), stop=(k >= 4), skip_group_check=True)
                ins.then_inc(part_ready, 1)

            def total(l):
                e.wait_ge(part_copied, l + 1)
                if l:
                    e.wait_ge(ada_copied, l)
                for mt in range(4):
                    ins = mm(PS[:, 5, NMOD * mt:NMOD * mt + NMOD], part[:, l % 2, P * mt:P * mt + P],
                             cst[:, C_SUM:C_SUM + NMOD], start=True, stop=True)
                ins.then_inc(ada_used, 1)

            def condition(g):
                for l in range(ADAS * g, ADAS * g + ADAS):
                    partial(l)
                    if l:
                        total(l - 1)

            e.wait_ge(csil_ready, 1)
            e.wait_ge(pe_copied, 1)
            e.wait_ge(f_copied, 4)
            compress(0)
            condition(0)
            compress(1)
            condition(1)
            e.wait_ge(hank_in, 16 * NH)
            for hd in range(NH):
                if hd:
                    e.wait_ge(flip_copied, hd)
                mm(PS[:, 4, :], cst[:, C_J:C_J + P], hank[:, hd, :], start=True, stop=True).then_inc(flip_ready, 1)
            compress(2)
            condition(2)
            compress(3)
            condition(3)
            e.wait_ge(hid_ready, 8)
            for g in range(2):
                mm(PS[64 * g:64 * g + 64, 0, 0:NB * NC].rearrange("p (b n) -> p b n", b=NB), w2[:, 0, :],
                   hid[:, 0, g, :, 0:NC], start=True, stop=True)
            for b in range(NB):
                for g in range(2):
                    c0 = (b % 4) * P + 64 * g
                    ins = mm(PS[0:NC, 1 + b // 4, c0:c0 + HD], hid[:, 1, g, b, 0:NC], w2[:, 1, :], start=True, stop=True)
            ins.then_inc(cmp_ready, 1)
            condition(4)
            condition(5)
            total(NADA - 1)

            def unit(u, slot, xh, xl, k0, first, last, more=0, ready=None):
                n = unit_k(u)
                o = out2(slot)
                e.wait_ge(lo_ready, u + 1 + more)
                for k in range(n):
                    if ready is not None:
                        e.wait_ge(ready[0], ready[1] + k0 + k + 1)
                    for w, x in ((wh, xh), (wh, xl), (wl, xh)):
                        for a in range(2):
                            ins = mm(o[:, a, :], w[:, u % SPLITS, k, :], x[:, k0 + k, HT * a:HT * a + HT],
                                     start=(first and k == 0 and w is wh and x is xh),
                                     stop=(last and k == n - 1 and w is wl))
                ins.then_inc(unit_used, 1)

            def norm_sum(n):
                e.wait_ge(ssq_ready, 9 * n + 9)
                for a in range(2):
                    ins = mm(out2(2)[:, a, :], ones[:, :], ssq[:, HT * a:HT * a + HT], start=True, stop=True)
                ins.then_inc(ssum_ready, 1)

            def ffn(ug, og, n, nn):
                def tile(fi, i=0, ready=None):
                    e.wait_ge(psum_free, og + 2 * fi - 2 + 4 * i)
                    unit(ug + 2 * fi, 2 * (fi % 2), uh, ul, 0, True, True, 4 * i, ready)
                    unit(ug + 2 * fi + 1, 2 * (fi % 2) + 1, uh, ul, 0, True, True, 4 * i)

                tile(0, 0, (u_lo, 8 * nn))
                tile(1)
                with e.Fori(0, KF // 2 - 1) as i:
                    tile(2, i)
                    tile(3, i)

            def down(ud, od, n):
                def tile(m, i=0, ready=None):
                    e.wait_ge(psum_free, od + m - 1 + 2 * i)
                    for j, (k0, nk) in enumerate(DOWN_K):
                        unit(ud + 4 * m + j, m % 2, hh, hl, k0, j == 0, j == 3, 8 * i, ready)

                tile(0, 0, (hid_lo, KF * n))
                tile(1)
                with e.Fori(0, KD // 2 - 1) as i:
                    tile(2, i)
                    tile(3, i)

            e.wait_ge(psum_free, O_GU1)
            e.wait_ge(flip_copied, NH)
            norm_sum(0)
            ffn(U_GU1, O_GU1, 0, 0)
            down(U_DN1, O_DN1, 0)
            norm_sum(1)
            for n in range(23):
                if n >= 4:
                    e.wait_ge(psum_free, O_WIN + n - 3)
                unit(U_WIN + n, n % 4, uh2, ul2, 0, True, True, 0, (u_lo, 8) if n == 0 else None)
            for m in range(KD):
                e.wait_ge(psum_free, O_MGB - 1 + m if m < 2 else O_MGB + 2 * m - 2)
                unit(U_MGB + 2 * m, 2 * (m % 2), uh2, ul2, 0, True, True)
                unit(U_MGB + 2 * m + 1, 2 * (m % 2) + 1, yh, yl, 0, True, True, 0, (y_lo, 0) if m == 0 else None)
            for m in range(KD):
                if m < 2:
                    e.wait_ge(psum_free, O_MGB + 14)
                else:
                    e.wait_ge(sga_ready, m - 1)
                unit(U_MGA + m, m % 2, uh2, ul2, 0, True, True)
                if m == 2:
                    e.wait_ge(psum_free, O_MGB + 16)
                    e.wait_ge(sig_ready, 1)
                    for br in range(2):
                        for t in range(4):
                            e.transpose(PS[:, 4 + br, P * t:P * t + P], vT[:, 1 + br, P * t:P * t + P], ident)
                        e.transpose(PS[0:TS, 6, P * br:P * br + P], vT[:, 1 + br, TP:T], ident)
                    for t in range(4):
                        ins = e.transpose(PS[:, 7, 24 * t:24 * t + 24], gT[:, P * t:P * t + P], ident[0:24, 0:24])
                    ins.then_inc(gv_ready, 1)
            e.wait_ge(compp_in, 32)
            e.wait_ge(chp_ready, 8)
            e.wait_ge(gv_copied, 1)
            for c in range(2):
                for m in range(2):
                    for lp in range(8):
                        ins = mm(PS[:, 4 + c, 1 - m:65 - m].rearrange("p (g n) -> p g n", g=2), w1p[:, c, 8 * m + lp, :],
                                 chp[:, lp, c, :, :], start=(m + lp == 0), stop=(m == 1 and lp == 7),
                                 skip_group_check=True)
                ins.then_inc(prep_ready, 1)
            e.wait_ge(hidp_ready, 2)
            for g in range(2):
                mm(PS[64 * g:64 * g + 64, 6, 0:NCP], w2p[:, 0, :], hidp[:, 0, g, 0:NCP], start=True, stop=True)
                ins = mm(PS[0:NCP, 7, 64 * g:64 * g + 64], hidp[:, 1, g, 0:NCP], w2p[:, 1, :], start=True, stop=True)
            ins.then_inc(cmpp_ready, 1)
            e.wait_ge(cmpp_copied, 2)
            e.wait_ge(sga_ready, KD)
            e.wait_ge(kz_ready, 4)

            def s_step(hb, k):
                q_all = qb[:, hb].rearrange("p b h q -> p (b h q)")
                bank = PS[:, S_BANK, :]
                base = S_ITEMS * hb
                if k == 0:
                    if hb:
                        e.wait_ge(so_lo, 1)
                    else:
                        e.wait_ge(qb_ready, 1)
                    mm(bank[:, 0:TS], q_all, kT[:, 1, TP:T], start=True, stop=True)
                    mm(bank[:, TS:2 * TS], q_all, kT[:, 2, TP:T], start=True, stop=True)
                    for b in range(4):
                        rows = slice(32 * b, 32 * b + 32)
                        ins = mm(PS[rows, S_BANK, 2 * TS:2 * TS + NC], q_all[:, rows], kcT[:, 4 * hb + b, :],
                                 start=True, stop=True)
                    ins.then_inc(s_work, 1)
                elif k <= 3:
                    x0 = {1: NPG, 2: 0, 3: 4}[k]
                    e.wait_ge(s_free, base + k)
                    for b in range(4):
                        rows = slice(32 * b, 32 * b + 32)
                        if k == 1:
                            e.wait_ge(kv_in[b], 144 * (2 * hb + 1))
                        ins = mm(PS[rows, S_BANK, :], q_all[:, rows],
                                 kv[:, b, x0:x0 + 4, :].rearrange("p t k -> p (t k)"), start=True, stop=True)
                    ins.then_inc(s_work, 1)
                elif k == 4:
                    e.wait_ge(s_prob, 2 * hb + 1)
                    e.wait_ge(s_free, base + 4)
                    mm(bank[:, 0:NC], cst[:, C_M:C_M + P], ss[:, S_CMP:S_END], start=True, stop=True).then_inc(s_work, 1)
                elif k in (6, 7):
                    e.wait_ge(s_prob, 2 * hb + 2)
                    for q in (2 * (k - 6), 2 * (k - 6) + 1):
                        e.wait_ge(s_free, base + 5 + q)
                        for x in range(4 * q, min(4 * q + 4, 15)):
                            a, n = (P * x, P) if x < 8 else (S_WIN + P * (x - 8), P) if x < 12 else \
                                (PAST, TS) if x == 12 else (S_WIN + WIN, TS) if x == 13 else (S_CMP, NC)
                            ins = e.transpose(PS[0:n, S_BANK, P * (x % 4):P * (x % 4) + P], ss[:, a:a + n], ident)
                        ins.then_inc(s_work, 1)
                elif k == 8:
                    e.wait_ge(s_free, base + S_ITEMS)
                    out = bank[:, 0:P]
                    for br in range(2):
                        mm(out, vn[0:TS, br, 4, :], pT[0:TS, 12 + br, :], start=(br == 0), stop=False,
                           skip_group_check=True)
                    for b in range(4):
                        rows = slice(32 * b, 32 * b + 32)
                        e.wait_ge(kv_in[b], 144 * (2 * hb + 2))
                        mm(out[:, rows], vc[:, 4 * hb + b, :], pT[0:NC, 14, rows], start=False, stop=False,
                           skip_group_check=True)
                        for x in range(12):
                            ins = mm(out[:, rows], kv[:, b, x, :], pT[:, x, rows], start=False,
                                     stop=(b == 3 and x == 11), skip_group_check=True)
                    ins.then_inc(v_used, 1)
            def p_score(j):
                g, i, br = JOBS[j]
                n = nkeys(i, br)
                keys = kcz[:, g, 0:n] if br == 0 else kz[:, g, br - 1, 0:n]
                for r in range(GQ):
                    if GQ * j + r >= 3:
                        e.wait_ge(p_evac, GQ * j + r - 2)
                    mm(PS[:, score_bank(j, r), 0:n], qT[:, r, P * i:P * i + P], keys, start=True, stop=True
                       ).then_inc(p_scores, 1)

            def p_values(j):
                g, i, br = JOBS[j]
                n = nkeys(i, br) if br == 0 else P
                u = j // 3
                out = prompt_psum(g, u)

                def turn(tr):
                    kt = tr - TR0[j]
                    if tr >= 2:
                        e.wait_ge(p_trc, tr - 1)
                    for r in range(GQ):
                        if kt == 0:
                            e.wait_ge(p_prob, GQ * j + r + 1)
                        ins = e.transpose(PS[0:n, 3 + tr % 2, P * r:P * r + P], sp[:, j % 2, r, P * kt:P * kt + n], ident)
                    ins.then_inc(p_tr, 1)

                turn(TR0[j])
                for tr in range(TR0[j], TR0[j + 1]):
                    if tr + 1 < TR0[j + 1]:
                        turn(tr + 1)
                    kt = tr - TR0[j]
                    v = vcp[0:n, 64 * g:64 * g + 64] if br == 0 else vn[:, br - 1, kt, 64 * g:64 * g + 64]
                    e.wait_ge(p_trc, tr + 1)
                    if br == 0 and u >= 2:
                        e.wait_ge(po_lo, u - 1)
                    mm(out, v, pTp[0:n, tr % 2, :].rearrange("p (r q) -> p r q", r=GQ), start=(br == 0),
                       stop=(br == 2 and tr + 1 == TR0[j + 1])).then_inc(p_pv, 1)

            p_score(0)
            for j in range(len(JOBS)):
                if j + 1 < len(JOBS):
                    p_score(j + 1)
                if sample_step(j):
                    s_step(*sample_step(j))
                p_values(j)

            e.wait_ge(po_lo, 8)
            e.wait_ge(so_lo, 2)
            for m in range(KD):
                if m >= 4:
                    e.wait_ge(psum_free, O_NSA + m - 3)
                unit(U_NSA + m, m % 4, oh, ol, 0, True, True)
            for m in range(KD):
                e.wait_ge(psum_free, O_OUT + m - 3)
                unit(U_OUT + m, m % 4, mh, ml, 0, True, True, 0, (m_lo, 0) if m == 0 else None)
            norm_sum(2)
            ffn(U_GU2, O_GU2, 1, 2)
            down(U_DN2, O_DN2, 1)
            norm_sum(3)


def _bucket(n):
    n = np.maximum(n, 0)
    nf = np.maximum(n, 1).astype(np.float32)
    large = 16 + (np.log(nf / np.float32(16)) / np.float32(np.log(8.0)) * np.float32(16)).astype(np.int32)
    return np.where(n < 16, n, np.minimum(large, 31))


def _constants():
    cst = np.zeros((P, C_END), np.float32)
    cst[:, C_ID:C_ID + P] = np.eye(P)
    cst[:, C_J:C_J + P] = np.eye(P)[::-1]
    row = np.arange(P)
    key = (row // 32) * 100 + (row % 32 // 16) * 10 + row % 4
    cst[:, C_M:C_M + P] = key[:, None] == key[None, :]
    for hb in range(2):
        b = np.arange(TS) // SQ
        cst[:, C_X + TS * hb:C_X + TS * hb + TS] = np.where(b[None, :] == 4 * hb + row[:, None] // 32, 0.0, NEG)
    cst[:, C_JI:C_JI + NSEL] = np.arange(1, NSEL + 1)
    cst[:, C_VAL] = row >= 31
    cst[:, C_SUM:C_SUM + NMOD] = row[:, None] % 32 == np.arange(NMOD)[None, :]
    oneh = np.zeros((33, LA + LW), np.float32)
    dist = np.concatenate([1027 - np.arange(LA), 515 - np.arange(LW)])
    seen = (dist >= 0) & ((np.arange(LA + LW) < LA) | (dist < WIN))
    oneh[np.where(seen, _bucket(dist), 32), np.arange(LA + LW)] = 1.0
    return cst, oneh


_OUTS = {
    "yT": (KD, P, T), "kvT": (6, P, T), "conv_p": (P, KC, 2), "conv_s": (P, KC, NB, SQ),
    "win_old": (NB, WIN - SQ, 256),
}
_SCRATCH = {"F": (NH, LA + LW), "toep": (P, NH, 512), "gscr": (24, TS)}


def _tiles(w, cols=P):
    k, n = w.shape
    return np.ascontiguousarray(w.reshape(k // P, P, n // cols, cols).transpose(2, 1, 0, 3)).reshape(n // cols, P, -1)


def _layout(x_prompt, x_sample, cache_kv_cmp, cache_kv_sel, state_kv_win, state_conv, page_table, c_prompt, c_sample,
            w_ada, b_ada, g_norm, w_ffn1_gu, w_ffn1_down, w_ffn2_gu, w_ffn2_down, w_in, w_cmp1, w_cmp2, pe_cmp,
            w_conv, w_nsa_out, w_conv_out, w_out, rel_bias, g_final):
    def fm(x):
        return np.ascontiguousarray(x.reshape(x.shape[0], -1, P).transpose(2, 1, 0))

    def gate_value(w):
        t = _tiles(w)
        return np.ascontiguousarray(t.reshape(2, KF, P, -1).transpose(1, 0, 2, 3)).reshape(2 * KF, P, -1)

    cst, oneh = _constants()
    w = w_in[0]
    blocks = [np.concatenate([w[:, 64 * r:64 * r + 64], w[:, 256 + 64 * r:320 + 64 * r]], 1) for r in range(4)]
    blocks += [w[:, OFF_KV + P * j:OFF_KV + P * j + P] for j in range(6)]
    blocks += [w[:, OFF_GN:OFF_GN + P]]
    for ct in range(KC):
        blocks += [w[:, o + P * ct:o + P * ct + P] for o in (OFF_C, OFF_H, OFF_B)]
    blocks += [w[:, OFF_MG + D + P * m:OFF_MG + D + P * m + P] for m in range(KD)]
    blocks += [w[:, OFF_MG + P * m:OFF_MG + P * m + P] for m in range(KD)]
    no = w_nsa_out[0].reshape(2, 4, HD, D).transpose(1, 0, 2, 3).reshape(DC, D)
    cmp_pages = cache_kv_cmp[0].reshape(NPHYS, 8, 8, 2, 2, 2, HD)
    cmp_pages = cmp_pages.transpose(0, 3, 6, 2, 4, 5, 1).reshape(NPHYS, P, 256)
    sel = cache_kv_sel[0].reshape(NPHYS, PAGE, 2, P)
    win = state_kv_win[0].reshape(NB, 4, P, 2, P)
    w1 = w_cmp1[0].reshape(2, 16, P, P).transpose(2, 0, 1, 3)
    vec = np.concatenate([b_ada[0].reshape(72, P), g_norm[0].reshape(24, P), g_final.reshape(8, P),
                          w_conv[0].reshape(12, P), pe_cmp[0].reshape(32, P)]).T
    a = {
        "ptab": page_table.reshape(1, -1),
        "w1": w1, "w2": w_cmp2[0].transpose(1, 0, 2), "vec": vec, "cst": cst, "oneh": oneh,
        "relx": np.concatenate([rel_bias, np.full((1, NH), NEG, np.float32)]),
        "cmp_pages": cmp_pages,
        "sel_pages": np.stack([sel[:, :, 0].transpose(0, 2, 1), sel[:, :, 1]]),
        "win_tiles": np.stack([win[:, :, :, 0].transpose(0, 3, 1, 2), win[:, :, :, 1].transpose(0, 2, 1, 3)]),
        "win_src": state_kv_win[0].reshape(NB, WIN, 256)[:, SQ:],
        "cT": fm(np.concatenate([c_prompt, c_sample])),
        "xT": fm(np.concatenate([x_prompt[0], x_sample.reshape(TS, D)])),
        "convT": state_conv[0].reshape(NB, 2, KC, P).transpose(3, 2, 0, 1),
        "w_ada": _tiles(w_ada[0], 512).reshape(18, P, KD, 512),
        "w_gu1": gate_value(w_ffn1_gu[0]), "w_dn1": _tiles(w_ffn1_down[0]),
        "w_gu2": gate_value(w_ffn2_gu[0]), "w_dn2": _tiles(w_ffn2_down[0]),
        "w_in": np.stack([_tiles(b)[0] for b in blocks]),
        "w_no": _tiles(no), "w_co": _tiles(w_conv_out[0]), "w_out": _tiles(w_out[0]),
    }
    return {k: np.ascontiguousarray(v) for k, v in a.items()}


def _results(r):
    y = r["yT"].transpose(2, 0, 1).reshape(T, D)
    kv = r["kvT"].reshape(3, 2, 2, HD, T).transpose(0, 4, 1, 2, 3)
    kvp = [kv[j, :TP][None, None] for j in range(3)]
    kvs = [kv[j, TP:].reshape(1, NB, SQ, 2, 2, HD) for j in range(3)]
    old = r["win_old"].reshape(1, NB, WIN - SQ, 2, 2, HD)
    win_s = np.concatenate([old, kvs[2]], axis=2)
    conv_p = r["conv_p"].transpose(2, 1, 0).reshape(1, 1, 2, DC)
    conv_s = r["conv_s"].transpose(2, 3, 1, 0).reshape(NB, SQ, DC)[None, :, SQ - 2:]
    out = (y[:TP][None], y[TP:].reshape(NB, SQ, D), kvp[0], kvp[1], kvp[2], conv_p, kvs[0], kvs[1], win_s, conv_s)
    return tuple(np.ascontiguousarray(x) for x in out)


def _program(nc, arrays):
    d = {}
    for name, a in arrays.items():
        d[name] = nc.dram_tensor("in_" + name, a.shape, mybir.dt.from_np(a.dtype), kind="ExternalInput").ap()
    for name, shape in _OUTS.items():
        d[name] = nc.dram_tensor("out_" + name, shape, F32, kind="ExternalOutput").ap()
    for name, shape in _SCRATCH.items():
        d[name] = nc.dram_tensor("scr_" + name, shape, F32, kind="Internal").ap()
    build(nc, d)


def kernel(**inputs):
    import concourse.bacc as _bacc
    from concourse.bass_utils import run_bass_kernel_spmd as _run

    nc = _bacc.Bacc("TRN2", target_bir_lowering=False, num_devices=1,
                     dynamic_dma_scratch_size=1024)
    arrays = _layout(**{k: np.asarray(v) for k, v in inputs.items()})
    _program(nc, arrays)
    r = _run(nc, [{"in_" + k: v for k, v in arrays.items()}], core_ids=[0])
    return _results({k: r.results[0]["out_" + k] for k in _OUTS})
```

```python
from contextlib import ExitStack

import numpy as np

import concourse.bass as bass
from concourse import mybir

F32 = mybir.dt.float32
F32R = mybir.dt.float32r
I32 = mybir.dt.int32
ALU = mybir.AluOpType
ACT = mybir.ActivationFunctionType
AX = mybir.AxisListType

P = 128
D = 1024
KD = D // P
TP, NB, SQ = 512, 8, 4
TS = NB * SQ
T = TP + TS
HT = T // 2
PA = TP - HT
DFF = 2816
KF = DFF // P
HD, NH, GQ = 64, 8, 4
PAST, PAGE = 1024, 128
NPG = PAST // PAGE
NPHYS = 80
WIN = 512
NC = 63
NCP = 31
NSEL = 14
DC = 512
KC = DC // P
NMOD = 9
EPS = 1e-6
NEG = -1e9
LA = 1155
LW = WIN + SQ - 1
SEL_W = PAST + TS
WIN_W = WIN + TS
RAWS, SPLITS = 4, 2
ADAS = 3
NADA = 7
ADA_AFTER = [(0, 1), (2, 3), (4,), (5,)]
ADA_LATE = 4 * NADA
DOWN_K = [(0, 6), (6, 6), (12, 5), (17, 5)]
OFF_Q, OFF_KV, OFF_GN, OFF_H, OFF_B, OFF_C, OFF_MG = 0, 512, 1280, 1304, 1816, 2328, 2840

U_GU1 = 0
U_DN1 = U_GU1 + 2 * KF
U_WIN = U_DN1 + 4 * KD
U_MGB = U_WIN + 23
U_MGA = U_MGB + 2 * KD
U_NSA = U_MGA + KD
U_OUT = U_NSA + KD
U_GU2 = U_OUT + KD
U_DN2 = U_GU2 + 2 * KF
U_END = U_DN2 + 4 * KD
O_GU1 = 3
O_DN1 = O_GU1 + 2 * KF
O_WIN = O_DN1 + KD
O_MGB = O_WIN + 23
O_NSA = O_MGB + 2 * KD
O_OUT = O_NSA + KD
O_GU2 = O_OUT + KD
O_DN2 = O_GU2 + 2 * KF


def unit_k(u):
    for base in (U_DN1, U_DN2):
        if base <= u < base + 4 * KD:
            return DOWN_K[(u - base) % 4][1]
    if U_MGB <= u < U_MGA:
        return 8 if (u - U_MGB) % 2 == 0 else 4
    return 4 if U_NSA <= u < U_OUT else 8


C_ID, C_J, C_M, C_X, C_JI, C_VAL, C_SUM, C_END = 0, 128, 256, 384, 448, 462, 463, 472
V_BADA, V_G, V_GF, V_WC, V_PE, V_END = 0, 72, 96, 104, 116, 148
S_SEL, S_WIN, S_CMP, S_END = 0, SEL_W, SEL_W + WIN_W, SEL_W + WIN_W + NC
S_PARTS = [(S_CMP, S_END), (S_WIN, S_CMP), (S_SEL, S_WIN)]


def build(nc, d):
    with ExitStack() as ctx:
        def sb(stack, name, shape, dt=F32):
            return stack.enter_context(nc.sbuf_tensor(name, shape, dt))

        def sem(name):
            return ctx.enter_context(nc.semaphore(name))

        h = sb(ctx, "h", [P, KD, T])
        mods = sb(ctx, "mods", [P, 72, NMOD])
        sw = ExitStack()
        tmp = sb(sw, "tmp", [P, 2, T])
        sg = sb(sw, "sg", [P, 2, T])
        sw.close()
        sp_2 = sb(ctx, "sp_2", [P, GQ, 512])
        sb(ctx, "unused_w", [P, 4 * T - GQ * 512])
        sq = sb(ctx, "sq", [P, T])
        ssq = sb(ctx, "ssq", [P, T])
        rinv = sb(ctx, "rinv", [P, T])
        smod = sb(ctx, "smod", [P, 4, TS])
        cst = sb(ctx, "cst", [P, C_END])
        ones = sb(ctx, "ones", [P, P])
        vec = sb(ctx, "vec", [P, V_END])
        kcT = sb(ctx, "kcT", [P, NB, NC])
        vc = sb(ctx, "vc", [NC, NB, P])
        peb = sb(ctx, "peb", [P, 2])
        sres = sb(ctx, "sres", [P, TS])
        csil = sb(ctx, "csil", [P, KD, 32])
        ptab = sb(ctx, "ptab", [1, NB * NPG], I32)
        ident = cst[:, C_ID:C_ID + P]

        sr0 = ExitStack()
        raw = sb(sr0, "raw", [P, RAWS, 8, P])

        s0 = ExitStack()
        w1 = sb(s0, "w1", [P, 2, 16, P])
        w2 = sb(s0, "w2", [P, 2, HD])
        ch = sb(s0, "ch", [P, 2, 2 * NPG, 8, 2, 2, 8])
        hid = sb(s0, "hid", [P, 2, 2, NB, 64])
        oneh = sb(s0, "oneh", [33, LA + LW])
        relx = sb(s0, "relx", [33, NH])
        Fsb = sb(s0, "Fsb", [NH, LA + LW])
        hank = sb(s0, "hank", [P, NH, 512])
        toep = sb(s0, "toep", [P, NH, 512])
        ada = sb(s0, "ada", [P, ADAS, KD, 512])
        part = sb(s0, "part", [P, 2, 512])
        cs = sb(s0, "cs", [P, KD, NMOD])
        s0.close()

        sr = ExitStack()
        wh = sb(sr, "wh", [P, SPLITS, 8, P], F32R)
        wl = sb(sr, "wl", [P, SPLITS, 8, P], F32R)
        uh = sb(sr, "uh", [P, KD, T], F32R)
        ul = sb(sr, "ul", [P, KD, T], F32R)
        hh = sb(sr, "hh", [P, KF, T], F32R)
        hl = sb(sr, "hl", [P, KF, T], F32R)
        ada_t = sb(sr, "ada_t", [P, 2, KD, P])
        part_t = sb(sr, "part_t", [P, 2, P])
        sr.close()
        sr0.close()
        sa = ExitStack()
        toep_g = [sb(sa, f"toep_g{g}", [P, GQ, 512]) for g in range(2)]
        bsel = sb(sa, "bsel", [P, PAST])
        bwin = sb(sa, "bwin", [P, WIN])
        bnew0 = sb(sa, "bnew0", [P, SQ])
        bnew = sb(sa, "bnew", [P, 2, NB, SQ])
        ss = sb(sa, "ss", [P, S_END])
        sx = sb(sa, "sx", [P, P])
        st = sb(sa, "st", [P, 20])
        sb(sa, "unused", [P, (RAWS + 2 * SPLITS) * D - 2 * GQ * 512 - PAST - WIN - SQ - 2 * TS - S_END - P - 20])

        sm = ExitStack()
        qT = sb(sm, "qT", [P, GQ, T])
        kT = sb(sm, "kT", [P, 3, T])
        vn = sb(sm, "vn", [P, 2, 5, P])
        mB = sb(sm, "mB", [P, KD, T])
        sgA = sb(sm, "sgA", [P, KD, T])
        gT = sb(sm, "gT", [24, T])
        grev = sb(sm, "grev", [24, NB, SQ])
        gq = sb(sm, "gq", [P, 4, 24])
        gs = sb(sm, "gs", [P, 2, 3])
        kz = sb(sm, "kz", [P, 2, 2, TP])
        kcz = sb(sm, "kcz", [P, 2, NCP])
        vcp = sb(sm, "vcp", [NCP, P])
        sm1 = ExitStack()
        vT = sb(sm1, "vT", [P, 3, T])
        uh2 = sb(sm1, "uh2", [P, KD, T], F32R)
        ul2 = sb(sm1, "ul2", [P, KD, T], F32R)
        fullp = sb(sm1, "fullp", [P, KC, 2 + TP])
        fulls = sb(sm1, "fulls", [P, KC, NB, 2 + SQ])
        yh = sb(sm1, "yh", [P, KC, T], F32R)
        yl = sb(sm1, "yl", [P, KC, T], F32R)
        sm1.close()
        sm4 = ExitStack()
        sb(sm4, "in_use", [P, 3 * T + 2 * KD * T])
        w2p = sb(sm4, "w2p", [P, 2, HD])
        chp = sb(sm4, "chp", [P, 8, 2, 2, 32])
        hidp = sb(sm4, "hidp", [P, 2, 2, 32])
        sb(sm4, "unused_conv", [P, KC * (2 + TP) + KC * NB * (2 + SQ) - 2 * HD - 8 * 128 - 128])
        w1p = sb(sm4, "w1p", [P, 2, 16, P])
        sm4.close()
        sm2 = ExitStack()
        oh = sb(sm2, "oh", [P, GQ, T], F32R)
        ol = sb(sm2, "ol", [P, GQ, T], F32R)
        sm3 = ExitStack()
        kv = sb(sm3, "kv", [P, 4, NPG + 4, P])
        qb = sb(sm3, "qb", [P, 2, 4, NH, SQ])
        pT = sb(sm3, "pT", [P, 15, P])
        sp = [sb(sm3, f"sp_{x}", [P, GQ, 512]) for x in range(2)] + [sp_2]
        pTp = sb(sm3, "pTp", [P, 2, GQ * P])
        stp = sb(sm3, "stp", [P, 3, 6, GQ])
        sm3.close()
        sm5 = ExitStack()
        mh = sb(sm5, "mh", [P, KD, T], F32R)
        ml = sb(sm5, "ml", [P, KD, T], F32R)
        sm5.close()
        sm2.close()
        sm.close()
        sa.close()

        PS = ctx.enter_context(nc.psum_tensor("PS", [P, 8, 512], F32))

        def out2(s):
            return PS[:, 2 * s:2 * s + 2, 0:HT]

        def ada_bank(fi):
            return 4 * (1 - fi % 2) + 2

        def norm_slot(n):
            return 2 if n else 0

        def halves(ap):
            return ap.rearrange("p (a t) -> p a t", a=2)

        def work(k):
            return (tmp, sg)[k // 2 % 2][:, k % 2, :]

        def f(ap):
            return ap.bitcast(F32)

        consts_in = sem("consts_in")
        vec_in = sem("vec_in")
        comp_in = sem("comp_in")
        ptab_in = sem("ptab_in")
        ch_in = [sem(f"ch_in{i}") for i in range(2)]
        bias_in = sem("bias_in")
        bias_out = sem("bias_out")
        hank_in = sem("hank_in")
        toep_out = sem("toep_out")
        x_in = sem("x_in")
        cond_in = sem("cond_in")
        ada_in = [sem(f"ada_in{i}") for i in range(ADAS)]
        ada_t_in = [sem(f"ada_t_in{i}") for i in range(2)]
        ada_used = sem("ada_used")
        f_ready = sem("f_ready")
        f_copied = sem("f_copied")
        flip_ready = sem("flip_ready")
        flip_copied = sem("flip_copied")
        csil_zero = sem("csil_zero")
        csil_ready = sem("csil_ready")
        part_ready = sem("part_ready")
        part_copied = sem("part_copied")
        ada_copied = sem("ada_copied")
        mods_ready = sem("mods_ready")
        pe_ready = sem("pe_ready")
        pe_copied = sem("pe_copied")
        pre_ready = sem("pre_ready")
        hid_ready = sem("hid_ready")
        cmp_ready = sem("cmp_ready")
        raw_in = [sem(f"raw_in{i}") for i in range(RAWS)]
        hi_ready = sem("hi_ready")
        lo_ready = sem("lo_ready")
        unit_used = sem("unit_used")
        psum_free = sem("psum_free")
        silu_ready = sem("silu_ready")
        hid_hi = sem("hid_hi")
        hid_lo = sem("hid_lo")
        h_ready = sem("h_ready")
        sq_ready = sem("sq_ready")
        sq_last = sem("sq_last")
        ssq_ready = sem("ssq_ready")
        ssum_ready = sem("ssum_ready")
        ms_ready = sem("ms_ready")
        root_ready = sem("root_ready")
        rinv_ready = sem("rinv_ready")
        nt_ready = sem("nt_ready")
        nt_mod = sem("nt_mod")
        ns_part = sem("ns_part")
        ns_mod = sem("ns_mod")
        u_hi = sem("u_hi")
        u_lo = sem("u_lo")
        out_done = sem("out_done")
        sig_ready = sem("sig_ready")
        grev_ready = sem("grev_ready")
        conv_in = sem("conv_in")
        conv_set = sem("conv_set")
        y_hi = sem("y_hi")
        y_lo = sem("y_lo")
        sgb_ready = sem("sgb_ready")
        sga_ready = sem("sga_ready")
        dchain = sem("dchain")
        gate_out = sem("gate_out")
        gate_in = sem("gate_in")
        compp_in = sem("compp_in")
        gv_ready = sem("gv_ready")
        gv_copied = sem("gv_copied")
        chp_ready = sem("chp_ready")
        prep_ready = sem("prep_ready")
        hidp_ready = sem("hidp_ready")
        cmpp_ready = sem("cmpp_ready")
        cmpp_copied = sem("cmpp_copied")
        att_bias_in = sem("att_bias_in")
        toepg_in = sem("toepg_in")
        kz_zero = sem("kz_zero")
        kz_ready = sem("kz_ready")
        kv_in = [sem(f"kv_in{i}") for i in range(3)]
        v_used = sem("v_used")
        qb_ready = sem("qb_ready")
        s_work = sem("s_work")
        s_free = sem("s_free")
        s_exp = sem("s_exp")
        s_prob = sem("s_prob")
        s_sum = sem("s_sum")
        s_out = sem("s_out")
        s_max = sem("s_max")
        so_hi = sem("so_hi")
        so_lo = sem("so_lo")
        p_scores = sem("p_scores")
        p_evac = sem("p_evac")
        p_max = sem("p_max")
        p_exp = sem("p_exp")
        p_prob = sem("p_prob")
        p_tr = sem("p_tr")
        p_trc = sem("p_trc")
        p_pv = sem("p_pv")
        po_hi = sem("po_hi")
        po_lo = sem("po_lo")
        m_ready = sem("m_ready")
        m_hi = sem("m_hi")
        m_lo = sem("m_lo")
        y_out_ready = sem("y_out_ready")
        y_out_sent = [sem(f"y_out_sent{i}") for i in range(4)]
        win_sent = sem("win_sent")

        block = ctx.enter_context(nc.Block())

        def sample_o(o, g, hb, q):
            t0 = TP + 16 * hb
            return o[64 * g:64 * g + 64, :, t0:t0 + 16].rearrange("p r (b q) -> p q r b", q=SQ)[:, q]

        def sample_psum(g, hb, q):
            src = PS[64 * g:64 * g + 64, S_BANK, 0:P].rearrange("p (b h q) -> p q h b", b=4, h=NH)
            return src[:, SQ - 1 - q, 4 * g:4 * g + 4]

        def prompt_psum(g):
            return PS[64 * g:64 * g + 64, 6, :].rearrange("p (r q) -> p r q", r=GQ)

        KV_IN = [16 * 4, 16 * 16, 16 * 16]
        S_BANK, S_ITEMS, S_STEPS, S_FIRST = 7, 9, 10, 2

        def sample_step(j):
            n = j - S_FIRST
            return divmod(n, S_STEPS) if 0 <= n < 2 * S_STEPS else None

        JOBS = [(g, (3 - n, n)[g], br) for n in range(4) for br in range(3) for g in range(2)]

        def outputs(j):
            return sum(br == 2 for _, _, br in JOBS[:j + 1])

        TR0 = [0]
        for _, i_, br_ in JOBS:
            TR0.append(TR0[-1] + (1 if br_ == 0 else i_ + 1))

        def nkeys(i, br):
            return 8 * i + 7 if br == 0 else P * (i + 1)

        def toep_cols(i, br):
            c = 384 - P * i
            return slice(c + 31, c + 32 + 16 * (8 * i + 6), 16) if br == 0 else slice(c, 512)

        @block.sync
        def _(sp_):
            e = sp_
            page_regs = [e.alloc_register(f"page{j}") for j in range(NPG)]
            e.dma_start(ptab[:, :], d["ptab"]).then_inc(ptab_in, 16)
            e.dma_start(w1[:, :, :, :], d["w1"]).then_inc(comp_in, 16)
            e.dma_start(w2[:, :, :], d["w2"]).then_inc(comp_in, 16)
            e.dma_start(vec[:, :], d["vec"]).then_inc(vec_in, 16)
            e.wait_ge(ptab_in, 16)

            def pages(t):
                if t >= 2:
                    e.wait_ge(pre_ready, 2 * (t - 1))
                for j0 in range(0, 2 * NPG, NPG):
                    e.load(page_regs, ptab[0:1, 16 * t + j0:16 * t + j0 + NPG])
                    for j in range(NPG):
                        r = e.snap(page_regs[j], min_val=0, max_val=NPHYS - 1)
                        e.dma_start(ch[:, t % 2, j0 + j].rearrange("p a b c n -> p (a b c n)"),
                                    d["cmp_pages"][bass.ds(r, 1)].rearrange("o p n -> (o p) n")
                                    ).then_inc(ch_in[t % 2], 16)

            def ada_load(l):
                if l >= ADAS:
                    e.wait_ge(part_ready, l - ADAS + 1)
                e.dma_start(ada[:, l % ADAS], d["w_ada"][l]).then_inc(ada_in[l % ADAS], 16)

            pages(0)
            e.dma_start(cs[:, :, :], d["cT"]).then_inc(cond_in, 16)
            e.dma_start(cst[:, :], d["cst"]).then_inc(consts_in, 16)
            e.dma_start(oneh[:, :], d["oneh"]).then_inc(bias_in, 16)
            e.dma_start(relx[:, :], d["relx"]).then_inc(bias_in, 16)
            ada_load(0)
            pages(1)
            ada_load(1)
            ada_load(2)
            e.wait_ge(f_copied, 4)
            e.dma_start(d["F"], Fsb[:, :]).then_inc(bias_out, 16)
            e.wait_ge(bias_out, 16)
            for hd in range(NH):
                e.dma_start(hank[:, hd, :], bass.AP(tensor=d["F"].tensor, offset=hd * (LA + LW) + 516,
                                                    ap=[[1, P], [1, 512]])).then_inc(hank_in, 16)
            e.dma_start(h[:, :, :], d["xT"]).then_inc(x_in, 16)
            pages(2)
            ada_load(3)
            pages(3)
            ada_load(4)
            ada_load(5)
            e.wait_ge(flip_copied, NH)
            e.dma_start(d["toep"], toep[:, :, :]).then_inc(toep_out, 16)
            for u in range(RAWS):
                e.dma_start(raw[:, u, :, :].rearrange("p k m -> p (k m)"), d["w_gu1"][u]).then_inc(raw_in[u], 16)
            ada_load(6)
            e.dma_start(d["win_old"], d["win_src"]).then_inc(win_sent, 16)

            def load(u, src, more=0):
                s = u % RAWS
                n = src.shape[-1] // P
                if u >= RAWS:
                    e.wait_ge(lo_ready, u - RAWS + 1 + more)
                e.dma_start(raw[:, s, 0:n, :].rearrange("p k m -> p (k m)"), src).then_inc(raw_in[s], 16)

            def row(ap, i):
                return ap[bass.ds(i, 1)].rearrange("o p n -> (o p) n")

            def ada_tile(n, i=0):
                e.wait_ge(part_ready, NADA + n - 1 + 4 * i)
                e.dma_start(ada_t[:, n % 2, :, :].rearrange("p k m -> p (k m)"), row(d["w_ada_t"], 4 * i + n)
                            ).then_inc(ada_t_in[n % 2], 16)

            def ffn_loads(w_gu, w_dn, ug, ud):
                first = ug == 0
                if not first:
                    for u in range(4):
                        load(ug + u, w_gu[u])
                with e.Fori(0, KF // 2 - 1) as i:
                    for j in range(4):
                        load(ug + 4 + j, row(w_gu, 4 * i + 4 + j), 4 * i)
                        if first:
                            ada_tile(j, i)
                for j, (k0, n) in enumerate(DOWN_K):
                    load(ud + j, w_dn[0][:, k0 * P:(k0 + n) * P])
                    if first:
                        ada_tile(2 * KF - 4 + j)
                with e.Fori(1, KD) as m:
                    for j, (k0, n) in enumerate(DOWN_K):
                        load(ud + j, row(w_dn, m)[:, k0 * P:(k0 + n) * P], 4 * m)

            e.wait_ge(ada_used, NADA)
            ffn_loads(d["w_gu1"], d["w_dn1"], U_GU1, U_DN1)
            for u in range(23):
                load(U_WIN + u, d["w_in"][u])
                if u == 4:
                    e.wait_ge(unit_used, U_WIN)
                    for ct in range(KC):
                        e.dma_start(fulls[:, ct, :, 0:2], d["convT"][:, ct]).then_inc(conv_in, 16)
            for m in range(KD):
                load(U_MGB + 2 * m, d["w_in"][23 + m])
                load(U_MGB + 2 * m + 1, d["w_co"][m])
            e.wait_ge(psum_free, O_WIN + 10)
            for j in range(3):
                e.dma_start(d["kvT"][2 * j], kT[:, j, :]).then_inc(out_done, 16)
                e.dma_start(d["kvT"][2 * j + 1], vT[:, j, :]).then_inc(out_done, 16)
            e.wait_ge(psum_free, O_MGB)
            e.dma_start(d["conv_p"], fullp[:, :, TP:TP + 2]).then_inc(out_done, 16)
            e.dma_start(d["conv_s"], fulls[:, :, :, 2:2 + SQ]).then_inc(out_done, 16)
            for m in range(KD):
                load(U_MGA + m, d["w_in"][31 + m])
                if m == 5:
                    e.wait_ge(unit_used, U_MGA)
                    e.dma_start(w1p[:, :, :, :], d["w1"]).then_inc(compp_in, 16)
                    e.wait_ge(out_done, 8 * 16)
                    e.dma_start(w2p[:, :, :], d["w2"]).then_inc(compp_in, 16)
            e.wait_ge(lo_ready, U_MGA + KD)
            for g in range(2):
                e.dma_start(toep_g[g][:, :, :], d["toep"][:, GQ * g:GQ * g + GQ, :]).then_inc(toepg_in, 16)
            e.wait_ge(grev_ready, 1)
            e.dma_start(d["gscr"], grev[:, :, :].rearrange("p b q -> p (b q)")).then_inc(gate_out, 16)
            e.wait_ge(unit_used, U_MGA + KD)
            for b in range(4):
                r0 = 32 * b
                fd = d["F"].tensor
                L = LA + LW
                e.dma_start(bsel[r0:r0 + 32, :], bass.AP(tensor=fd, offset=0, ap=[[L, NH], [1, SQ], [1, PAST]])
                            ).then_inc(att_bias_in, 16)
                e.dma_start(bwin[r0:r0 + 32, :], bass.AP(tensor=fd, offset=LA, ap=[[L, NH], [1, SQ], [1, WIN]])
                            ).then_inc(att_bias_in, 16)
                e.dma_start(bnew0[r0:r0 + 32, :], bass.AP(tensor=fd, offset=PAST, ap=[[L, NH], [1, SQ], [1, SQ]])
                            ).then_inc(att_bias_in, 16)

            def cached(hb, v):
                for b in range(4):
                    e.dma_start(kv[:, b, NPG:NPG + 4, :], d["win_tiles"][v, 4 * hb + b]).then_inc(kv_in[0], 16)
                for part in range(2):
                    for b in range(4):
                        j0 = (4 * hb + b) * NPG + 4 * part
                        e.load(page_regs[0:4], ptab[0:1, j0:j0 + 4])
                        for j in range(4):
                            r = e.snap(page_regs[j], min_val=0, max_val=NPHYS - 1)
                            e.dma_start(kv[:, b, 4 * part + j, :],
                                        d["sel_pages"][v][bass.ds(r, 1)].rearrange("o p n -> (o p) n")
                                        ).then_inc(kv_in[1 + part], 16)

            e.wait_ge(cmpp_copied, 2)
            cached(0, 0)
            e.wait_ge(gate_out, 16)
            for hb in range(2):
                for b in range(4):
                    for br in range(3):
                        e.dma_start(gs[32 * b:32 * b + 32, hb, br:br + 1],
                                    bass.AP(tensor=d["gscr"].tensor, offset=br * NH * TS + SQ * (4 * hb + b),
                                            ap=[[TS, NH], [1, SQ], [1, 1]])).then_inc(gate_in, 16)
            e.wait_ge(s_work, 4)
            cached(0, 1)
            e.wait_ge(v_used, 1)
            cached(1, 0)
            e.wait_ge(s_work, S_ITEMS + 4)
            cached(1, 1)
            e.wait_ge(p_evac, GQ * len(JOBS))
            e.wait_ge(so_hi, 2)
            for m in range(KD):
                load(U_NSA + m, d["w_no"][m])
            for m in range(KD):
                load(U_OUT + m, d["w_out"][m])
            ffn_loads(d["w_gu2"], d["w_dn2"], U_GU2, U_DN2)
            for k in range(KD):
                e.wait_ge(y_out_ready, k + 1)
                e.dma_start(d["yT"][k], work(k)).then_inc(y_out_sent[k % 4], 16)
            for s in y_out_sent:
                e.wait_ge(s, 16 * KD // 4)
            e.wait_ge(win_sent, 16)
            e.wait_ge(gate_in, 24 * 16)
            e.wait_ge(toep_out, 16)

        @block.gpsimd
        def _(e):
            e.memset(csil[:, :, :], 0.0).then_inc(csil_zero, 1)
            e.memset(ones[:, :], 1.0)

            def sum_squares(n):
                e.memset(ssq[:, :], 0.0).then_inc(ssq_ready, 1)
                if n == 0:
                    e.wait_ge(x_in, 16)
                with e.Fori(0, KD - 1) as k:
                    if n:
                        e.wait_ge(h_ready, 8 * (n - 1) + 1 + k)
                    e.wait_ge(ssq_ready, 8 * n + 1 + k)
                    e.tensor_tensor(sq[:, :], h[:, bass.ds(k, 1), :].rearrange("p o t -> p (o t)"),
                                    h[:, bass.ds(k, 1), :].rearrange("p o t -> p (o t)"), ALU.mult).then_inc(sq_ready, 1)
                    e.wait_ge(sq_ready, 7 * n + 1 + k)
                    e.tensor_tensor(ssq[:, :], ssq[:, :], sq[:, :], ALU.add).then_inc(ssq_ready, 1)

            def modulate_samples(n):
                for k in range(KD):
                    c = 8 * n + k
                    t3 = work(k)[:, TP:T].rearrange("p (b q) -> p b q", b=NB)
                    s3 = smod[:, k % 4, :].rearrange("p (b q) -> p b q", b=NB)
                    gain = mods[:, 24 * n + 8 + k, 1:NMOD].unsqueeze(2).broadcast_to([P, NB, SQ])
                    shift = mods[:, 24 * n + k, 1:NMOD].unsqueeze(2).broadcast_to([P, NB, SQ])
                    e.wait_ge(nt_ready, c + 1)
                    e.tensor_tensor(s3, t3, gain, ALU.mult).then_inc(ns_part, 1)
                    e.wait_ge(ns_part, c + 1)
                    e.tensor_tensor(t3, s3, shift, ALU.add).then_inc(ns_mod, 1)

            for n in range(4):
                if n == 2:
                    for m in range(KD):
                        e.wait_ge(psum_free, O_NSA + m + 1)
                        e.tensor_tensor(work(m), work(m), mB[:, m, :], ALU.add).then_inc(m_ready, 1)
                if n > 0:
                    e.wait_ge(ssum_ready, n)
                sum_squares(n)
                if n < 2:
                    e.wait_ge(mods_ready, n + 1)
                if n < 3:
                    modulate_samples(n)
                if n == 1:
                    e.memset(kcz[:, :, :], 0.0).then_inc(kz_zero, 1)
                    e.memset(kz[:, :, :, :], 0.0).then_inc(kz_zero, 1)
                    e.wait_ge(kz_zero, 2)
                    for br in range(2):
                        e.wait_ge(psum_free, O_WIN + 7 + 2 * br)
                        for g in range(2):
                            e.tensor_copy(kz[64 * g:64 * g + 64, g, br, :], kT[64 * g:64 * g + 64, 1 + br, 0:TP]
                                          ).then_inc(kz_ready, 1)
                            e.wait_ge(kz_ready, 2 * br + g + 1)

        @block.scalar
        def _(e):
            e.wait_ge(cond_in, 16)
            e.wait_ge(csil_zero, 1)
            e.activation(csil[:, :, 0:NMOD], cs[:, :, :], ACT.Silu).then_inc(csil_ready, 1)

            def copy_part(l, more=0):
                e.wait_ge(part_ready, l + 1 + more)
                if l >= 2:
                    e.wait_ge(ada_used, l - 1 + more)
                e.activation(part[:, l % 2, :], PS[:, 6 + l % 2, :], ACT.Copy).then_inc(part_copied, 1)

            e.wait_ge(pe_copied, 1)
            for t in range(4):
                for c in range(2):
                    e.wait_ge(pre_ready, 2 * t + c + 1)
                    pre = PS[:, 2 * (t % 2) + c, 1:257].rearrange("p (g b n) -> p g b n", g=2, b=2)
                    for g in range(2):
                        ins = e.activation(hid[:, c, g, 2 * t:2 * t + 2, 0:NC], pre[:, g, :, 0:NC],
                                           ACT.Gelu_apprx_tanh, bias=peb[:, c:c + 1])
                    ins.then_inc(hid_ready, 1)
                for l in ADA_AFTER[t]:
                    copy_part(l)

            def split(u, more=0, nk=None):
                n = nk or unit_k(u)
                e.wait_ge(raw_in[u % RAWS], 16 * (u // RAWS + 1) + 4 * more)
                if u >= SPLITS:
                    e.wait_ge(unit_used, u - SPLITS + 1 + more)
                e.activation(wh[:, u % SPLITS, 0:n, :], raw[:, u % RAWS, 0:n, :], ACT.Copy).then_inc(hi_ready, 1)

            def square(n):
                if n:
                    e.wait_ge(h_ready, 8 * n)
                else:
                    e.wait_ge(x_in, 16)
                e.activation(rinv[:, :], h[:, KD - 1, :], ACT.Square).then_inc(sq_last, 1)

            def root(n):
                e.wait_ge(ms_ready, n + 1)
                e.activation(rinv[:, :], rinv[:, :], ACT.Sqrt).then_inc(root_ready, 1)

            def norm(n, hi):
                if n:
                    square(n)
                root(n)
                if n == 1:
                    e.wait_ge(mods_ready, 2)

                def rounded(k):
                    e.wait_ge(nt_mod, 8 * n + k + 1)
                    e.wait_ge(ns_mod, 8 * n + k + 1)
                    e.activation(hi[:, k, :], work(k), ACT.Copy).then_inc(u_hi, 1)

                for k in range(KD):
                    e.wait_ge(nt_ready, 8 * n + k + 1)
                    e.activation(work(k)[:, 0:TP], work(k)[:, 0:TP], ACT.Identity,
                                 scale=mods[:, 24 * n + 8 + k, 0:1], bias=mods[:, 24 * n + k, 0:1]).then_inc(nt_mod, 1)
                    if k:
                        rounded(k - 1)
                rounded(KD - 1)

            def ffn(ug, ud, og):
                def tile(fi, i=0, nk=None):
                    split(ug + 2 * fi + 2, 4 * i, nk)
                    e.wait_ge(unit_used, ug + 2 * fi + 1 + 4 * i)
                    e.activation(halves(sg[:, fi % 2, :]), out2(2 * (fi % 2)), ACT.Silu).then_inc(silu_ready, 1)
                    split(ug + 2 * fi + 3, 4 * i, nk)
                    e.wait_ge(psum_free, og + 2 * fi + 2 + 4 * i)
                    dst = hh[:, fi, :] if isinstance(i, int) else \
                        hh[:, bass.ds(2 * i + fi, 1), :].rearrange("p o t -> p (o t)")
                    e.activation(dst, tmp[:, fi % 2, :], ACT.Copy).then_inc(hid_hi, 1)

                with e.Fori(0, KF // 2 - 1) as i:
                    tile(0, i)
                    tile(1, i)
                tile(KF - 2)
                tile(KF - 1)

            def down(ud):
                with e.Fori(0, KD - 1) as m:
                    for j in range(4):
                        split(ud + j + 2, 4 * m)
                for u in range(ud + 4 * KD - 2, ud + 4 * KD + 2):
                    if u < U_END:
                        split(u)

            split(0)
            split(1)
            square(0)
            copy_part(NADA - 1)
            e.wait_ge(mods_ready, 1)
            norm(0, uh)
            ffn(U_GU1, U_DN1, O_GU1)
            down(U_DN1)
            norm(1, uh2)
            for n in range(23):
                split(U_WIN + n + 2)
                if n == 11:
                    e.wait_ge(psum_free, O_WIN + 11)
                    e.activation(gT[:, :], gT[:, :], ACT.Sigmoid).then_inc(sig_ready, 1)
                    e.wait_ge(sig_ready, 1)
                    for q in range(SQ):
                        ins = e.activation(grev[:, :, SQ - 1 - q],
                                           gT[:, TP:T].rearrange("p (b q) -> p b q", b=NB)[:, :, q], ACT.Copy)
                    ins.then_inc(grev_ready, 1)
                if n >= 13 and (n - 13) % 3 == 0:
                    e.wait_ge(psum_free, O_WIN + n + 1)
                    e.activation(yh[:, (n - 13) // 3, :], tmp[:, 1, :], ACT.Copy).then_inc(y_hi, 1)
            for m in range(KD):
                split(U_MGB + 2 * m + 2)
                e.wait_ge(unit_used, U_MGB + 2 * m + 1)
                if m == 0:
                    e.wait_ge(psum_free, O_MGB)
                e.activation(halves(sg[:, m % 2, :]), out2(2 * (m % 2)), ACT.Sigmoid).then_inc(sgb_ready, 1)
                split(U_MGB + 2 * m + 3)
            for m in range(KD):
                if m + 2 < KD:
                    split(U_MGA + m + 2)
                e.wait_ge(unit_used, U_MGA + m + 1)
                e.activation(halves(sgA[:, m, :]), out2(m % 2), ACT.Sigmoid).then_inc(sga_ready, 1)

            for c in range(2):
                e.wait_ge(prep_ready, c + 1)
                e.activation(hidp[:, c, :, 0:NCP],
                             PS[:, 4 + c, 1:65].rearrange("p (g n) -> p g n", g=2)[:, :, 0:NCP],
                             ACT.Gelu_apprx_tanh, bias=peb[:, c:c + 1]).then_inc(hidp_ready, 1)

            def s_turned(hb, k):
                if (k, hb) == (6, 1):
                    e.wait_ge(v_used, 1)
                for q in (2 * (k - 6), 2 * (k - 6) + 1):
                    e.wait_ge(s_work, S_ITEMS * hb + 5 + q + 1)
                    bank = PS[:, S_BANK, :].rearrange("p (a r) -> p a r", a=4)
                    if q < 3:
                        e.activation(pT[:, 4 * q:4 * q + 4, :], bank, ACT.Copy).then_inc(s_free, 1)
                    else:
                        e.activation(pT[0:TS, 12:14, :], bank[0:TS, 0:2, :], ACT.Copy)
                        e.activation(pT[0:NC, 14, :], bank[0:NC, 2, :], ACT.Copy).then_inc(s_free, 1)

            def s_exps(hb, j):
                a, b = S_PARTS[j]
                e.wait_ge(s_max, 3 * hb + j + 1)
                e.activation(ss[:, a:b], ss[:, a:b], ACT.Exp, bias=st[:, 3 + j:4 + j],
                             accum_out=st[:, 6 + j:7 + j]).then_inc(s_exp, 1)

            def s_output(hb):
                e.wait_ge(s_out, hb + 1)
                for g in range(2):
                    for q in range(SQ):
                        ins = e.activation(sample_o(oh, g, hb, q), sample_psum(g, hb, q), ACT.Copy)
                ins.then_inc(so_hi, 1)

            def p_exp_head(j, r):
                g, i, br = JOBS[j]
                n = nkeys(i, br)
                e.wait_ge(p_max, j + 1)
                e.activation(sp[j % 3][:, r, 0:n], sp[j % 3][:, r, 0:n], ACT.Exp, bias=stp[:, j % 3, 0, r:r + 1],
                             accum_out=stp[:, j % 3, 1, r:r + 1]).then_inc(p_exp, 1)

            def p_output(j):
                g, i, _ = JOBS[j]
                e.wait_ge(p_pv, TR0[j + 1])
                e.activation(oh[64 * g:64 * g + 64, :, P * i:P * i + P], prompt_psum(g), ACT.Copy).then_inc(po_hi, 1)

            e.wait_ge(out_done, 8 * 16)
            for r in range(GQ):
                p_exp_head(0, r)
            for j, (g, i, br) in enumerate(JOBS):
                hb, k = sample_step(j) or (0, -1)
                if k in (6, 7):
                    s_turned(hb, k)
                if k == 9:
                    e.wait_ge(v_used, hb + 1)
                    e.activation(sx[:, :], PS[:, S_BANK, 0:P], ACT.Copy).then_inc(s_sum, 1)
                single = TR0[j + 1] - TR0[j] == 1
                if single and j + 1 < len(JOBS):
                    for r in range(GQ):
                        p_exp_head(j + 1, r)
                for r in range(GQ):
                    tr = TR0[j] + r
                    if tr < TR0[j + 1]:
                        n = nkeys(i, br) if br == 0 else P
                        e.wait_ge(p_tr, tr + 1)
                        if tr >= 2:
                            e.wait_ge(p_pv, tr - 1)
                        e.activation(pTp[0:n, tr % 2, :], PS[0:n, 4 + tr % 2, :], ACT.Copy).then_inc(p_trc, 1)
                    if not single and j + 1 < len(JOBS) and r < 2:
                        p_exp_head(j + 1, 2 * r)
                        p_exp_head(j + 1, 2 * r + 1)
                    if r == 0 and j and JOBS[j - 1][2] == 2:
                        p_output(j - 1)
                if k in (0, 1, 4):
                    s_exps(hb, {0: 0, 1: 1, 4: 2}[k])
                if k == 9:
                    s_output(hb)
            split(U_NSA)
            split(U_NSA + 1)
            p_output(len(JOBS) - 1)

            for m in range(KD + 1):
                if m < KD:
                    split(U_NSA + m + 2)
                if m:
                    e.wait_ge(m_ready, m)
                    e.activation(mh[:, m - 1, :], work(m - 1), ACT.Copy).then_inc(m_hi, 1)
            for u in range(U_OUT + 2, U_OUT + KD + 2):
                split(u)
            norm(2, uh)
            ffn(U_GU2, U_DN2, O_GU2)
            down(U_DN2)
            square(3)
            root(3)

        @block.vector
        def _(e):
            chained = [0]

            def chain(ins):
                chained[0] += 1
                ins.then_inc(dchain, 1)
                e.wait_ge(dchain, chained[0])

            e.wait_ge(pe_ready, 1)
            e.tensor_copy(peb[:, :], PS[:, 7, 0:2]).then_inc(pe_copied, 1)
            for c in range(4):
                a, b = 512 * c, min(512 * c + 512, LA + LW)
                e.wait_ge(f_ready, c + 1)
                e.tensor_copy(Fsb[:, a:b], PS[0:NH, 4 + c % 2, 0:b - a]).then_inc(f_copied, 1)

            def add_bias(l):
                e.wait_ge(ada_used, l + 1)
                e.tensor_tensor(mods[:, 4 * l:4 * l + 4, :],
                                PS[:, 5, 0:4 * NMOD].rearrange("p (m c) -> p m c", m=4),
                                vec[:, V_BADA + 4 * l:V_BADA + 4 * l + 4].unsqueeze(2).broadcast_to([P, 4, NMOD]),
                                ALU.add).then_inc(ada_copied, 1)

            def gains(subs):
                for n in subs:
                    gain = mods[:, 24 * n + 8:24 * n + 16, :]
                    ins = e.scalar_tensor_tensor(
                        out=gain, in0=gain, scalar=1.0,
                        in1=vec[:, V_G + 8 * n:V_G + 8 * n + 8].unsqueeze(2).broadcast_to([P, KD, NMOD]),
                        op0=ALU.add, op1=ALU.mult)
                    if n != 1:
                        gate = mods[:, 24 * n + 16:24 * n + 24, :]
                        ins = e.tensor_scalar(gate, gate, 0.5, None, ALU.mult)
                ins.then_inc(mods_ready, 1)

            e.wait_ge(vec_in, 16)
            for l in range(NADA - 2):
                if l == ADA_AFTER[1][-1]:
                    for hd in range(NH):
                        e.wait_ge(flip_ready, hd + 1)
                        e.tensor_copy(toep[:, hd, :], PS[:, 4 + hd % 2, :]).then_inc(flip_copied, 1)
                add_bias(l)
            e.wait_ge(cmp_ready, 1)
            e.tensor_copy(kcT[:, :, :], PS[:, 0, 0:NB * NC].rearrange("p (b n) -> p b n", b=NB))
            e.tensor_copy(vc[:, :, :], PS[0:NC, 1:3, :].rearrange("p a (b f) -> p (a b) f", b=4)
                          ).then_inc(psum_free, O_GU1)

            def lo(u, more=0, nk=None):
                n = nk or unit_k(u)
                e.wait_ge(hi_ready, u + 1 + more)
                e.tensor_tensor(wl[:, u % SPLITS, 0:n, :], raw[:, u % RAWS, 0:n, :], f(wh[:, u % SPLITS, 0:n, :]),
                                ALU.subtract).then_inc(lo_ready, 1)

            def inv_root(n):
                e.wait_ge(ssum_ready, n + 1)
                e.tensor_scalar(halves(rinv[:, :]), out2(norm_slot(n)), 1.0 / D, EPS, ALU.mult, ALU.add).then_inc(ms_ready, 1)
                e.wait_ge(root_ready, n + 1)
                e.reciprocal(rinv[:, :], rinv[:, :]).then_inc(rinv_ready, 1)
                e.wait_ge(rinv_ready, n + 1)

            def norm(n, hi, low):
                inv_root(n)

                def scaled(k):
                    e.tensor_tensor(work(k), h[:, k, :], rinv[:, :], ALU.mult).then_inc(nt_ready, 1)

                for k in range(3):
                    scaled(k)
                for k in range(KD):
                    if k + 3 < KD:
                        if k:
                            e.wait_ge(u_lo, 8 * n + k)
                        scaled(k + 3)
                    e.wait_ge(u_hi, 8 * n + k + 1)
                    e.tensor_tensor(low[:, k, :], work(k), f(hi[:, k, :]), ALU.subtract).then_inc(u_lo, 1)
                e.wait_ge(u_lo, 8 * n + KD)

            def residual(m, more, gate, slot, of, n):
                at = slice(m, m + 1) if isinstance(more, int) else bass.ds(more + m, 1)
                gat = slice(gate + m, gate + m + 1) if isinstance(more, int) else bass.ds(more + m + gate, 1)
                ht = h[:, at, :].rearrange("p o t -> p (o t)")
                gm = mods[:, gat, :].rearrange("p o c -> p (o c)")
                o = out2(slot)
                e.scalar_tensor_tensor(out=ht[:, 0:HT], in0=o[:, 0, :], scalar=gm[:, 0:1], in1=ht[:, 0:HT],
                                       op0=ALU.mult, op1=ALU.add)
                e.scalar_tensor_tensor(out=ht[:, HT:TP], in0=o[:, 1, 0:PA], scalar=gm[:, 0:1], in1=ht[:, HT:TP],
                                       op0=ALU.mult, op1=ALU.add)
                e.tensor_tensor(sres[:, :].rearrange("p (b q) -> p b q", b=NB),
                                o[:, 1, PA:HT].rearrange("p (b q) -> p b q", b=NB),
                                gm[:, 1:NMOD].unsqueeze(2).broadcast_to([P, NB, SQ]), ALU.mult).then_inc(psum_free, 1)
                e.wait_ge(psum_free, of + m + 1 + more)
                e.tensor_tensor(ht[:, TP:T], ht[:, TP:T], sres[:, :], ALU.add).then_inc(h_ready, 1)
                e.wait_ge(h_ready, n + m + 1 + more)

            def at(base, i, step):
                return slice(base, base + 1) if isinstance(i, int) else bass.ds(step * i + base, 1)

            def late_part(n, fi, i=0):
                e.wait_ge(part_ready, NADA + n + 1 + 4 * i)
                e.wait_ge(ada_used, NADA + n - 1 + 4 * i)
                e.tensor_copy(part_t[:, n % 2, :], PS[:, ada_bank(fi), 0:P]).then_inc(part_copied, 1)

            def late_bias(n, fi, i=0):
                e.wait_ge(ada_used, NADA + n + 1 + 4 * i)
                e.tensor_scalar(mods[:, at(ADA_LATE + n, i, 4), :].rearrange("p o c -> p (o c)"),
                                PS[:, ada_bank(fi) + 1, 0:NMOD], vec[:, at(V_BADA + ADA_LATE + n, i, 4)], None,
                                ALU.add).then_inc(ada_copied, 1)

            def ffn(ug, og, n):
                first = ug == 0

                def tile(fi, i=0):
                    lo(ug + 2 * fi + 2, 4 * i)
                    if first:
                        late_part(2 * fi, fi, i)
                        if fi:
                            late_bias(2 * fi - 1, fi, i)
                    e.wait_ge(silu_ready, KF * n + fi + 1 + 2 * i)
                    e.wait_ge(unit_used, ug + 2 * fi + 2 + 4 * i)
                    e.tensor_tensor(halves(tmp[:, fi % 2, :]), halves(sg[:, fi % 2, :]), out2(2 * (fi % 2) + 1),
                                    ALU.mult).then_inc(psum_free, 2)
                    lo(ug + 2 * fi + 3, 4 * i)
                    if first:
                        late_part(2 * fi + 1, fi, i)
                        late_bias(2 * fi, fi, i)
                    e.wait_ge(hid_hi, KF * n + fi + 1 + 2 * i)
                    a = at(fi, i, 2)
                    e.tensor_tensor(hl[:, a, :].rearrange("p o t -> p (o t)"), tmp[:, fi % 2, :],
                                    f(hh[:, a, :].rearrange("p o t -> p (o t)")), ALU.subtract).then_inc(hid_lo, 1)
                    e.wait_ge(hid_lo, KF * n + fi + 1 + 2 * i)

                tile(0)
                with e.Fori(0, KF // 2 - 1) as i:
                    tile(1, i)
                    tile(2, i)
                tile(KF - 1)
                if first:
                    late_bias(2 * KF - 1, KF - 1)
                    e.wait_ge(ada_copied, NADA + 2 * KF)
                    gains((1, 2))

            def down(ud, od, gate, n):
                with e.Fori(0, KD // 2 - 1) as i:
                    for m in range(2):
                        for j in range(4):
                            lo(ud + 4 * m + j + 2, 8 * i)
                        e.wait_ge(unit_used, ud + 4 * m + 4 + 8 * i)
                        residual(m, 2 * i, gate, m, od, n)
                for m in range(KD - 2, KD):
                    for j in range(4):
                        if ud + 4 * m + j + 2 < U_END:
                            lo(ud + 4 * m + j + 2)
                    e.wait_ge(unit_used, ud + 4 * m + 4)
                    residual(m, 0, gate, m % 2, od, n)

            lo(0)
            lo(1)
            add_bias(NADA - 2)
            e.wait_ge(ada_copied, NADA - 1)
            gains((0,))
            norm(0, uh, ul)
            add_bias(NADA - 1)
            ffn(U_GU1, O_GU1, 0)
            down(U_DN1, O_DN1, 16, 0)
            norm(1, uh2, ul2)
            e.memset(fullp[:, :, 0:2], 0.0).then_inc(conv_set, 1)
            for n in range(23):
                lo(U_WIN + n + 2)
                e.wait_ge(unit_used, U_WIN + n + 1)
                o = out2(n % 4)
                if n < 4:
                    e.tensor_scalar(halves(qT[:, n, :]), o, HD ** -0.5, None, ALU.mult).then_inc(psum_free, 1)
                elif n < 10:
                    dst = (kT if n % 2 == 0 else vT)[:, (n - 4) // 2, :]
                    e.tensor_copy(halves(dst), o).then_inc(psum_free, 1)
                elif n == 10:
                    e.tensor_copy(halves(gT[:, :]), o[0:24]).then_inc(psum_free, 1)
                else:
                    ct, what = divmod(n - 11, 3)
                    if what == 0:
                        e.tensor_copy(halves(tmp[:, 0, :]), o).then_inc(psum_free, 1)
                    elif what == 1:
                        e.wait_ge(psum_free, O_WIN + n)
                        e.tensor_tensor(fullp[:, ct, 2:2 + HT], o[:, 0, :], tmp[:, 0, 0:HT], ALU.mult)
                        e.tensor_tensor(fullp[:, ct, 2 + HT:2 + TP], o[:, 1, 0:PA], tmp[:, 0, HT:TP], ALU.mult)
                        e.tensor_tensor(fulls[:, ct, :, 2:2 + SQ],
                                        o[:, 1, PA:HT].rearrange("p (b q) -> p b q", b=NB),
                                        tmp[:, 0, TP:T].rearrange("p (b q) -> p b q", b=NB), ALU.mult
                                        ).then_inc(psum_free, 1)
                    else:
                        e.wait_ge(psum_free, O_WIN + n)
                        if ct == 0:
                            e.wait_ge(conv_set, 1)
                            e.wait_ge(conv_in, 16 * KC)
                        for tap in range(3):
                            w = vec[:, V_WC + 4 * tap + ct:V_WC + 4 * tap + ct + 1]
                            src, dst = sg[:, (tap + 1) % 2, :], sg[:, tap % 2, :]
                            p_in, s_in = fullp[:, ct, tap:tap + TP], fulls[:, ct, :, tap:tap + SQ]
                            s3 = dst[:, TP:T].rearrange("p (b q) -> p b q", b=NB)
                            if tap == 0:
                                e.tensor_scalar(dst[:, 0:TP], p_in, w, None, ALU.mult)
                                chain(e.tensor_scalar(s3, s_in, w, None, ALU.mult))
                            else:
                                e.scalar_tensor_tensor(out=dst[:, 0:TP], in0=p_in, scalar=w, in1=src[:, 0:TP],
                                                       op0=ALU.mult, op1=ALU.add)
                                chain(e.scalar_tensor_tensor(
                                    out=s3, in0=s_in, scalar=w,
                                    in1=src[:, TP:T].rearrange("p (b q) -> p b q", b=NB),
                                    op0=ALU.mult, op1=ALU.add))
                        e.tensor_tensor(halves(tmp[:, 1, :]), halves(sg[:, 0, :]), o, ALU.mult).then_inc(psum_free, 1)
                        e.wait_ge(y_hi, ct + 1)
                        e.tensor_tensor(yl[:, ct, :], tmp[:, 1, :], f(yh[:, ct, :]), ALU.subtract).then_inc(y_lo, 1)
            for m in range(KD):
                lo(U_MGB + 2 * m + 2)
                e.wait_ge(sgb_ready, m + 1)
                e.wait_ge(unit_used, U_MGB + 2 * m + 2)
                e.tensor_tensor(halves(mB[:, m, :]), halves(sg[:, m % 2, :]), out2(2 * (m % 2) + 1),
                                ALU.mult).then_inc(psum_free, 2)
                lo(U_MGB + 2 * m + 3)
            for m in range(2, KD):
                lo(U_MGA + m)
                if m == 3:
                    e.wait_ge(out_done, 8 * 16)
                    for c, src in enumerate((kT, vT)):
                        for g in range(2):
                            for l2 in range(2):
                                e.tensor_copy(
                                    chp[64 * l2:64 * l2 + 64, :, c, g, :],
                                    src[64 * g:64 * g + 64, 0, 0:TP].rearrange("p (n lp l) -> p l lp n", lp=8, l=2)[:, l2]
                                    ).then_inc(chp_ready, 1)
                if m == 5:
                    e.wait_ge(gv_ready, 1)
                    for br in range(2):
                        e.tensor_copy(vn[:, br, 0:4, :], PS[:, 4 + br, :].rearrange("p (t c) -> p t c", t=4))
                    e.tensor_copy(vn[0:TS, :, 4, :], PS[0:TS, 6, 0:2 * P].rearrange("p (b c) -> p b c", b=2))
                    e.tensor_copy(gq[:, :, :], PS[:, 7, 0:96].rearrange("p (t c) -> p t c", t=4)).then_inc(gv_copied, 1)
            e.wait_ge(cmpp_ready, 1)
            e.wait_ge(kz_zero, 2)
            for g in range(2):
                rows = slice(64 * g, 64 * g + 64)
                ins = e.tensor_copy(kcz[rows, g, :], PS[rows, 6, 0:NCP])
            ins.then_inc(cmpp_copied, 1)
            e.tensor_copy(vcp[:, :], PS[0:NCP, 7, 0:P]).then_inc(cmpp_copied, 1)

            def sample_queries():
                chain(e.memset(qb[:, :, :, :, :], 0.0))
                for g in range(2):
                    for q in range(SQ):
                        ins = e.tensor_copy(
                            qb[64 * g:64 * g + 64, :, :, 4 * g:4 * g + 4, SQ - 1 - q].rearrange("p a b r -> p (a b) r"),
                            qT[64 * g:64 * g + 64, :, TP:T].rearrange("p r (b q) -> p q b r", q=SQ)[:, q])
                ins.then_inc(qb_ready, 1)

            def s_item(hb, w):
                e.wait_ge(s_work, S_ITEMS * hb + w + 1)

            def s_read(hb, w, ins):
                ins.then_inc(s_free, 1)
                e.wait_ge(s_free, S_ITEMS * hb + w + 1)

            def s_step(hb, k):
                bank = PS[:, S_BANK, :]
                if k == 0:
                    if hb == 0:
                        e.wait_ge(att_bias_in, 12 * 16)
                        for half in range(2):
                            ins = e.tensor_tensor(
                                bnew[:, half, :, :], cst[:, C_X + TS * half:C_X + TS * half + TS].rearrange(
                                    "p (b q) -> p b q", b=NB), bnew0[:, :].unsqueeze(1).broadcast_to([P, NB, SQ]), ALU.add)
                        chain(ins)
                    bn = bnew[:, hb, :, :].rearrange("p b q -> p (b q)")
                    s_item(hb, 0)
                    e.tensor_tensor(ss[:, PAST:SEL_W], bank[:, 0:TS], bn, ALU.add)
                    e.tensor_tensor(ss[:, S_WIN + WIN:S_WIN + WIN_W], bank[:, TS:2 * TS], bn, ALU.add)
                    s_read(hb, 0, e.tensor_tensor(ss[:, S_CMP:S_END], bank[:, 2 * TS:2 * TS + NC],
                                                  bsel[:, 31:PAST:16], ALU.add))
                    e.tensor_reduce(st[:, 3:4], ss[:, S_CMP:S_END], AX.X, ALU.max, negate=True).then_inc(s_max, 1)
                elif k == 1:
                    s_item(hb, 1)
                    s_read(hb, 1, e.tensor_tensor(ss[:, S_WIN:S_WIN + WIN], bank, bwin[:, :], ALU.add))
                    e.tensor_reduce(st[:, 4:5], ss[:, S_WIN:S_WIN + WIN_W], AX.X, ALU.max, negate=True
                                    ).then_inc(s_max, 1)
                    e.wait_ge(s_exp, 3 * hb + 1)
                    chain(e.tensor_scalar(st[:, 9:10], st[:, 6:7], 1e-30, None, ALU.max))
                    chain(e.reciprocal(st[:, 10:11], st[:, 9:10]))
                    e.tensor_scalar(ss[:, S_CMP:S_END], ss[:, S_CMP:S_END], st[:, 10:11], None, ALU.mult
                                    ).then_inc(s_prob, 1)
                elif k in (2, 3):
                    c0 = 512 * (k - 2)
                    s_item(hb, k)
                    s_read(hb, k, e.tensor_tensor(ss[:, c0:c0 + 512], bank, bsel[:, c0:c0 + 512], ALU.add))
                elif k == 4:
                    s_item(hb, 4)
                    s_read(hb, 4, e.tensor_copy(sx[:, 0:NC], bank[:, 0:NC]))
                    e.tensor_tensor(sx[:, 64:78], sx[:, 3:56:4], sx[:, 7:60:4], ALU.add)
                    chain(e.tensor_tensor(sx[:, 80:94], sx[:, 4:57:4], sx[:, 5:58:4], ALU.add))
                    chain(e.tensor_tensor(sx[:, 96:110], sx[:, 80:94], sx[:, 6:59:4], ALU.add))
                    chain(e.scalar_tensor_tensor(out=sx[:, 112:126], in0=sx[:, 96:110], scalar=2.0, in1=sx[:, 64:78],
                                                 op0=ALU.mult, op1=ALU.add))
                    chain(e.tensor_reduce(st[:, 11:12], sx[:, 112:126], AX.X, ALU.min))
                    chain(e.scalar_tensor_tensor(out=sx[:, 80:94], in0=sx[:, 112:126], scalar=st[:, 11:12],
                                                 in1=cst[:, C_JI:C_JI + NSEL], op0=ALU.is_le, op1=ALU.mult))
                    chain(e.tensor_reduce(st[:, 12:13], sx[:, 80:94], AX.X, ALU.max))
                    chain(e.tensor_scalar(sx[:, 96:110], cst[:, C_JI:C_JI + NSEL], st[:, 12:13], NEG,
                                          ALU.is_equal, ALU.mult))
                    sel = ss[:, 64:960].rearrange("p (j k) -> p j k", k=64)
                    chain(e.tensor_tensor(sel, sel, sx[:, 96:110].unsqueeze(2).broadcast_to([P, NSEL, 64]), ALU.add))
                    e.tensor_reduce(st[:, 5:6], ss[:, 0:SEL_W], AX.X, ALU.max, negate=True).then_inc(s_max, 1)
                elif k == 5:
                    if hb == 0:
                        e.wait_ge(gate_in, 24 * 16)
                    e.wait_ge(s_prob, 2 * hb + 1)
                    e.tensor_scalar(ss[:, S_CMP:S_END], ss[:, S_CMP:S_END], gs[:, hb, 0:1], None, ALU.mult)
                    e.wait_ge(s_exp, 3 * hb + 3)
                    chain(e.tensor_scalar(st[:, 13:15], st[:, 7:9], 1e-30, None, ALU.max))
                    chain(e.reciprocal(st[:, 15:17], st[:, 13:15]))
                    e.tensor_tensor(st[:, 17:18], st[:, 15:16], gs[:, hb, 2:3], ALU.mult)
                    chain(e.tensor_tensor(st[:, 18:19], st[:, 16:17], gs[:, hb, 1:2], ALU.mult))
                    e.tensor_scalar(ss[:, S_WIN:S_WIN + WIN_W], ss[:, S_WIN:S_WIN + WIN_W], st[:, 17:18], None, ALU.mult)
                    e.tensor_scalar(ss[:, 0:SEL_W], ss[:, 0:SEL_W], st[:, 18:19], None, ALU.mult).then_inc(s_prob, 1)

            def s_output(hb):
                e.wait_ge(so_hi, hb + 1)
                for g in range(2):
                    for q in range(SQ):
                        ins = e.tensor_tensor(sample_o(ol, g, hb, q), sample_psum(g, hb, q),
                                              f(sample_o(oh, g, hb, q)), ALU.subtract)
                ins.then_inc(so_lo, 1)

            def p_add(j):
                g, i, br = JOBS[j]
                n = nkeys(i, br)
                if j >= 3:
                    e.wait_ge(p_tr, TR0[j - 2])
                if j == 0:
                    e.wait_ge(toepg_in, 32)
                for r in range(GQ):
                    e.wait_ge(p_scores, GQ * j + r + 1)
                    e.tensor_tensor_reduce(sp[j % 3][:, r, 0:n], PS[:, r, 0:n],
                                           toep_g[g][:, r, toep_cols(i, br)],
                                           1.0, -3e38, ALU.add, ALU.max, stp[:, j % 3, 2, r:r + 1]).then_inc(p_evac, 1)
                e.wait_ge(p_evac, GQ * (j + 1))
                e.tensor_scalar(stp[:, j % 3, 0, :], stp[:, j % 3, 2, :], -1.0, None, ALU.mult).then_inc(p_max, 1)

            def p_scale(j):
                g, i, br = JOBS[j]
                n = nkeys(i, br)
                s = stp[:, j % 3]
                e.wait_ge(p_exp, GQ * (j + 1))
                chain(e.tensor_scalar(s[:, 3, :], s[:, 1, :], 1e-30, None, ALU.max))
                chain(e.reciprocal(s[:, 4, :], s[:, 3, :]))
                chain(e.tensor_tensor(s[:, 5, :], s[:, 4, :], gq[:, i, 8 * br + 4 * g:8 * br + 4 * g + 4], ALU.mult))
                if br == 0 and i == 0:
                    chain(e.tensor_scalar(s[:, 5, :], s[:, 5, :], cst[:, C_VAL:C_VAL + 1], None, ALU.mult))
                for r in range(GQ):
                    e.tensor_scalar(sp[j % 3][:, r, 0:n], sp[j % 3][:, r, 0:n], s[:, 5, r:r + 1], None,
                                    ALU.mult).then_inc(p_prob, 1)

            def p_output(j):
                g, i, _ = JOBS[j]
                e.wait_ge(po_hi, outputs(j))
                e.tensor_tensor(ol[64 * g:64 * g + 64, :, P * i:P * i + P], prompt_psum(g),
                                f(oh[64 * g:64 * g + 64, :, P * i:P * i + P]), ALU.subtract).then_inc(po_lo, 1)

            p_add(0)
            sample_queries()
            for j, (g, i, br) in enumerate(JOBS):
                if j + 1 < len(JOBS):
                    p_add(j + 1)
                if j > 1 and JOBS[j - 2][2] == 2:
                    p_output(j - 2)
                p_scale(j)
                if j and (sample_step(j - 1) or (0, 0))[1] == 9:
                    s_output(sample_step(j - 1)[0])
                if sample_step(j):
                    s_step(*sample_step(j))
            p_output(len(JOBS) - 2)
            lo(U_NSA)
            lo(U_NSA + 1)
            p_output(len(JOBS) - 1)

            def merged_lo(m):
                e.wait_ge(m_hi, m + 1)
                e.tensor_tensor(ml[:, m, :], work(m), f(mh[:, m, :]), ALU.subtract).then_inc(m_lo, 1)

            for m in range(KD):
                lo(U_NSA + m + 2)
                e.wait_ge(unit_used, U_NSA + m + 1)
                if m >= 4:
                    e.wait_ge(m_lo, m - 3)
                e.tensor_tensor(halves(work(m)), halves(sgA[:, m, :]), out2(m % 4), ALU.mult).then_inc(psum_free, 1)
                if m > 1:
                    merged_lo(m - 2)
            merged_lo(KD - 2)
            merged_lo(KD - 1)
            for m in range(KD):
                lo(U_OUT + m + 2)
                e.wait_ge(unit_used, U_OUT + m + 1)
                residual(m, 0, 24 + 16, m % 4, O_OUT, KD)
            norm(2, uh, ul)
            ffn(U_GU2, O_GU2, 1)
            down(U_DN2, O_DN2, 48 + 16, 2 * KD)
            inv_root(3)
            for k in range(KD):
                if k >= 4:
                    e.wait_ge(y_out_sent[k % 4], 16)
                e.scalar_tensor_tensor(out=work(k), in0=h[:, k, :], scalar=vec[:, V_GF + k:V_GF + k + 1],
                                       in1=rinv[:, :], op0=ALU.mult, op1=ALU.mult).then_inc(y_out_ready, 1)

        @block.tensor
        def _(e):
            mm = e.matmul

            e.wait_ge(comp_in, 32)
            e.wait_ge(vec_in, 16)
            for c in range(2):
                for kt in range(16):
                    ins = mm(PS[:, 7, c:c + 1], w1[:, c, kt, :], vec[:, V_PE + 16 * c + kt:V_PE + 16 * c + kt + 1],
                             start=kt == 0, stop=kt == 15)
            ins.then_inc(pe_ready, 1)
            e.wait_ge(bias_in, 32)
            for c in range(4):
                a, b = 512 * c, min(512 * c + 512, LA + LW)
                if c >= 2:
                    e.wait_ge(f_copied, c - 1)
                mm(PS[0:NH, 4 + c % 2, 0:b - a], relx[:, :], oneh[:, a:b], start=True, stop=True).then_inc(f_ready, 1)

            def compress(t):
                e.wait_ge(ch_in[t % 2], 16 * 2 * NPG * (t // 2 + 1))
                for c in range(2):
                    if t >= 2:
                        e.wait_ge(hid_ready, 2 * (t - 2) + c + 1)
                    for m in range(2):
                        for lp in range(8):
                            ins = mm(PS[:, 2 * (t % 2) + c, 1 - m:257 - m].rearrange("p (g j n) -> p g j n", g=2, n=8),
                                     w1[:, c, 8 * m + lp, :],
                                     ch[:, t % 2, :, lp, c, :, :].rearrange("p j g n -> p g j n"),
                                     start=(m + lp == 0), stop=(m == 1 and lp == 7), skip_group_check=True)
                    ins.then_inc(pre_ready, 1)

            def partial(l):
                e.wait_ge(ada_in[l % ADAS], 16 * (l // ADAS + 1))
                if l >= 2:
                    e.wait_ge(part_copied, l - 1)
                for k in range(KD):
                    q = k % 4
                    ins = mm(PS[32 * q:32 * q + 32, 6 + l % 2, :], csil[:, k, :], ada[:, l % ADAS, k, :],
                             start=(k < 4), stop=(k >= 4), skip_group_check=True)
                ins.then_inc(part_ready, 1)

            def total(l):
                e.wait_ge(part_copied, l + 1)
                e.wait_ge(consts_in, 16)
                if l:
                    e.wait_ge(ada_copied, l)
                if l == ADA_AFTER[1][-1]:
                    e.wait_ge(flip_copied, NH)
                for mt in range(4):
                    ins = mm(PS[:, 5, NMOD * mt:NMOD * mt + NMOD], part[:, l % 2, P * mt:P * mt + P],
                             cst[:, C_SUM:C_SUM + NMOD], start=True, stop=True)
                ins.then_inc(ada_used, 1)

            def condition(loads):
                for l in loads:
                    partial(l)
                    if l:
                        total(l - 1)

            e.wait_ge(csil_ready, 1)
            e.wait_ge(pe_copied, 1)
            e.wait_ge(f_copied, 4)
            compress(0)
            condition(ADA_AFTER[0])
            compress(1)
            condition(ADA_AFTER[1])
            e.wait_ge(hank_in, 16 * NH)
            e.wait_ge(consts_in, 16)
            e.wait_ge(ada_copied, ADA_AFTER[1][-1])
            for hd in range(NH):
                if hd >= 2:
                    e.wait_ge(flip_copied, hd - 1)
                mm(PS[:, 4 + hd % 2, :], cst[:, C_J:C_J + P], hank[:, hd, :], start=True, stop=True).then_inc(flip_ready, 1)
            compress(2)
            condition(ADA_AFTER[2])
            compress(3)
            condition(ADA_AFTER[3])
            e.wait_ge(hid_ready, 8)
            for g in range(2):
                mm(PS[64 * g:64 * g + 64, 0, 0:NB * NC].rearrange("p (b n) -> p b n", b=NB), w2[:, 0, :],
                   hid[:, 0, g, :, 0:NC], start=True, stop=True)
            for b in range(NB):
                for g in range(2):
                    c0 = (b % 4) * P + 64 * g
                    ins = mm(PS[0:NC, 1 + b // 4, c0:c0 + HD], hid[:, 1, g, b, 0:NC], w2[:, 1, :], start=True, stop=True)
            ins.then_inc(cmp_ready, 1)
            total(NADA - 2)

            def unit(u, slot, xh, xl, k0, first, last, more=0, ready=None):
                n = unit_k(u)
                o = out2(slot)
                e.wait_ge(lo_ready, u + 1 + more)
                for k in range(n):
                    if ready is not None:
                        e.wait_ge(ready[0], ready[1] + k0 + k + 1)
                    for w, x in ((wh, xh), (wh, xl), (wl, xh)):
                        for a in range(2):
                            ins = mm(o[:, a, :], w[:, u % SPLITS, k, :], x[:, k0 + k, HT * a:HT * a + HT],
                                     start=(first and k == 0 and w is wh and x is xh),
                                     stop=(last and k == n - 1 and w is wl))
                ins.then_inc(unit_used, 1)

            def norm_sum(n):
                o = out2(norm_slot(n))
                e.wait_ge(ssq_ready, 8 * n + 8)
                for a in range(2):
                    mm(o[:, a, :], ones[:, :], ssq[:, HT * a:HT * a + HT], start=True, stop=False)
                e.wait_ge(sq_last, n + 1)
                for a in range(2):
                    ins = mm(o[:, a, :], ones[:, :], rinv[:, HT * a:HT * a + HT], start=False, stop=True)
                ins.then_inc(ssum_ready, 1)

            def late_partial(n, fi, i=0):
                e.wait_ge(ada_t_in[n % 2], 16 * (n // 2 + 1) + 32 * i)
                for k in range(KD):
                    q = k % 4
                    ins = mm(PS[32 * q:32 * q + 32, ada_bank(fi), 0:P], csil[:, k, :], ada_t[:, n % 2, k, :],
                             start=(k < 4), stop=(k >= 4), skip_group_check=True)
                ins.then_inc(part_ready, 1)

            def late_total(n, fi, i=0):
                e.wait_ge(part_copied, NADA + n + 1 + 4 * i)
                mm(PS[:, ada_bank(fi) + 1, 0:NMOD], part_t[:, n % 2, :], cst[:, C_SUM:C_SUM + NMOD],
                   start=True, stop=True).then_inc(ada_used, 1)

            def ffn(ug, og, n, nn):
                first = ug == 0

                def tile(fi, i=0, ready=None):
                    e.wait_ge(psum_free, og + 2 * fi - 2 + 4 * i)
                    unit(ug + 2 * fi, 2 * (fi % 2), uh, ul, 0, True, True, 4 * i, ready)
                    if first:
                        e.wait_ge(psum_free, og + 2 * fi + 4 * i)
                        late_partial(2 * fi, fi, i)
                        if fi:
                            late_total(2 * fi - 1, fi, i)
                        e.wait_ge(ada_copied, NADA + 2 * fi - 1 + 4 * i)
                    unit(ug + 2 * fi + 1, 2 * (fi % 2) + 1, uh, ul, 0, True, True, 4 * i)
                    if first:
                        e.wait_ge(part_copied, NADA + 2 * fi + 1 + 4 * i)
                        late_partial(2 * fi + 1, fi, i)
                        e.wait_ge(ada_copied, NADA + 2 * fi + 4 * i)
                        late_total(2 * fi, fi, i)

                tile(0, 0, (u_lo, 8 * nn))
                tile(1)
                with e.Fori(0, KF // 2 - 1) as i:
                    tile(2, i)
                    tile(3, i)
                if first:
                    e.wait_ge(ada_copied, NADA + 2 * KF - 1)
                    late_total(2 * KF - 1, KF - 1)

            def down(ud, od, n):
                def tile(m, i=0, ready=None):
                    e.wait_ge(psum_free, od + m - 1 + 2 * i)
                    for j, (k0, nk) in enumerate(DOWN_K):
                        unit(ud + 4 * m + j, m % 2, hh, hl, k0, j == 0, j == 3, 8 * i, ready)

                tile(0, 0, (hid_lo, KF * n))
                tile(1)
                with e.Fori(0, KD // 2 - 1) as i:
                    tile(2, i)
                    tile(3, i)

            e.wait_ge(psum_free, O_GU1)
            norm_sum(0)
            partial(NADA - 1)
            total(NADA - 1)
            ffn(U_GU1, O_GU1, 0, 0)
            down(U_DN1, O_DN1, 0)
            norm_sum(1)
            for n in range(23):
                if n >= 4:
                    e.wait_ge(psum_free, O_WIN + n - 3)
                unit(U_WIN + n, n % 4, uh2, ul2, 0, True, True, 0, (u_lo, 8) if n == 0 else None)
            for m in range(KD):
                e.wait_ge(psum_free, O_MGB - 1 + m if m < 2 else O_MGB + 2 * m - 2)
                unit(U_MGB + 2 * m, 2 * (m % 2), uh2, ul2, 0, True, True)
                unit(U_MGB + 2 * m + 1, 2 * (m % 2) + 1, yh, yl, 0, True, True, 0, (y_lo, 0) if m == 0 else None)
            for m in range(KD):
                if m < 2:
                    e.wait_ge(psum_free, O_MGB + 14)
                else:
                    e.wait_ge(sga_ready, m - 1)
                unit(U_MGA + m, m % 2, uh2, ul2, 0, True, True)
                if m == 2:
                    e.wait_ge(psum_free, O_MGB + 16)
                    e.wait_ge(sig_ready, 1)
                    for br in range(2):
                        for t in range(4):
                            e.transpose(PS[:, 4 + br, P * t:P * t + P], vT[:, 1 + br, P * t:P * t + P], ident)
                        e.transpose(PS[0:TS, 6, P * br:P * br + P], vT[:, 1 + br, TP:T], ident)
                    for t in range(4):
                        ins = e.transpose(PS[:, 7, 24 * t:24 * t + 24], gT[:, P * t:P * t + P], ident[0:24, 0:24])
                    ins.then_inc(gv_ready, 1)
            e.wait_ge(compp_in, 32)
            e.wait_ge(chp_ready, 8)
            e.wait_ge(gv_copied, 1)
            for c in range(2):
                for m in range(2):
                    for lp in range(8):
                        ins = mm(PS[:, 4 + c, 1 - m:65 - m].rearrange("p (g n) -> p g n", g=2), w1p[:, c, 8 * m + lp, :],
                                 chp[:, lp, c, :, :], start=(m + lp == 0), stop=(m == 1 and lp == 7),
                                 skip_group_check=True)
                ins.then_inc(prep_ready, 1)
            e.wait_ge(hidp_ready, 2)
            for g in range(2):
                mm(PS[64 * g:64 * g + 64, 6, 0:NCP], w2p[:, 0, :], hidp[:, 0, g, 0:NCP], start=True, stop=True)
                ins = mm(PS[0:NCP, 7, 64 * g:64 * g + 64], hidp[:, 1, g, 0:NCP], w2p[:, 1, :], start=True, stop=True)
            ins.then_inc(cmpp_ready, 1)
            e.wait_ge(cmpp_copied, 2)
            e.wait_ge(sga_ready, KD)
            e.wait_ge(kz_ready, 4)

            def s_step(hb, k):
                q_all = qb[:, hb].rearrange("p b h q -> p (b h q)")
                bank = PS[:, S_BANK, :]
                base = S_ITEMS * hb
                if k == 0:
                    if hb:
                        e.wait_ge(so_lo, 1)
                    else:
                        e.wait_ge(qb_ready, 1)
                    mm(bank[:, 0:TS], q_all, kT[:, 1, TP:T], start=True, stop=True)
                    mm(bank[:, TS:2 * TS], q_all, kT[:, 2, TP:T], start=True, stop=True)
                    for b in range(4):
                        rows = slice(32 * b, 32 * b + 32)
                        ins = mm(PS[rows, S_BANK, 2 * TS:2 * TS + NC], q_all[:, rows], kcT[:, 4 * hb + b, :],
                                 start=True, stop=True)
                    ins.then_inc(s_work, 1)
                elif k <= 3:
                    x0 = {1: NPG, 2: 0, 3: 4}[k]
                    e.wait_ge(s_free, base + k)
                    e.wait_ge(kv_in[k - 1], KV_IN[k - 1] * (2 * hb + 1))
                    for b in range(4):
                        rows = slice(32 * b, 32 * b + 32)
                        ins = mm(PS[rows, S_BANK, :], q_all[:, rows],
                                 kv[:, b, x0:x0 + 4, :].rearrange("p t k -> p (t k)"), start=True, stop=True)
                    ins.then_inc(s_work, 1)
                elif k == 4:
                    e.wait_ge(s_prob, 2 * hb + 1)
                    e.wait_ge(s_free, base + 4)
                    mm(bank[:, 0:NC], cst[:, C_M:C_M + P], ss[:, S_CMP:S_END], start=True, stop=True).then_inc(s_work, 1)
                elif k in (6, 7):
                    e.wait_ge(s_prob, 2 * hb + 2)
                    for q in (2 * (k - 6), 2 * (k - 6) + 1):
                        e.wait_ge(s_free, base + 5 + q)
                        for x in range(4 * q, min(4 * q + 4, 15)):
                            a, n = (P * x, P) if x < 8 else (S_WIN + P * (x - 8), P) if x < 12 else \
                                (PAST, TS) if x == 12 else (S_WIN + WIN, TS) if x == 13 else (S_CMP, NC)
                            ins = e.transpose(PS[0:n, S_BANK, P * (x % 4):P * (x % 4) + P], ss[:, a:a + n], ident)
                        ins.then_inc(s_work, 1)
                elif k == 8:
                    e.wait_ge(s_free, base + S_ITEMS)
                    for br in range(2):
                        mm(bank[:, 0:P], pT[0:TS, 12 + br, :], vn[0:TS, br, 4, :], start=(br == 0), stop=False,
                           skip_group_check=True)
                    for x in range(3):
                        e.wait_ge(kv_in[x], KV_IN[x] * (2 * hb + 2))
                    for x in range(13):
                        for b in range(4):
                            rows = slice(32 * b, 32 * b + 32)
                            p_x, v_x = (pT[:, x, rows], kv[:, b, x, :]) if x < 12 else \
                                (pT[0:NC, 14, rows], vc[:, 4 * hb + b, :])
                            ins = mm(PS[rows, S_BANK, 0:P], p_x, v_x, start=False, stop=(x == 12),
                                     skip_group_check=True)
                    ins.then_inc(v_used, 1)
                elif k == 9:
                    e.wait_ge(s_sum, hb + 1)
                    e.transpose(bank[:, 0:P], sx[:, :], ident).then_inc(s_out, 1)

            def p_score(j):
                g, i, br = JOBS[j]
                n = nkeys(i, br)
                keys = kcz[:, g, 0:n] if br == 0 else kz[:, g, br - 1, 0:n]
                for r in range(GQ):
                    if j:
                        e.wait_ge(p_evac, GQ * (j - 1) + r + 1)
                    mm(PS[:, r, 0:n], qT[:, r, P * i:P * i + P], keys, start=True, stop=True
                       ).then_inc(p_scores, 1)

            def p_turn(j, tr):
                _, i, br = JOBS[j]
                n = nkeys(i, br) if br == 0 else P
                kt = tr - TR0[j]
                if tr >= 2:
                    e.wait_ge(p_trc, tr - 1)
                for r in range(GQ):
                    if kt == 0:
                        e.wait_ge(p_prob, GQ * j + r + 1)
                    ins = e.transpose(PS[0:n, 4 + tr % 2, P * r:P * r + P], sp[j % 3][:, r, P * kt:P * kt + n], ident)
                ins.then_inc(p_tr, 1)

            def p_value(j, tr):
                g, i, br = JOBS[j]
                n = nkeys(i, br) if br == 0 else P
                v = vcp[0:n, 64 * g:64 * g + 64] if br == 0 else vn[:, br - 1, tr - TR0[j], 64 * g:64 * g + 64]
                e.wait_ge(p_trc, tr + 1)
                if br == 0 and j >= 6:
                    e.wait_ge(po_lo, outputs(j - 2))
                mm(prompt_psum(g), v, pTp[0:n, tr % 2, :].rearrange("p (r q) -> p r q", r=GQ), start=(br == 0),
                   stop=(br == 2 and tr + 1 == TR0[j + 1]), skip_group_check=True).then_inc(p_pv, 1)

            p_score(0)
            p_score(1)
            late = None
            for j in range(len(JOBS)):
                if j + 2 < len(JOBS):
                    p_score(j + 2)
                if sample_step(j):
                    s_step(*sample_step(j))
                for tr in range(TR0[j], TR0[j + 1]):
                    p_turn(j, tr)
                    if late:
                        p_value(*late)
                    late = (j, tr)
            p_value(*late)

            e.wait_ge(po_lo, 8)
            e.wait_ge(so_lo, 2)
            for m in range(KD):
                if m >= 4:
                    e.wait_ge(psum_free, O_NSA + m - 3)
                unit(U_NSA + m, m % 4, oh, ol, 0, True, True)
            for m in range(KD):
                e.wait_ge(psum_free, O_OUT + m - 3)
                unit(U_OUT + m, m % 4, mh, ml, 0, True, True, 0, (m_lo, 0) if m == 0 else None)
            norm_sum(2)
            ffn(U_GU2, O_GU2, 1, 2)
            down(U_DN2, O_DN2, 1)
            norm_sum(3)


def _bucket(n):
    n = np.maximum(n, 0)
    nf = np.maximum(n, 1).astype(np.float32)
    large = 16 + (np.log(nf / np.float32(16)) / np.float32(np.log(8.0)) * np.float32(16)).astype(np.int32)
    return np.where(n < 16, n, np.minimum(large, 31))


def _constants():
    cst = np.zeros((P, C_END), np.float32)
    cst[:, C_ID:C_ID + P] = np.eye(P)
    cst[:, C_J:C_J + P] = np.eye(P)[::-1]
    row = np.arange(P)
    key = (row // 32) * 100 + (row % 32 // 16) * 10 + row % 4
    cst[:, C_M:C_M + P] = key[:, None] == key[None, :]
    for hb in range(2):
        b = np.arange(TS) // SQ
        cst[:, C_X + TS * hb:C_X + TS * hb + TS] = np.where(b[None, :] == 4 * hb + row[:, None] // 32, 0.0, NEG)
    cst[:, C_JI:C_JI + NSEL] = np.arange(1, NSEL + 1)
    cst[:, C_VAL] = row >= 31
    cst[:, C_SUM:C_SUM + NMOD] = row[:, None] % 32 == np.arange(NMOD)[None, :]
    oneh = np.zeros((33, LA + LW), np.float32)
    dist = np.concatenate([1027 - np.arange(LA), 515 - np.arange(LW)])
    seen = (dist >= 0) & ((np.arange(LA + LW) < LA) | (dist < WIN))
    oneh[np.where(seen, _bucket(dist), 32), np.arange(LA + LW)] = 1.0
    return cst, oneh


_OUTS = {
    "yT": (KD, P, T), "kvT": (6, P, T), "conv_p": (P, KC, 2), "conv_s": (P, KC, NB, SQ),
    "win_old": (NB, WIN - SQ, 256),
}
_SCRATCH = {"F": (NH, LA + LW), "toep": (P, NH, 512), "gscr": (24, TS)}


def _tiles(w, cols=P):
    k, n = w.shape
    return np.ascontiguousarray(w.reshape(k // P, P, n // cols, cols).transpose(2, 1, 0, 3)).reshape(n // cols, P, -1)


def _layout(x_prompt, x_sample, cache_kv_cmp, cache_kv_sel, state_kv_win, state_conv, page_table, c_prompt, c_sample,
            w_ada, b_ada, g_norm, w_ffn1_gu, w_ffn1_down, w_ffn2_gu, w_ffn2_down, w_in, w_cmp1, w_cmp2, pe_cmp,
            w_conv, w_nsa_out, w_conv_out, w_out, rel_bias, g_final):
    def fm(x):
        return np.ascontiguousarray(x.reshape(x.shape[0], -1, P).transpose(2, 1, 0))

    def gate_value(w):
        t = _tiles(w)
        return np.ascontiguousarray(t.reshape(2, KF, P, -1).transpose(1, 0, 2, 3)).reshape(2 * KF, P, -1)

    cst, oneh = _constants()
    w = w_in[0]
    blocks = [np.concatenate([w[:, 64 * r:64 * r + 64], w[:, 256 + 64 * r:320 + 64 * r]], 1) for r in range(4)]
    blocks += [w[:, OFF_KV + P * j:OFF_KV + P * j + P] for j in range(6)]
    blocks += [w[:, OFF_GN:OFF_GN + P]]
    for ct in range(KC):
        blocks += [w[:, o + P * ct:o + P * ct + P] for o in (OFF_C, OFF_H, OFF_B)]
    blocks += [w[:, OFF_MG + D + P * m:OFF_MG + D + P * m + P] for m in range(KD)]
    blocks += [w[:, OFF_MG + P * m:OFF_MG + P * m + P] for m in range(KD)]
    no = w_nsa_out[0].reshape(2, 4, HD, D).transpose(1, 0, 2, 3).reshape(DC, D)
    cmp_pages = cache_kv_cmp[0].reshape(NPHYS, 8, 8, 2, 2, 2, HD)
    cmp_pages = cmp_pages.transpose(0, 3, 6, 2, 4, 5, 1).reshape(NPHYS, P, 256)
    sel = cache_kv_sel[0].reshape(NPHYS, PAGE, 2, P)
    win = state_kv_win[0].reshape(NB, 4, P, 2, P)
    w1 = w_cmp1[0].reshape(2, 16, P, P).transpose(2, 0, 1, 3)
    vec = np.concatenate([b_ada[0].reshape(72, P), g_norm[0].reshape(24, P), g_final.reshape(8, P),
                          w_conv[0].reshape(12, P), pe_cmp[0].reshape(32, P)]).T
    a = {
        "ptab": page_table.reshape(1, -1),
        "w1": w1, "w2": w_cmp2[0].transpose(1, 0, 2), "vec": vec, "cst": cst, "oneh": oneh,
        "relx": np.concatenate([rel_bias, np.full((1, NH), NEG, np.float32)]),
        "cmp_pages": cmp_pages,
        "sel_pages": np.stack([sel[:, :, 0].transpose(0, 2, 1), sel[:, :, 1]]),
        "win_tiles": np.stack([win[:, :, :, 0].transpose(0, 3, 1, 2), win[:, :, :, 1].transpose(0, 2, 1, 3)]),
        "win_src": state_kv_win[0].reshape(NB, WIN, 256)[:, SQ:],
        "cT": fm(np.concatenate([c_prompt, c_sample])),
        "xT": fm(np.concatenate([x_prompt[0], x_sample.reshape(TS, D)])),
        "convT": state_conv[0].reshape(NB, 2, KC, P).transpose(3, 2, 0, 1),
        "w_ada": _tiles(w_ada[0][:, :ADA_LATE * P], 512).reshape(NADA, P, KD, 512),
        "w_ada_t": _tiles(w_ada[0][:, ADA_LATE * P:]),
        "w_gu1": gate_value(w_ffn1_gu[0]), "w_dn1": _tiles(w_ffn1_down[0]),
        "w_gu2": gate_value(w_ffn2_gu[0]), "w_dn2": _tiles(w_ffn2_down[0]),
        "w_in": np.stack([_tiles(b)[0] for b in blocks]),
        "w_no": _tiles(no), "w_co": _tiles(w_conv_out[0]), "w_out": _tiles(w_out[0]),
    }
    return {k: np.ascontiguousarray(v) for k, v in a.items()}


def _results(r):
    y = r["yT"].transpose(2, 0, 1).reshape(T, D)
    kv = r["kvT"].reshape(3, 2, 2, HD, T).transpose(0, 4, 1, 2, 3)
    kvp = [kv[j, :TP][None, None] for j in range(3)]
    kvs = [kv[j, TP:].reshape(1, NB, SQ, 2, 2, HD) for j in range(3)]
    old = r["win_old"].reshape(1, NB, WIN - SQ, 2, 2, HD)
    win_s = np.concatenate([old, kvs[2]], axis=2)
    conv_p = r["conv_p"].transpose(2, 1, 0).reshape(1, 1, 2, DC)
    conv_s = r["conv_s"].transpose(2, 3, 1, 0).reshape(NB, SQ, DC)[None, :, SQ - 2:]
    out = (y[:TP][None], y[TP:].reshape(NB, SQ, D), kvp[0], kvp[1], kvp[2], conv_p, kvs[0], kvs[1], win_s, conv_s)
    return tuple(np.ascontiguousarray(x) for x in out)


def _program(nc, arrays):
    d = {}
    for name, a in arrays.items():
        d[name] = nc.dram_tensor("in_" + name, a.shape, mybir.dt.from_np(a.dtype), kind="ExternalInput").ap()
    for name, shape in _OUTS.items():
        d[name] = nc.dram_tensor("out_" + name, shape, F32, kind="ExternalOutput").ap()
    for name, shape in _SCRATCH.items():
        d[name] = nc.dram_tensor("scr_" + name, shape, F32, kind="Internal").ap()
    build(nc, d)


def kernel(**inputs):
    import concourse.bacc as _bacc
    from concourse.bass_utils import run_bass_kernel_spmd as _run

    nc = _bacc.Bacc("TRN2", target_bir_lowering=False, num_devices=1,
                     dynamic_dma_scratch_size=1024)
    arrays = _layout(**{k: np.asarray(v) for k, v in inputs.items()})
    _program(nc, arrays)
    r = _run(nc, [{"in_" + k: v for k, v in arrays.items()}], core_ids=[0])
    return _results({k: r.results[0]["out_" + k] for k in _OUTS})
```
